# Optimizing a Trainium2 kernel written in Bass

```python
import math
import jax
import jax.numpy as jnp
from jax import lax
import numpy as np

D_MODEL = 1024
BATCH = 1
SEQ = 1024
DEPTH = 1
DEC_BATCH = 8
DEC_SEQ = 1
PAST_LEN = 4096
PAGE_SIZE = 128

A_HEADS = 4
A_DH = 64
B_HEADS = 4
B_DH = 64
CMP_BLOCK = 64
SEL_BLOCK = 64
TOPK_BLOCKS = 16
WINDOW = 512
C_HEADS = 4
C_DK = 32
C_DV = 64
C_RANK = 16
GLA_TAU = 16.0
GLA_CHUNK = 64
M_HEADS = 4
M_DH = 64
N_BRANCH = 4
BRANCH_W = 256
N_GROUPS = 4
E_PER_GROUP = 4
N_EXPERTS = N_GROUPS * E_PER_GROUP
TOP_IN_GROUP = 2
D_EXPERT = 256
N_BUCKETS = 32
MAX_DIST = 128
QBLK = 128
EPS = 1e-6
BIG = 1e9

IN_LAYOUT = (
    ('sb_q', A_HEADS * A_DH), ('sb_k', A_HEADS * A_DH), ('sb_v', A_HEADS * A_DH),
    ('nsa_q', B_HEADS * B_DH), ('nsa_kc', B_DH), ('nsa_vc', B_DH), ('nsa_ks', B_DH), ('nsa_vs', B_DH),
    ('nsa_kw', B_DH), ('nsa_vw', B_DH), ('nsa_g', B_HEADS * 3),
    ('gla_q', C_HEADS * C_DK), ('gla_k', C_HEADS * C_DK), ('gla_v', C_HEADS * C_DV), ('gla_a', C_RANK),
    ('gla_r', C_HEADS * C_DV),
    ('mem_q', M_HEADS * M_DH), ('merge_g', N_BRANCH * D_MODEL))
N_IN = sum(w for _, w in IN_LAYOUT)

kernel_name = 'hybrid_sb_nsa_gla_hmoe_step'

def rmsnorm(x, g):
    xf = x.astype(jnp.float32)
    y = xf * lax.rsqrt(jnp.mean(xf * xf, axis=-1, keepdims=True) + EPS)
    return (y * g.astype(jnp.float32)).astype(x.dtype)

def masked_softmax(logits, mask):
    l = jnp.where(mask, logits.astype(jnp.float32), -1e30)
    e = jnp.where(mask, jnp.exp(l - jnp.max(l, axis=-1, keepdims=True)), 0.0)
    return e / jnp.maximum(jnp.sum(e, axis=-1, keepdims=True), 1e-30)

def rel_bucket(dist):
    n = jnp.maximum(dist, 0)
    exact = N_BUCKETS // 2
    nf = jnp.maximum(n, 1).astype(jnp.float32)
    large = exact + (jnp.log(nf / exact) / math.log(MAX_DIST / exact) * (N_BUCKETS - exact)).astype(jnp.int32)
    return jnp.where(n < exact, n, jnp.minimum(large, N_BUCKETS - 1))

def rel_bias_lookup(table, dist):
    return table[rel_bucket(dist)].astype(jnp.float32)

def q_blocks(t):
    b, s = t.shape[:2]
    return t.reshape((b, s // QBLK, QBLK) + t.shape[2:]).swapaxes(0, 1)

def un_q_blocks(t):
    nb, b = t.shape[:2]
    return t.swapaxes(0, 1).reshape((b, nb * t.shape[2]) + t.shape[3:])

def to_blocks(rows, size):
    b, l, d = rows.shape
    nb = -(-l // size)
    return jnp.pad(rows, ((0, 0), (0, nb * size - l), (0, 0))).reshape(b, nb, size, d)

def compress_blocks(rows, pe, phi):
    return jnp.einsum('bnd,de->bne', jnp.mean(to_blocks(rows, CMP_BLOCK) + pe, axis=2), phi)

def stick_breaking(q, k, v, q_pos, k_pos):
    z = jnp.einsum('bqhd,bkhd->bhqk', q, k).astype(jnp.float32) * (q.shape[-1] ** -0.5)
    past = k_pos[None, :] < q_pos[:, None]
    log_keep = jnp.where(past, jax.nn.log_sigmoid(-z), 0.0)
    after = lax.cumsum(log_keep, axis=3, reverse=True) - log_keep
    a = jnp.where(past, jnp.exp(jax.nn.log_sigmoid(z) + after), 0.0)
    return jnp.einsum('bhqk,bkhd->bqhd', a.astype(v.dtype), v)

def sb_prompt(q, k, v):
    s = q.shape[1]
    k_pos = jnp.arange(s, dtype=jnp.int32)

    def body(args):
        q_blk, i = args
        return stick_breaking(q_blk, k, v, i * QBLK + jnp.arange(QBLK, dtype=jnp.int32), k_pos)

    return un_q_blocks(lax.map(body, (q_blocks(q), jnp.arange(s // QBLK, dtype=jnp.int32))))

def nsa_attend(q, g, q_pos, kcmp, vcmp, ks_blk, vs_blk, kw, vw, kw_pos, rel_bias):
    b, lq, h, dh = q.shape
    nb = kcmp.shape[1]
    scale = dh ** -0.5
    blk = jnp.arange(nb, dtype=jnp.int32)
    cmp_end = (blk + 1) * CMP_BLOCK - 1
    dist_c = q_pos[:, None] - cmp_end[None, :]
    lc = jnp.einsum('bqhd,bnd->bqhn', q, kcmp).astype(jnp.float32) * scale
    lc = lc + rel_bias_lookup(rel_bias, dist_c).transpose(0, 2, 1)[None]
    p_c = masked_softmax(lc, (dist_c >= 0)[None, :, None, :])
    o_c = jnp.einsum('bqhn,bnd->bqhd', p_c.astype(vcmp.dtype), vcmp)
    cur = q_pos // SEL_BLOCK
    imp = jnp.sum(p_c, axis=2)
    forced = (blk[None, :] == 0) | (blk[None, :] == cur[:, None]) | (blk[None, :] == cur[:, None] - 1)
    valid = blk[None, :] <= cur[:, None]
    score = jnp.where(forced[None], BIG, jnp.where(valid[None], imp, -BIG))
    n_sel = min(TOPK_BLOCKS, nb)
    _, idx = lax.top_k(score, n_sel)
    bidx = jnp.arange(b)[:, None, None]
    ks_g = ks_blk[bidx, idx].reshape(b, lq, n_sel * SEL_BLOCK, dh)
    vs_g = vs_blk[bidx, idx].reshape(b, lq, n_sel * SEL_BLOCK, dh)
    pos_s = (idx[..., None] * SEL_BLOCK + jnp.arange(SEL_BLOCK, dtype=jnp.int32)).reshape(b, lq, n_sel * SEL_BLOCK)
    dist_s = q_pos[None, :, None] - pos_s
    ls = jnp.einsum('bqhd,bqkd->bqhk', q, ks_g).astype(jnp.float32) * scale
    ls = ls + rel_bias_lookup(rel_bias, dist_s).transpose(0, 1, 3, 2)
    p_s = masked_softmax(ls, (dist_s >= 0)[:, :, None, :])
    o_s = jnp.einsum('bqhk,bqkd->bqhd', p_s.astype(vs_g.dtype), vs_g)
    dist_w = q_pos[:, None] - kw_pos[None, :]
    lw = jnp.einsum('bqhd,bkd->bqhk', q, kw).astype(jnp.float32) * scale
    lw = lw + rel_bias_lookup(rel_bias, dist_w).transpose(0, 2, 1)[None]
    mask_w = (dist_w >= 0) & (dist_w <= WINDOW) & (kw_pos[None, :] >= 0)
    p_w = masked_softmax(lw, mask_w[None, :, None, :])
    o_w = jnp.einsum('bqhk,bkd->bqhd', p_w.astype(vw.dtype), vw)
    return g[..., 0:1] * o_c + g[..., 1:2] * o_s + g[..., 2:3] * o_w

def gla_chunked(q, k, v, log_a, s0):
    b, l, h, dk = q.shape
    dv = v.shape[-1]
    c = min(GLA_CHUNK, l)
    n = -(-l // c)
    pad = n * c - l

    def prep(t):
        t = jnp.pad(t.astype(jnp.float32), ((0, 0), (0, pad), (0, 0), (0, 0)))
        return t.reshape(b, n, c, h, t.shape[-1]).swapaxes(0, 1)

    tri = jnp.tril(jnp.ones((c, c), dtype=bool))

    def step(s, inp):
        qc, kc, vc, ac = inp
        cb = jnp.cumsum(ac, axis=1)
        inter = jnp.einsum('bthk,bhkv->bthv', qc * jnp.exp(cb), s)
        diff = cb[:, :, None] - cb[:, None, :]
        w = jnp.exp(jnp.where(tri[None, :, :, None, None], diff, -jnp.inf))
        att = jnp.einsum('bthk,bshk,btshk->bths', qc, kc, w)
        intra = jnp.einsum('bths,bshv->bthv', att, vc)
        last = cb[:, -1]
        s_new = jnp.exp(last)[..., None] * s + jnp.einsum('bshk,bshv->bhkv', kc * jnp.exp(last[:, None] - cb), vc)
        return s_new, inter + intra

    s_fin, o = lax.scan(step, s0.astype(jnp.float32), (prep(q), prep(k), prep(v), prep(log_a)))
    o = o.swapaxes(0, 1).reshape(b, n * c, h, dv)[:, :l]
    return o.astype(q.dtype), s_fin.astype(s0.dtype)

def mem_kv(mem, lp):
    b, n, _ = mem.shape
    kv = rmsnorm(mem, lp['norm_mem_g']) @ lp['w_mem_kv']
    mk = rmsnorm(kv[..., :M_HEADS * M_DH].reshape(b, n, M_HEADS, M_DH), lp['mem_kn_g'])
    mv = kv[..., M_HEADS * M_DH:].reshape(b, n, M_HEADS, M_DH)
    return mk, mv

def mem_attend(q, mk, mv):
    logits = jnp.einsum('bqhd,bmhd->bhqm', q, mk).astype(jnp.float32) * (M_DH ** -0.5)
    p = jax.nn.softmax(logits, axis=-1)
    return jnp.einsum('bhqm,bmhd->bqhd', p.astype(mv.dtype), mv)

def branch_inputs(x, lp):
    b, l, _ = x.shape
    proj = rmsnorm(x, lp['norm_mix_g']) @ lp['w_in']
    p = {}
    off = 0
    for name, w in IN_LAYOUT:
        p[name] = proj[..., off:off + w]
        off += w
    heads = lambda t, nh: t.reshape(b, l, nh, -1)
    log_a = jax.nn.log_sigmoid((p['gla_a'] @ lp['gla_gate_up'] + lp['gla_gate_b']).astype(jnp.float32)) / GLA_TAU
    return dict(
        qA=heads(p['sb_q'], A_HEADS), kA=heads(p['sb_k'], A_HEADS), vA=heads(p['sb_v'], A_HEADS),
        qB=rmsnorm(heads(p['nsa_q'], B_HEADS), lp['nsa_qn_g']),
        kc=p['nsa_kc'], vc=p['nsa_vc'],
        ks=rmsnorm(p['nsa_ks'], lp['nsa_kn_g'][1]), vs=p['nsa_vs'],
        kw=rmsnorm(p['nsa_kw'], lp['nsa_kn_g'][2]), vw=p['nsa_vw'],
        gB=jax.nn.sigmoid(heads(p['nsa_g'], B_HEADS)),
        qC=heads(p['gla_q'], C_HEADS) * (C_DK ** -0.5), kC=heads(p['gla_k'], C_HEADS),
        vC=heads(p['gla_v'], C_HEADS), la=heads(log_a, C_HEADS), rC=p['gla_r'],
        qM=rmsnorm(heads(p['mem_q'], M_HEADS), lp['mem_qn_g']), gM=p['merge_g'])

def hmoe(h, lp):
    b, l, d = h.shape
    t = h.reshape(b * l, d)
    pg = jax.nn.softmax((t @ lp['w_grp'] + lp['b_grp']).astype(jnp.float32), axis=-1)
    g_idx = jnp.argmax(pg, axis=-1)
    g_w = jnp.take_along_axis(pg, g_idx[:, None], axis=-1)
    le = (t @ lp['w_rt'] + lp['b_rt']).astype(jnp.float32).reshape(-1, N_GROUPS, E_PER_GROUP)
    le = jnp.take_along_axis(le, g_idx[:, None, None], axis=1)[:, 0]
    top_p, top_i = lax.top_k(jax.nn.softmax(le, axis=-1), TOP_IN_GROUP)
    top_p = top_p / jnp.sum(top_p, axis=-1, keepdims=True)
    eid = g_idx[:, None] * E_PER_GROUP + top_i
    comb = jnp.sum(jax.nn.one_hot(eid, N_EXPERTS, dtype=jnp.float32) * (g_w * top_p)[..., None], axis=1)
    hid = jax.nn.silu(jnp.einsum('td,edf->tef', t, lp['w_eg'])) * jnp.einsum('td,edf->tef', t, lp['w_eu'])
    out = jnp.einsum('tef,efd->td', hid * comb.astype(hid.dtype)[..., None], lp['w_ed'])
    return out.reshape(b, l, d)

def finish_layer(x, bi, o_a, o_b, o_c, o_m, lp):
    b, l, _ = x.shape
    o_c = rmsnorm(o_c, lp['gla_norm_g']) * jax.nn.silu(bi['rC']).reshape(b, l, C_HEADS, C_DV)
    o = jnp.stack([o_a.reshape(b, l, BRANCH_W), o_b.reshape(b, l, BRANCH_W),
                   o_c.reshape(b, l, BRANCH_W), o_m.reshape(b, l, BRANCH_W)], axis=2)
    u = jnp.einsum('blnc,ncd->blnd', o, lp['w_branch'])
    gates = jax.nn.sigmoid(bi['gM'].reshape(b, l, N_BRANCH, D_MODEL))
    x = x + jnp.sum(gates * u, axis=2) @ lp['w_out']
    return x + hmoe(rmsnorm(x, lp['norm_ffn_g']), lp)

def layer_prompt(x, mem, lp, rel_bias):
    b, s, _ = x.shape
    bi = branch_inputs(x, lp)
    o_a = sb_prompt(bi['qA'], bi['kA'], bi['vA'])
    kcmp = rmsnorm(compress_blocks(bi['kc'], lp['nsa_pe_k'], lp['nsa_phi_k']), lp['nsa_kn_g'][0])
    vcmp = compress_blocks(bi['vc'], lp['nsa_pe_v'], lp['nsa_phi_v'])
    ks_blk = to_blocks(bi['ks'], SEL_BLOCK)
    vs_blk = to_blocks(bi['vs'], SEL_BLOCK)
    kw_pad = jnp.pad(bi['kw'], ((0, 0), (WINDOW, 0), (0, 0)))
    vw_pad = jnp.pad(bi['vw'], ((0, 0), (WINDOW, 0), (0, 0)))

    def nsa_body(args):
        q_blk, g_blk, i = args
        q_pos = i * QBLK + jnp.arange(QBLK, dtype=jnp.int32)
        kw_seg = lax.dynamic_slice_in_dim(kw_pad, i * QBLK, WINDOW + QBLK, axis=1)
        vw_seg = lax.dynamic_slice_in_dim(vw_pad, i * QBLK, WINDOW + QBLK, axis=1)
        kw_pos = i * QBLK - WINDOW + jnp.arange(WINDOW + QBLK, dtype=jnp.int32)
        return nsa_attend(q_blk, g_blk, q_pos, kcmp, vcmp, ks_blk, vs_blk, kw_seg, vw_seg, kw_pos, rel_bias)

    o_b = un_q_blocks(lax.map(nsa_body, (q_blocks(bi['qB']), q_blocks(bi['gB']),
                                         jnp.arange(s // QBLK, dtype=jnp.int32))))
    s0 = jnp.zeros((b, C_HEADS, C_DK, C_DV), dtype=x.dtype)
    o_c, s_fin = gla_chunked(bi['qC'], bi['kC'], bi['vC'], bi['la'], s0)
    mk, mv = mem_kv(mem, lp)
    o_m = mem_attend(bi['qM'], mk, mv)
    y = finish_layer(x, bi, o_a, o_b, o_c, o_m, lp)
    wb = min(WINDOW, s)
    return y, (bi['kA'], bi['vA'], bi['kc'], bi['vc'], bi['ks'], bi['vs'],
               bi['kw'][:, s - wb:], bi['vw'][:, s - wb:], s_fin, mk, mv)

def layer_sample(x, c_sbk, c_sbv, c_ck, c_cv, c_sk, c_sv, c_wk, c_wv, s_gla, c_mk, c_mv, page_table, lp, rel_bias):
    b, l, _ = x.shape
    past = page_table.shape[1] * c_sbk.shape[1]
    gather = lambda c: c[page_table].reshape((b, past) + c.shape[2:])
    bi = branch_inputs(x, lp)
    q_pos = past + jnp.arange(l, dtype=jnp.int32)
    k_a = jnp.concatenate([gather(c_sbk), bi['kA']], axis=1)
    v_a = jnp.concatenate([gather(c_sbv), bi['vA']], axis=1)
    o_a = stick_breaking(bi['qA'], k_a, v_a, q_pos, jnp.arange(past + l, dtype=jnp.int32))
    kc_all = jnp.concatenate([gather(c_ck), bi['kc']], axis=1)
    vc_all = jnp.concatenate([gather(c_cv), bi['vc']], axis=1)
    kcmp = rmsnorm(compress_blocks(kc_all, lp['nsa_pe_k'], lp['nsa_phi_k']), lp['nsa_kn_g'][0])
    vcmp = compress_blocks(vc_all, lp['nsa_pe_v'], lp['nsa_phi_v'])
    ks_blk = to_blocks(jnp.concatenate([gather(c_sk), bi['ks']], axis=1), SEL_BLOCK)
    vs_blk = to_blocks(jnp.concatenate([gather(c_sv), bi['vs']], axis=1), SEL_BLOCK)
    wb = c_wk.shape[1]
    kw_all = jnp.concatenate([c_wk, bi['kw']], axis=1)
    vw_all = jnp.concatenate([c_wv, bi['vw']], axis=1)
    kw_pos = past - wb + jnp.arange(wb + l, dtype=jnp.int32)
    o_b = nsa_attend(bi['qB'], bi['gB'], q_pos, kcmp, vcmp, ks_blk, vs_blk, kw_all, vw_all, kw_pos, rel_bias)
    o_c, s_new = gla_chunked(bi['qC'], bi['kC'], bi['vC'], bi['la'], s_gla)
    o_m = mem_attend(bi['qM'], c_mk, c_mv)
    y = finish_layer(x, bi, o_a, o_b, o_c, o_m, lp)
    wbn = min(WINDOW, wb + l)
    return y, (bi['kA'], bi['vA'], bi['kc'], bi['vc'], bi['ks'], bi['vs'],
               kw_all[:, wb + l - wbn:], vw_all[:, wb + l - wbn:], s_new)

def setup_inputs(seed: int = 0) -> dict:
    key = jax.random.key(seed)
    keys = iter(jax.random.split(key, 48))
    f32 = jnp.float32
    nrm = lambda shape, scale: jax.random.normal(next(keys), shape, f32) * scale
    gain = lambda shape: 1.0 + 0.05 * jax.random.normal(next(keys), shape, f32)
    n_pages = PAST_LEN // PAGE_SIZE
    n_pool = (DEC_BATCH * n_pages * 5 + 3) // 4
    win_buf = min(WINDOW, PAST_LEN)
    return {
        'x_prompt': nrm((BATCH, SEQ, D_MODEL), 1.0),
        'x_sample': nrm((DEC_BATCH, DEC_SEQ, D_MODEL), 1.0),
        'mem_prompt': nrm((BATCH, 256, D_MODEL), 1.0),
        'cache_sb_k': nrm((DEPTH, n_pool, PAGE_SIZE, A_HEADS, A_DH), 1.0),
        'cache_sb_v': nrm((DEPTH, n_pool, PAGE_SIZE, A_HEADS, A_DH), 1.0),
        'cache_nsa_cmp_k': nrm((DEPTH, n_pool, PAGE_SIZE, B_DH), 1.0),
        'cache_nsa_cmp_v': nrm((DEPTH, n_pool, PAGE_SIZE, B_DH), 1.0),
        'cache_nsa_sel_k': nrm((DEPTH, n_pool, PAGE_SIZE, B_DH), 1.0),
        'cache_nsa_sel_v': nrm((DEPTH, n_pool, PAGE_SIZE, B_DH), 1.0),
        'cache_nsa_win_k': nrm((DEPTH, DEC_BATCH, win_buf, B_DH), 1.0),
        'cache_nsa_win_v': nrm((DEPTH, DEC_BATCH, win_buf, B_DH), 1.0),
        'state_gla': nrm((DEPTH, DEC_BATCH, C_HEADS, C_DK, C_DV), 0.5),
        'cache_mem_k': nrm((DEPTH, DEC_BATCH, 256, M_HEADS, M_DH), 1.0),
        'cache_mem_v': nrm((DEPTH, DEC_BATCH, 256, M_HEADS, M_DH), 1.0),
        'page_table': jax.random.permutation(next(keys), n_pool)[:DEC_BATCH * n_pages].reshape(DEC_BATCH, n_pages).astype(jnp.int32),
        'norm_mix_g': gain((DEPTH, D_MODEL)),
        'norm_ffn_g': gain((DEPTH, D_MODEL)),
        'norm_mem_g': gain((DEPTH, D_MODEL)),
        'w_in': nrm((DEPTH, D_MODEL, N_IN), D_MODEL ** -0.5),
        'gla_gate_up': nrm((DEPTH, C_RANK, C_HEADS * C_DK), C_RANK ** -0.5),
        'gla_gate_b': nrm((DEPTH, C_HEADS * C_DK), 0.1),
        'gla_norm_g': gain((DEPTH, C_DV)),
        'nsa_pe_k': nrm((DEPTH, CMP_BLOCK, B_DH), 0.1),
        'nsa_pe_v': nrm((DEPTH, CMP_BLOCK, B_DH), 0.1),
        'nsa_phi_k': nrm((DEPTH, B_DH, B_DH), B_DH ** -0.5),
        'nsa_phi_v': nrm((DEPTH, B_DH, B_DH), B_DH ** -0.5),
        'nsa_qn_g': gain((DEPTH, B_DH)),
        'nsa_kn_g': gain((DEPTH, 3, B_DH)),
        'mem_qn_g': gain((DEPTH, M_DH)),
        'mem_kn_g': gain((DEPTH, M_DH)),
        'w_mem_kv': nrm((DEPTH, D_MODEL, 2 * M_HEADS * M_DH), D_MODEL ** -0.5),
        'w_branch': nrm((DEPTH, N_BRANCH, BRANCH_W, D_MODEL), BRANCH_W ** -0.5),
        'w_out': nrm((DEPTH, D_MODEL, D_MODEL), D_MODEL ** -0.5),
        'rel_bias': nrm((N_BUCKETS, B_HEADS), 0.2),
        'w_grp': nrm((DEPTH, D_MODEL, N_GROUPS), D_MODEL ** -0.5),
        'b_grp': nrm((DEPTH, N_GROUPS), 0.01),
        'w_rt': nrm((DEPTH, D_MODEL, N_EXPERTS), D_MODEL ** -0.5),
        'b_rt': nrm((DEPTH, N_EXPERTS), 0.01),
        'w_eg': nrm((DEPTH, N_EXPERTS, D_MODEL, D_EXPERT), D_MODEL ** -0.5),
        'w_eu': nrm((DEPTH, N_EXPERTS, D_MODEL, D_EXPERT), D_MODEL ** -0.5),
        'w_ed': nrm((DEPTH, N_EXPERTS, D_EXPERT, D_MODEL), D_EXPERT ** -0.5),
    }

def reference(x_prompt, x_sample, mem_prompt, cache_sb_k, cache_sb_v, cache_nsa_cmp_k, cache_nsa_cmp_v,
              cache_nsa_sel_k, cache_nsa_sel_v, cache_nsa_win_k, cache_nsa_win_v, state_gla, cache_mem_k,
              cache_mem_v, page_table, norm_mix_g, norm_ffn_g, norm_mem_g, w_in, gla_gate_up, gla_gate_b,
              gla_norm_g, nsa_pe_k, nsa_pe_v, nsa_phi_k, nsa_phi_v, nsa_qn_g, nsa_kn_g, mem_qn_g, mem_kn_g,
              w_mem_kv, w_branch, w_out, rel_bias, w_grp, b_grp, w_rt, b_rt, w_eg, w_eu, w_ed):
    xp, xs = x_prompt, x_sample
    p_states, s_states = [], []
    for l in range(DEPTH):
        lp = dict(norm_mix_g=norm_mix_g[l], norm_ffn_g=norm_ffn_g[l], norm_mem_g=norm_mem_g[l], w_in=w_in[l],
                  gla_gate_up=gla_gate_up[l], gla_gate_b=gla_gate_b[l], gla_norm_g=gla_norm_g[l],
                  nsa_pe_k=nsa_pe_k[l], nsa_pe_v=nsa_pe_v[l], nsa_phi_k=nsa_phi_k[l], nsa_phi_v=nsa_phi_v[l],
                  nsa_qn_g=nsa_qn_g[l], nsa_kn_g=nsa_kn_g[l], mem_qn_g=mem_qn_g[l], mem_kn_g=mem_kn_g[l],
                  w_mem_kv=w_mem_kv[l], w_branch=w_branch[l], w_out=w_out[l], w_grp=w_grp[l], b_grp=b_grp[l],
                  w_rt=w_rt[l], b_rt=b_rt[l], w_eg=w_eg[l], w_eu=w_eu[l], w_ed=w_ed[l])
        xp, sp = layer_prompt(xp, mem_prompt, lp, rel_bias)
        xs, ss = layer_sample(xs, cache_sb_k[l], cache_sb_v[l], cache_nsa_cmp_k[l], cache_nsa_cmp_v[l],
                              cache_nsa_sel_k[l], cache_nsa_sel_v[l], cache_nsa_win_k[l], cache_nsa_win_v[l],
                              state_gla[l], cache_mem_k[l], cache_mem_v[l], page_table, lp, rel_bias)
        p_states.append(sp)
        s_states.append(ss)
    (p_sb_k, p_sb_v, p_cmp_k, p_cmp_v, p_sel_k, p_sel_v, p_win_k, p_win_v, p_gla, p_mem_k, p_mem_v) = [
        jnp.stack(t, axis=0) for t in zip(*p_states)]
    (s_sb_k, s_sb_v, s_cmp_k, s_cmp_v, s_sel_k, s_sel_v, s_win_k, s_win_v, s_gla) = [
        jnp.stack(t, axis=0) for t in zip(*s_states)]
    return (xp, xs, p_sb_k, p_sb_v, p_cmp_k, p_cmp_v, p_sel_k, p_sel_v, p_win_k, p_win_v, p_gla, p_mem_k, p_mem_v,
            s_sb_k, s_sb_v, s_cmp_k, s_cmp_v, s_sel_k, s_sel_v, s_win_k, s_win_v, s_gla)


_drawn_inputs = setup_inputs


def setup_inputs(seed=0):
    import zlib

    import numpy as np

    out = dict(_drawn_inputs(seed))
    spreads = {}
    factors = {'cache_nsa_cmp_k': 4.587,
     'cache_nsa_cmp_v': 8.0,
     'gla_norm_g': 2.901,
     'nsa_pe_k': 8.0,
     'nsa_pe_v': 8.0,
     'nsa_phi_k': 3.12,
     'nsa_qn_g': 8.0,
     'mem_qn_g': 7.644,
     'rel_bias': 4.258,
     'b_grp': 3.463,
     'b_rt': 17.974}
    for name, (base, spread) in spreads.items():
        noise = np.random.default_rng([zlib.crc32(name.encode()), seed]).standard_normal(out[name].shape)
        drawn = base * np.exp(spread * noise) if base else spread * noise
        out[name] = jnp.asarray(drawn.astype(out[name].dtype))
    for name, factor in factors.items():
        out[name] = (out[name] * factor).astype(out[name].dtype)
    return out
```

```python
import math
from contextlib import ExitStack

import numpy as np

import concourse.bass as bass
from concourse import mybir

F32 = mybir.dt.float32
I32 = mybir.dt.int32
U32 = mybir.dt.uint32
ALU = mybir.AluOpType
ACT = mybir.ActivationFunctionType
AX = mybir.AxisListType

D = 1024
KD = D // 128
SEQ = 1024
NT = SEQ // 128
NB = 8
NCOL = SEQ + NB
MEM = 256
PAST = 4096
PAGE = 128
NPAGE = PAST // PAGE
NP1 = 2460
CH = 492
NCH = NP1 // CH
EPS = 1e-6
NEG = -1e30
NE = 16
DE = 256
(SBQ, SBK, SBV, NQ, KC, VC, KS, VS, KW, VW, NG, GQ, GK, GV, GA, GR, MQ) = (
    0, 256, 512, 768, 1024, 1088, 1152, 1216, 1280, 1344, 1408, 1420, 1548, 1676, 1932, 1948, 2204)
QNB, QNM, QNS, QNW = 0, 256, 512, 640
(RQA, RQB, RQM, RKS, RVS, RKW, RVW, RG, RW) = (0, 256, 512, 768, 832, 896, 960, 1024, 1036)


def bucket(dist):
    n = np.maximum(dist, 0)
    nf = np.maximum(n, 1).astype(np.float32)
    large = 16 + (np.log(nf / np.float32(16)) / np.float32(math.log(8)) * np.float32(16)).astype(np.int32)
    return np.where(n < 16, n, np.minimum(large, 31))


def onehot(dist):
    row = np.where(dist < 0, 32, bucket(dist))
    return (np.arange(33).reshape((33,) + (1,) * dist.ndim) == row[None]).astype(np.float32)


OHC = 1984
NEAR = 384
NSEL, NWIN = 33, 5


def shape_constants():
    p = np.arange(128)
    a, b = p[:, None], p[None, :]
    same = (a // 64) == (b // 64)
    mid = (b // 64) * 64 + 31
    c = {}
    c["ident"] = (a == b)
    c["ones"] = np.ones((128, 128))
    c["gm_mid"] = -(1.0 * (a <= b) * same - 1.0 * (a <= mid) * same) / 16.0
    c["gm_cum"] = -1.0 * (a <= b) * same / 16.0
    c["gm_suf"] = -1.0 * (a > b) * same / 16.0
    c["glamask"] = 1.0 * (a <= b) * same
    c["bd256"] = 1.0 * ((a // 32) == (np.arange(256)[None, :] // 64))
    c["ind2"] = ((a // 64) == np.arange(2)[None, :]) / 64.0
    c["hcol"] = np.stack([p < 64, p >= 64], 1)
    c["eye88"] = 1.0 * np.broadcast_to((np.arange(64) // 8) == (np.arange(64) % 8), (128, 64))
    c["negtri"] = -1.0 * (a >= b)
    c["negones"] = -np.ones((128, 128))
    c["causal01"] = 1.0 * (a < b)
    c["causalneg"] = NEG * (a >= b)
    c["winneg"] = NEG * (b < a)
    c["strict"] = 1.0 * (a > b)
    c["blk4"] = 1.0 * (a == (np.arange(256)[None, :] // 64))
    c["pair"] = ((a // 2) == np.arange(64)[None, :]) / 64.0
    c["rep16"] = 1.0 * (a == (np.arange(64)[None, :] % 16))
    c["cbd"] = 1.0 * ((a // 16) == (np.arange(256)[None, :] // 64))
    c["restart"] = np.broadcast_to(1.0 * ((np.arange(128) % 32) != 31), (128, 128))
    c["expand"] = 1.0 * (a == (b // 2))
    c["jlti"] = 1.0 * (np.arange(64)[None, :] < a)
    forced = 1e9 * np.isin(np.arange(64), (0, 63)).astype(np.float64)
    c["forced"] = np.broadcast_to(forced, (128, 64))
    c["onehot8"] = 1.0 * (a == (np.arange(1024)[None, :] // 128))
    at, out, cols = {}, [], 0
    for name, v in c.items():
        v = np.broadcast_to(v, (128, v.shape[1])).astype(np.float32)
        at[name] = (cols, v.shape[1])
        cols += v.shape[1]
        out.append(v)
    return at, np.ascontiguousarray(np.concatenate(out, 1))


def distance_onehots():
    p = np.arange(128)
    parts = [onehot(np.arange(OHC) - 1023)]
    r = np.arange(NSEL)[:, None]
    parts.append(onehot(np.where(r < 32, PAST - 32 * p[None] - r, np.where(p[None] == 0, 0, -1))).reshape(33, -1))
    r = np.arange(NWIN)[:, None]
    parts.append(onehot(np.where(r < 4, 512 - 4 * p[None] - r, np.where(p[None] == 0, 0, -1))).reshape(33, -1))
    parts.append(onehot(PAST - 64 * np.arange(64) - 63))
    parts.append(onehot(255 - np.arange(NEAR)))
    return np.ascontiguousarray(np.concatenate(parts, 1))


def row_offsets():
    p = np.arange(128)[:, None]
    return np.ascontiguousarray(np.concatenate([(p % 4) * 8 + np.arange(8)[None], p % 4], 1).astype(np.int32))


class Chain:

    def __init__(self, eng, sem):
        self.eng, self.sem, self.base, self.n = eng, sem, 0, 0

    def __call__(self, ins):
        self.n += 1
        ins.then_inc(self.sem, 1)
        self.eng.wait_ge(self.sem, self.base + self.n)

    def enter(self, i, per):
        self.start = self.base + self.n
        self.base, self.n, self.per = self.start + i * per, 0, per

    def leave(self, trips, unrolled=1):
        assert self.n == self.per * unrolled, f"chain {self.sem}: {self.n} steps in the body"
        self.base, self.n = self.start + trips * self.per, 0


CHAIN_V1, CHAIN_A1 = 11, 6
SMALL = 10240


def build(nc, I, O, consts_at, C_d, OH_d, RO_d, stages):
    ctx = ExitStack()
    with ctx:
        ctx.enter_context(nc.allow_non_contiguous_dma(reason="small gains and biases"))

        def sb(name, shape, dt=F32):
            return ctx.enter_context(nc.sbuf_tensor(name, shape, dt))

        def sem(name):
            live.append(nc.alloc_semaphore(name))
            return live[-1]

        live = []

        def stage_over():
            nc.clear_and_free_semaphores(live)
            live.clear()
            nc.all_engine_barrier()

        hT_d = nc.dram_tensor("hT_scratch", [128, KD, SEQ], F32).ap()
        srow_d = nc.dram_tensor("sample_rows", [NB, RW], F32).ap()
        skew_d = nc.dram_tensor("near_bias", [128, 4, NEAR], F32)
        osam_d = nc.dram_tensor("sample_branch_rows", [NB, 1024], F32).ap()

        c_early, c_late = consts_at["negtri"][0], consts_at["onehot8"][0]
        cst = sb("cst", [128, c_early])

        def K(name, r=128):
            a, w = consts_at[name]
            return cst[0:r, a:a + w] if a < c_early else late[0:r, a - c_early:a - c_early + w]

        eps = sb("eps", [128, 1])
        one = sb("one", [128, 1])
        g_mix, g_ffn, g_mem = sb("g_mix", [128, KD]), sb("g_ffn", [128, KD]), sb("g_mem", [128, KD])
        qn_gain = sb("qn_gain", [128, 640])
        kn_mem = sb("kn_mem", [128, 64])
        kn_cmp = sb("kn_cmp", [128, 64])
        g_gla = sb("g_gla", [128, 64])
        pe_kv = sb("pe_kv", [64, 2, 64])
        phi_kv = sb("phi_kv", [64, 2, 64])
        pe_mean = sb("pe_mean", [64, 2])
        gate_up = sb("gate_up", [16, 128])
        gate_b = sb("gate_b", [1, 128])
        tab = sb("tab", [33, 4])
        TT = sb("TT", [128, 8, SEQ])
        VA = sb("VA", [128, NT, 256])
        VSt = sb("VSt", [128, NT, 64])
        VWt = sb("VWt", [128, NT, 64])
        KWt = sb("KWt", [128, NT, 64])
        NGt = sb("NGt", [128, NT, 12])
        OT = sb("OT", [128, 8, NCOL])
        kmT = sb("kmT", [64, 2, 16])
        hT_s = sb("hT_s", [128, KD, NB])
        arena = sb("arena", [128, KD * NP1])
        W1 = arena[:, :].rearrange("p (j n) -> p j n", j=KD)
        wmem = TT[:, 0:4, :].rearrange("p a b -> p (a b)").rearrange("p (j n) -> p j n", j=KD)
        early = OT[:, 0:4, :].rearrange("p a b -> p (a b)")
        xt = early[:, 0:1024]
        xn = early[:, 1024:2048]
        hTs = early[:, 2048:3072].rearrange("p (j t) -> p j t", j=KD)
        sqx = early[:, 3072:4096]
        small = sb("small", [128, SMALL])
        late_w = c_late - c_early
        late = arena[:, 0:late_w]
        cursor = [0]

        def tmp(*dims, r=128):
            n = int(np.prod(dims))
            v = small[0:r, cursor[0]:cursor[0] + n]
            cursor[0] += n
            assert cursor[0] <= SMALL, cursor[0]
            if len(dims) == 2:
                return v.rearrange("p (a b) -> p a b", a=dims[0])
            if len(dims) == 3:
                return v.rearrange("p (a b c) -> p a b c", a=dims[0], b=dims[1])
            return v

        P = tmp(NP1)
        sq = tmp(768)
        QN = tmp(768)
        ss, r10 = tmp(10), tmp(10)
        ssq, lnx, rstd = tmp(1), tmp(1), tmp(1)
        mq = tmp(2, 2, 128)
        mkT = tmp(2, MEM)
        mv = tmp(2, 256)
        mp = sqx.rearrange("p (a b) -> p a b", a=4)
        mpT = xn.rearrange("p (a b) -> p a b", a=8)
        nmx, lm, rlm = tmp(4), tmp(4), tmp(4)
        gqT, gkT = tmp(128), tmp(128)
        aT = tmp(128, r=16)
        pab, pln, sp = tmp(128), tmp(128), tmp(128)
        cclip = tmp(128)
        Emid, Eimid, Ecum, Esuf = (sq[:, n * 128:(n + 1) * 128] for n in range(4))
        q1bd = tmp(4, 128)
        k1T = tmp(128)
        q3 = tmp(2, 128)
        k4 = tmp(2, 128)
        attm = tmp(4, 128)
        updm = tmp(2, 256)
        Sa, Sb = tmp(256), tmp(256)
        er = tmp(256)
        sil = er
        oCM = tmp(512)
        sq2 = sq[:, 512:768]
        s4, l4, r4 = tmp(4), tmp(4), tmp(4)
        km8 = TT[0:8, 5, :].rearrange("p (a b) -> p a b", a=8)
        oh8 = TT[0:8, 6, :].rearrange("p (a b) -> p a b", a=8)
        S0s = TT[:, 4, 0:512].rearrange("p (a b) -> p a b", a=8)
        S1s = TT[:, 4, 512:1024].rearrange("p (a b) -> p a b", a=8)
        qTm = tmp(8, 8)
        PS = ctx.enter_context(nc.psum_tensor("PS", [128, 4096], F32))

        def bank(b, n=1):
            return PS[:, b * 512:(b + n) * 512]

        (c_in, w_in_s, x_in, hT_out, rows_out, kv_out, const_ready, rstd_ready, xn_ready, xn_tp, hts_ready,
         kv_done, kv_p, proj_done, p_ready, sq_ready, ss_ready, r_ready, qn_ready, qn_tp, tt_evac, slots_ready,
         kv_tp, mk_ready, km_done, km_evac, aT_tp, aT_ready, pre_done, ln_ready, sp_ready, cum_done, clip_ready,
         exps_ready, gl_ready, att_done, attm_ready, upd_done, sb_ready, oc_done, sa_ready, sq2_ready, s4_ready,
         r4_ready, er_ready, oc_ready, msc_done, nmx_ready, mp_ready, mpt_tp, mpt_evac, mo_done, om_ready, ot_tp,
         ot_evac, pool_done, seT_done, seT_ready, supd_done, supd_used, sbd_ready, chA, chV, w_done, gla_out) = (
            sem(n) for n in (
                "c_in", "w_in_s", "x_in", "hT_out", "rows_out", "kv_out", "const_ready", "rstd_ready", "xn_ready",
                "xn_tp", "hts_ready", "kv_done", "kv_p", "proj_done", "p_ready", "sq_ready", "ss_ready", "r_ready",
                "qn_ready", "qn_tp", "tt_evac", "slots_ready", "kv_tp", "mk_ready", "km_done", "km_evac", "aT_tp",
                "aT_ready", "pre_done", "ln_ready", "sp_ready", "cum_done", "clip_ready", "exps_ready", "gl_ready",
                "att_done", "attm_ready", "upd_done", "sb_ready", "oc_done", "sa_ready", "sq2_ready", "s4_ready",
                "r4_ready", "er_ready", "oc_ready", "msc_done", "nmx_ready", "mp_ready", "mpt_tp", "mpt_evac",
                "mo_done", "om_ready", "ot_tp", "ot_evac", "pool_done", "seT_done", "seT_ready", "supd_done",
                "supd_used", "sbd_ready", "chA", "chV", "w_done", "gla_out"))

        w_in = I["w_in"][0]
        W1_d = w_in.rearrange("(p j) n -> p j n", j=KD)
        x_p = I["x_prompt"][0]
        x_s = I["x_sample"][:, 0, :]
        mem_d = I["mem_prompt"][0]
        stage1 = ExitStack()
        block = stage1.enter_context(nc.Block())
        CIN = [0]
        ROWS_S, ROWS_P = 15, 6

        def wait_min(eng, s, v):
            if not (isinstance(v, int) and v <= 0):
                eng.wait_ge(s, v)

        @block.sync
        def _(sp_e):
            def load(dst, src, s=c_in):
                sp_e.dma_start(dst, src).then_inc(s, 16)
                if s is c_in:
                    CIN[0] += 16

            load(xt, mem_d[0:128, :], x_in)
            load(cst[:, :], C_d[:, 0:c_early])
            load(TT[0:8, 6, :], C_d[0:8, c_late:c_late + 1024])
            for g, n in ((g_mix, "norm_mix_g"), (g_ffn, "norm_ffn_g"), (g_mem, "norm_mem_g")):
                load(g[:, :], I[n][0].rearrange("(p j) -> p j", j=KD))
            load(wmem, I["w_mem_kv"][0].rearrange("(p j) n -> p j n", j=KD))
            for h in range(4):
                load(qn_gain[:, h * 64:(h + 1) * 64], I["nsa_qn_g"][0:1].broadcast_to([128, 64]))
                load(qn_gain[:, 256 + h * 64:256 + (h + 1) * 64], I["mem_qn_g"][0:1].broadcast_to([128, 64]))
            load(qn_gain[:, 512:576], I["nsa_kn_g"][0, 1:2].broadcast_to([128, 64]))
            load(qn_gain[:, 576:640], I["nsa_kn_g"][0, 2:3].broadcast_to([128, 64]))
            load(kn_cmp[:, :], I["nsa_kn_g"][0, 0:1].broadcast_to([128, 64]))
            load(kn_mem[:, :], I["mem_kn_g"][0:1].broadcast_to([128, 64]))
            load(g_gla[:, :], I["gla_norm_g"][0:1].broadcast_to([128, 64]))
            for n, (a, b) in enumerate((("nsa_pe_k", "nsa_phi_k"), ("nsa_pe_v", "nsa_phi_v"))):
                load(pe_kv[:, n, :], I[a][0])
                load(phi_kv[:, n, :], I[b][0])
            load(gate_up[:, :], I["gla_gate_up"][0])
            load(gate_b[:, :], I["gla_gate_b"][0:1])
            load(tab[0:32, :], I["rel_bias"])
            load(S0s[:, :, :], I["state_gla"][0].rearrange("b h k v -> (h k) b v"))
            load(W1, W1_d[:, :, 0:NP1], w_in_s)
            load(O[19][0, :, 0:511, :], I["cache_nsa_win_k"][0, :, 1:512, :], rows_out)
            load(O[20][0, :, 0:511, :], I["cache_nsa_win_v"][0, :, 1:512, :], hT_out)

            sp_e.wait_ge(xn_ready, 1)
            load(xt, mem_d[128:256, :], x_in)
            for u in range(2):
                sp_e.wait_ge(mk_ready, u + 1)
                load(O[11][0, 0, u * 128:(u + 1) * 128].rearrange("t h d -> t (h d)"), QN[:, 0:256], kv_out)
                load(O[12][0, 0, u * 128:(u + 1) * 128].rearrange("t h d -> t (h d)"), mv[:, u, :], kv_out)
            sp_e.wait_ge(xn_ready, 2)
            load(xt[0:8, :], x_s, x_in)
            sp_e.wait_ge(xn_ready, 3)
            load(xt, x_p[0:128, :], x_in)
            sp_e.wait_ge(p_ready, NCH)
            for c, w, o in ((SBK, 256, 13), (SBV, 256, 14)):
                load(O[o][0, :, 0].rearrange("t h d -> t (h d)"), P[0:8, c:c + w], rows_out)
            for c, o in ((KC, 15), (VC, 16), (VS, 18)):
                load(O[o][0, :, 0, :], P[0:8, c:c + 64], rows_out)
            load(O[20][0, :, 511, :], P[0:8, VW:VW + 64], rows_out)
            load(srow_d[:, RQA:RQA + 256], P[0:8, SBQ:SBQ + 256], rows_out)
            load(srow_d[:, RVS:RVS + 64], P[0:8, VS:VS + 64], rows_out)
            load(srow_d[:, RVW:RVW + 64], P[0:8, VW:VW + 64], rows_out)
            load(srow_d[:, RG:RG + 12], P[0:8, NG:NG + 12], rows_out)
            sp_e.wait_ge(qn_ready, 1)
            load(O[17][0, :, 0, :], QN[0:8, QNS:QNS + 64], rows_out)
            load(O[19][0, :, 511, :], QN[0:8, QNW:QNW + 64], rows_out)
            load(srow_d[:, RQB:RQB + 512], QN[0:8, 0:512], rows_out)
            load(srow_d[:, RKS:RKS + 64], QN[0:8, QNS:QNS + 64], rows_out)
            load(srow_d[:, RKW:RKW + 64], QN[0:8, QNW:QNW + 64], rows_out)

            def tile(i, last=False):
                rows = bass.ds(i * 128, 128)
                sp_e.wait_ge(hts_ready, i + 4)
                sp_e.dma_start(hT_d[:, :, rows], hTs).then_inc(hT_out, 16)
                if not last:
                    sp_e.wait_ge(xn_ready, i + 4)
                    sp_e.dma_start(xt, x_p[bass.ds(i * 128 + 128, 128), :]).then_inc(x_in, 16)
                sp_e.wait_ge(p_ready, i * NCH + 2 * NCH)
                for c, o in ((SBK, 2), (SBV, 3)):
                    sp_e.dma_start(O[o][0, 0, rows].rearrange("t h d -> t (h d)"),
                                   P[:, c:c + 256]).then_inc(rows_out, 16)
                for c, o in ((KC, 4), (VC, 5), (VS, 7)):
                    sp_e.dma_start(O[o][0, 0, rows, :], P[:, c:c + 64]).then_inc(rows_out, 16)
                sp_e.wait_ge(qn_ready, i + 2)
                sp_e.dma_start(O[6][0, 0, rows, :], QN[:, QNS:QNS + 64]).then_inc(rows_out, 16)

            sp_e.wait_ge(sbd_ready, 8)
            load(O[21][0].rearrange("b h k v -> (h k) b v"), S1s, gla_out)
            with sp_e.Fori(0, NT - 1) as i:
                tile(i)
            tile(NT - 1, last=True)
            sp_e.wait_ge(pool_done, NT + 1)
            sp_e.dma_start(O[8][0, 0].rearrange("(j p) d -> p j d", p=128), KWt[:, 4:8, :]).then_inc(rows_out, 16)
            sp_e.dma_start(O[9][0, 0].rearrange("(j p) d -> p j d", p=128), VWt[:, 4:8, :]).then_inc(rows_out, 16)
            sp_e.wait_ge(sa_ready, NT + 1)
            for h in range(4):
                sp_e.dma_start(O[10][0, 0, h], Sa[32 * h:32 * h + 32, 64 * h:64 * h + 64]).then_inc(gla_out, 16)
            sp_e.wait_ge(gla_out, 80)
            sp_e.wait_ge(hT_out, 16 * NT + 16)
            sp_e.wait_ge(kv_out, 64)
            sp_e.wait_ge(rows_out, 16 * (1 + ROWS_S + ROWS_P * NT + 2))
            sp_e.wait_ge(ot_evac, NT + 1)

        @block.gpsimd
        def _(pool):
            def tile(i):
                for dst, src, w in ((VA, SBV, 256), (VSt, VS, 64), (VWt, VW, 64), (NGt, NG, 12)):
                    if dst is VA:
                        pool.wait_ge(p_ready, i * NCH + 2 * NCH)
                    nc.gpsimd.tensor_copy(dst[:, bass.ds(i, 1), :], P[:, None, src:src + w])
                pool.wait_ge(qn_ready, i + 2)
                nc.gpsimd.tensor_copy(KWt[:, bass.ds(i, 1), :], QN[:, None, QNW:QNW + 64]).then_inc(pool_done, 1)

            nc.gpsimd.memset(NGt[:, :, :], 0.0).then_inc(pool_done, 1)
            pool.wait_ge(pool_done, 1)
            with pool.Fori(0, NT) as i:
                tile(i)

        @block.scalar
        def _(act):
            chain = Chain(act, chA)
            A = nc.scalar.activation

            def norm(k, R):
                act.wait_ge(x_in, 16 * (k + 1))
                chain(A(sqx[0:R, :], xt[0:R, :], ACT.Square, accum_out=ssq[0:R, :]))
                chain(A(lnx[0:R, :], ssq[0:R, :], ACT.Ln, bias=eps[0:R, :], scale=1.0 / D))
                wait_min(act, xn_ready, k)
                A(rstd[0:R, :], lnx[0:R, :], ACT.Exp, scale=-0.5).then_inc(rstd_ready, 1)

            def head_rstd(k, R, n):
                act.wait_ge(ss_ready, k + 1)
                chain(A(r10[0:R, 0:n], ss[0:R, 0:n], ACT.Ln, bias=eps[0:R, :], scale=1.0 / 64))
                A(r10[0:R, 0:n], r10[0:R, 0:n], ACT.Exp, scale=-0.5).then_inc(r_ready, 1)

            act.wait_ge(const_ready, 1)
            nc.scalar.preload_act_table_set("natural_log_exp_and_others")
            for u in range(2):
                norm(u, 128)
                act.wait_ge(kv_done, u + 1)
                if u:
                    act.wait_ge(kv_tp, 1)
                    act.wait_ge(mk_ready, 1)
                chain(A(P[:, 0:512], bank(2), ACT.Copy))
                chain(A(mv[:, u, :], P[:, 256:512], ACT.Copy))
                A(sq[:, 0:256], P[:, 0:256], ACT.Square).then_inc(sq_ready, 1)
                head_rstd(u, 128, 4)
                act.wait_ge(kv_tp, u + 1)
                A(mkT[:, :, u * 128:(u + 1) * 128], bank(7)[:, 0:256].rearrange("p (a b) -> p a b", a=2),
                  ACT.Copy).then_inc(kv_p, 1)

            def tile(i, R):
                k, m = (2, 0) if i is None else (i + 3, i + 1)
                norm(k, R)
                if i is not None:
                    act.wait_ge(ot_evac, m)
                    act.wait_ge(pool_done, i + 1)
                    act.wait_ge(rows_out, 16 * (1 + ROWS_S) + i * (16 * ROWS_P))
                for c in range(NCH):
                    act.wait_ge(proj_done, m * NCH + (c + 1))
                    A(P[0:R, c * CH:(c + 1) * CH], bank((2, 3, 2, 3, 4)[c])[0:R, 0:CH], ACT.Copy).then_inc(p_ready, 1)
                act.wait_ge(p_ready, m * NCH + NCH)
                A(sq[0:R, 0:256], P[0:R, NQ:NQ + 256], ACT.Square)
                A(sq[0:R, 256:512], P[0:R, MQ:MQ + 256], ACT.Square)
                A(sq[0:R, 512:576], P[0:R, KS:KS + 64], ACT.Square)
                A(sq[0:R, 576:640], P[0:R, KW:KW + 64], ACT.Square).then_inc(sq_ready, 1)
                A(er[0:R, :], P[0:R, GR:GR + 256], ACT.Exp, scale=-1.0).then_inc(er_ready, 1)
                act.wait_ge(aT_tp, m + 1)
                A(aT[:, 0:R], bank(6)[0:16, 0:R], ACT.Copy).then_inc(aT_ready, 1)
                head_rstd(k, R, 10)
                act.wait_ge(pre_done, m + 1)
                pre = bank(6)[0:R, 128:256]
                chain(A(pab[0:R, :], pre, ACT.Abs))
                chain(A(pab[0:R, :], pab[0:R, :], ACT.Exp, scale=-1.0))
                A(pln[0:R, :], pab[0:R, :], ACT.Ln, bias=one[0:R, :]).then_inc(ln_ready, 1)
                if i is not None:
                    cols = bass.ds(i * 128, 128)
                    act.wait_ge(qn_tp, m + 1)
                    A(TT[:, 0:8, cols], bank(0, 2).rearrange("p (a b) -> p a b", a=8), ACT.Copy)
                    A(mq[0:64, :, 0, :], bank(7)[0:64, 0:256].rearrange("p (a b) -> p a b", a=2), ACT.Copy)
                    A(mq[64:128, :, 1, :], bank(7)[64:128, 0:256].rearrange("p (a b) -> p a b", a=2),
                      ACT.Copy).then_inc(tt_evac, 1)
                else:
                    act.wait_ge(qn_tp, m + 1)
                A(gqT[:, 0:R], bank(7)[:, 256:256 + R], ACT.Copy, scale=32 ** -0.5)
                A(gkT[:, 0:R], bank(7)[:, 384:384 + R], ACT.Copy).then_inc(slots_ready, 1)
                if i is not None:
                    act.wait_ge(km_done, i + 1)
                    A(kmT[:, :, bass.ds(i * 2, 2)], bank(4)[0:64, 0:4].rearrange("p (a b) -> p a b", a=2),
                      ACT.Copy).then_inc(km_evac, 1)
                    act.wait_ge(clip_ready, i + 1)
                    A(Emid[:, :], cclip[:, :], ACT.Exp)
                    A(Eimid[:, :], cclip[:, :], ACT.Exp, scale=-1.0)
                    A(Ecum[:, :], bank(7)[:, 128:256], ACT.Exp)
                    A(Esuf[:, :], bank(7)[:, 256:384], ACT.Exp).then_inc(exps_ready, 1)
                else:
                    act.wait_ge(seT_done, 1)
                    A(Ecum[:, 0:R], bank(7)[:, 0:R], ACT.Exp, scale=-1.0 / 16).then_inc(seT_ready, 1)
                act.wait_ge(oc_done, m + 1)
                A(sq2[0:R, :], bank(6)[0:R, 0:256], ACT.Square).then_inc(sq2_ready, 1)
                act.wait_ge(s4_ready, m + 1)
                chain(A(l4[0:R, :], s4[0:R, :], ACT.Ln, bias=eps[0:R, :], scale=1.0 / 64))
                A(r4[0:R, :], l4[0:R, :], ACT.Exp, scale=-0.5).then_inc(r4_ready, 1)
                if i is not None:
                    act.wait_ge(nmx_ready, i + 1)
                    for h in range(4):
                        last = A(mp[:, h, :], bank(5, 2)[:, h * 256:(h + 1) * 256], ACT.Exp, bias=nmx[:, h:h + 1],
                                 accum_out=lm[:, h:h + 1])
                    last.then_inc(mp_ready, 1)
                    act.wait_ge(mpt_tp, i + 1)
                    A(mpT[:, :, :], bank(0, 2).rearrange("p (a b) -> p a b", a=8), ACT.Copy).then_inc(mpt_evac, 1)
                    act.wait_ge(ot_tp, m + 1)
                    A(OT[:, 4:8, cols], bank(7).rearrange("p (a b) -> p a b", a=4), ACT.Copy).then_inc(ot_evac, 1)
                else:
                    act.wait_ge(ot_tp, 1)
                    A(OT[:, 4:6, SEQ:NCOL], bank(7)[:, 0:256].rearrange("p (a b) -> p a b", a=2)[:, :, 0:8],
                      ACT.Copy).then_inc(ot_evac, 1)

            tile(None, NB)
            act.wait_ge(gla_out, 16)
            with act.Fori(0, NT) as i:
                chain.enter(i, CHAIN_A1)
                tile(i, 128)
            chain.leave(NT)

        @block.vector
        def _(dve):
            chain = Chain(dve, chV)
            V = nc.vector
            V.memset(eps[:, :], EPS)
            V.memset(mq[:, :, :, :], 0.0)
            V.memset(q1bd[:, :, :], 0.0)
            V.memset(q3[:, :, :], 0.0)
            V.memset(tab[32:33, :], NEG)
            chain(V.memset(one[:, :], 1.0))
            dve.wait_ge(c_in, CIN[0])
            V.tensor_scalar(qn_gain[:, 0:512], qn_gain[:, 0:512], 0.125, None, ALU.mult)
            V.memset(Sa[:, :], 0.0).then_inc(const_ready, 1)
            dve.wait_ge(const_ready, 1)

            def norm(k, R, gain):
                dve.wait_ge(rstd_ready, k + 1)
                wait_min(dve, xn_tp, k)
                V.tensor_scalar(xn[0:R, :], xt[0:R, :], rstd[0:R, :], None, ALU.mult).then_inc(xn_ready, 1)
                dve.wait_ge(xn_tp, k + 1)
                V.tensor_tensor(hTs[:, :, 0:R], bank(0, 2).rearrange("p (j t) -> p j t", j=KD)[:, :, 0:R],
                                gain[:, :, None].broadcast_to([128, KD, R]), ALU.mult).then_inc(hts_ready, 1)

            def groups(k, R, n):
                dve.wait_ge(sq_ready, k + 1)
                V.tensor_reduce(ss[0:R, 0:n], sq[0:R, 0:64 * n].rearrange("p (a b) -> p a b", b=64), AX.X,
                                ALU.add).then_inc(ss_ready, 1)
                dve.wait_ge(r_ready, k + 1)

            for u in range(2):
                norm(u, 128, g_mem)
                groups(u, 128, 4)
                if u:
                    dve.wait_ge(kv_out, 32)
                    dve.wait_ge(kv_tp, 1)
                chain(V.tensor_tensor(QN[:, 0:256].rearrange("p (a b) -> p a b", b=64),
                                      P[:, 0:256].rearrange("p (a b) -> p a b", b=64),
                                      r10[:, 0:4, None].broadcast_to([128, 4, 64]), ALU.mult))
                V.tensor_tensor(QN[:, 0:256].rearrange("p (a b) -> p a b", b=64),
                                QN[:, 0:256].rearrange("p (a b) -> p a b", b=64),
                                kn_mem[:, None, :].broadcast_to([128, 4, 64]), ALU.mult).then_inc(mk_ready, 1)

            def tile(i, R):
                k, m = (2, 0) if i is None else (i + 3, i + 1)
                if i is None:
                    dve.wait_ge(kv_done, 2)
                else:
                    dve.wait_ge(proj_done, m * NCH)
                    dve.wait_ge(hT_out, i * 16 + 16)
                norm(k, R, g_mix)
                if i is None:
                    dve.wait_ge(hts_ready, 3)
                    V.tensor_copy(hT_s[:, :, :], hTs[:, :, 0:8])
                groups(k, R, 10)
                if i is None:
                    dve.wait_ge(kv_out, 64)
                    dve.wait_ge(kv_tp, 2)
                else:
                    dve.wait_ge(qn_tp, m)
                    dve.wait_ge(pool_done, i + 1)
                    dve.wait_ge(rows_out, 16 * (1 + ROWS_S) + i * (16 * ROWS_P))
                def part(dst, src, r, n):
                    return V.tensor_tensor(QN[0:R, dst:dst + 64 * n].rearrange("p (a b) -> p a b", b=64),
                                           P[0:R, src:src + 64 * n].rearrange("p (a b) -> p a b", b=64),
                                           r10[0:R, r:r + n, None].broadcast_to([R, n, 64]), ALU.mult)
                part(QNB, NQ, 0, 4)
                part(QNM, MQ, 4, 4)
                part(QNS, KS, 8, 1)
                chain(part(QNW, KW, 9, 1))
                V.tensor_tensor(QN[0:R, 0:512], QN[0:R, 0:512], qn_gain[0:R, 0:512], ALU.mult)
                chain(V.tensor_tensor(QN[0:R, 512:768].rearrange("p (a b) -> p a b", b=128)[:, :, 0:64],
                                QN[0:R, 512:768].rearrange("p (a b) -> p a b", b=128)[:, :, 0:64],
                                qn_gain[0:R, 512:640].rearrange("p (a b) -> p a b", b=64), ALU.mult))
                V.tensor_copy(QN[0:R, 512:768].rearrange("p (a b) -> p a b", b=128)[:, :, 64:128],
                              QN[0:R, 512:768].rearrange("p (a b) -> p a b", b=128)[:, :, 0:64]).then_inc(qn_ready, 1)
                dve.wait_ge(ln_ready, m + 1)
                chain(V.tensor_scalar(sp[0:R, :], bank(6)[0:R, 128:256], -1.0, 0.0, ALU.mult, ALU.max))
                V.tensor_tensor(sp[0:R, :], sp[0:R, :], pln[0:R, :], ALU.add).then_inc(sp_ready, 1)
                dve.wait_ge(er_ready, m + 1)
                chain(V.tensor_scalar(sil[0:R, :], er[0:R, :], 1.0, None, ALU.add))
                chain(V.reciprocal(sil[0:R, :], sil[0:R, :]))
                chain(V.tensor_tensor(sil[0:R, :], sil[0:R, :], P[0:R, GR:GR + 256], ALU.mult))
                chain(V.tensor_tensor(sil[0:R, :].rearrange("p (a b) -> p a b", b=64),
                                      sil[0:R, :].rearrange("p (a b) -> p a b", b=64),
                                      g_gla[0:R, None, :].broadcast_to([R, 4, 64]), ALU.mult))
                if i is not None:
                    dve.wait_ge(cum_done, i + 1)
                    V.tensor_scalar(cclip[:, :], bank(7)[:, 0:128], -40.0, 40.0, ALU.max, ALU.min).then_inc(clip_ready, 1)
                    dve.wait_ge(slots_ready, m + 1)
                    dve.wait_ge(exps_ready, i + 1)
                    for h in range(4):
                        r = slice(32 * h, 32 * h + 32)
                        V.tensor_tensor(q1bd[r, h, :], gqT[r, :], Emid[r, :], ALU.mult)
                    V.tensor_tensor(k1T[:, :], gkT[:, :], Eimid[:, :], ALU.mult)
                    for c in range(2):
                        V.tensor_tensor(q3[:, c, c * 64:c * 64 + 64], gqT[:, c * 64:c * 64 + 64],
                                        Ecum[:, c * 64:c * 64 + 64], ALU.mult)
                        last = V.scalar_tensor_tensor(k4[:, c, :], P[:, GK:GK + 128], K("hcol")[:, c:c + 1],
                                                      Esuf[:, :], ALU.mult, ALU.mult)
                    last.then_inc(gl_ready, 1)
                    dve.wait_ge(att_done, i + 1)
                    chain(V.tensor_scalar(attm[:, :, :].rearrange("p a b -> p (a b)"), bank(5), -1e30, 1e30, ALU.max, ALU.min))
                    V.tensor_tensor(attm[:, :, :], attm[:, :, :], K("glamask")[:, None, :].broadcast_to([128, 4, 128]),
                                    ALU.mult).then_inc(attm_ready, 1)
                    dve.wait_ge(upd_done, i + 1)
                    chain(V.tensor_tensor(updm[:, :, :], bank(5).rearrange("p (a b) -> p a b", a=2),
                                          K("bd256")[:, None, :].broadcast_to([128, 2, 256]), ALU.mult))
                    V.scalar_tensor_tensor(Sb[:, :], Sa[:, :], Ecum[:, 63:64], updm[:, 0, :], ALU.mult,
                                           ALU.add).then_inc(sb_ready, 1)
                    dve.wait_ge(sb_ready, i + 1)
                    dve.wait_ge(oc_done, m + 1)
                    V.scalar_tensor_tensor(Sa[:, :], Sb[:, :], Ecum[:, 127:128], updm[:, 1, :], ALU.mult,
                                           ALU.add).then_inc(sa_ready, 1)
                else:
                    dve.wait_ge(slots_ready, 1)
                    dve.wait_ge(seT_ready, 1)
                    V.tensor_tensor(qTm[:, :, :], gqT[:, None, 0:8].broadcast_to([128, 8, 8]),
                                    K("eye88").rearrange("p (a b) -> p a b", a=8), ALU.mult)
                    V.tensor_tensor(km8[:, :, :], P[0:8, None, GK:GK + 128].broadcast_to([8, 8, 128]),
                                    oh8, ALU.mult).then_inc(gl_ready, 1)
                    for b in range(NB):
                        dve.wait_ge(supd_done, b + 1)
                        chain(V.tensor_tensor(updm[:, 0, :], bank(5)[:, 0:256], K("bd256"), ALU.mult))
                        chain(V.tensor_reduce(updm[:, 1, 0:64], updm[:, 0, :].rearrange("p (h v) -> p v h", h=4),
                                              AX.X, ALU.add))
                        V.scalar_tensor_tensor(S1s[:, b, :], S0s[:, b, :], Ecum[:, b:b + 1], updm[:, 1, 0:64],
                                               ALU.mult, ALU.add).then_inc(supd_used, 1)
                        dve.wait_ge(supd_used, b + 1)
                        if b:
                            dve.wait_ge(seT_done, b + 1)
                        V.tensor_tensor(Sb[:, :].rearrange("p (h v) -> p h v", h=4),
                                        S1s[:, b:b + 1, :].broadcast_to([128, 4, 64]),
                                        K("bd256").rearrange("p (h v) -> p h v", h=4), ALU.mult).then_inc(sbd_ready, 1)
                    dve.wait_ge(oc_done, 1)
                    V.memset(updm[:, 0, 0:1], 0.0).then_inc(sa_ready, 1)
                dve.wait_ge(sq2_ready, m + 1)
                V.tensor_reduce(s4[0:R, :], sq2[0:R, :].rearrange("p (a b) -> p a b", b=64), AX.X,
                                ALU.add).then_inc(s4_ready, 1)
                dve.wait_ge(r4_ready, m + 1)
                chain(V.tensor_tensor(oCM[0:R, 0:256].rearrange("p (a b) -> p a b", b=64),
                                      bank(6)[0:R, 0:256].rearrange("p (a b) -> p a b", b=64),
                                      r4[0:R, :, None].broadcast_to([R, 4, 64]), ALU.mult))
                V.tensor_tensor(oCM[0:R, 0:256], oCM[0:R, 0:256], sil[0:R, :], ALU.mult).then_inc(oc_ready, 1)
                if i is not None:
                    dve.wait_ge(msc_done, i + 1)
                    V.tensor_reduce(nmx[:, :], bank(5, 2).rearrange("p (a b) -> p a b", a=4), AX.X, ALU.max,
                                    negate=True).then_inc(nmx_ready, 1)
                    dve.wait_ge(mp_ready, i + 1)
                    chain(V.reciprocal(rlm[:, :], lm[:, :]))
                    dve.wait_ge(mo_done, i + 1)
                    V.tensor_tensor(oCM[:, 256:512].rearrange("p (a b) -> p a b", b=64),
                                    bank(7)[:, 0:256].rearrange("p (a b) -> p a b", b=64),
                                    rlm[:, :, None].broadcast_to([128, 4, 64]), ALU.mult).then_inc(om_ready, 1)

            tile(None, NB)
            with dve.Fori(0, NT) as i:
                chain.enter(i, CHAIN_V1)
                tile(i, 128)
            chain.leave(NT)

        @block.tensor
        def _(pe):
            MM, TR = nc.tensor.matmul, nc.tensor.transpose
            ident = K("ident")

            def transposes(k, R):
                pe.wait_ge(xn_ready, k + 1)
                for j in range(KD):
                    last = TR(bank(0, 2)[:, j * 128:j * 128 + R], xn[0:R, j:D:KD], ident[0:R, 0:R])
                last.then_inc(xn_tp, 1)
                pe.wait_ge(hts_ready, k + 1)

            pe.wait_ge(const_ready, 1)
            for u in range(2):
                transposes(u, 128)
                for j in range(KD):
                    last = MM(bank(2), hTs[:, j, :], wmem[:, j, :], start=(j == 0), stop=(j == KD - 1))
                last.then_inc(kv_done, 1)
                pe.wait_ge(mk_ready, u + 1)
                for a in range(2):
                    last = TR(bank(7)[:, a * 128:(a + 1) * 128], QN[:, a * 128:(a + 1) * 128], ident)
                last.then_inc(kv_tp, 1)
                pe.wait_ge(kv_p, u + 1)
            pe.wait_ge(w_in_s, 16)

            def tile(i, R):
                k, m = (2, 0) if i is None else (i + 3, i + 1)
                transposes(k, R)
                for c in range(NCH):
                    if c in (2, 3):
                        pe.wait_ge(p_ready, m * NCH + (c - 1))
                    for j in range(KD):
                        last = MM(bank((2, 3, 2, 3, 4)[c])[0:R, 0:CH], hTs[:, j, 0:R], W1[:, j, c * CH:(c + 1) * CH],
                                  start=(j == 0), stop=(j == KD - 1))
                    last.then_inc(proj_done, 1)
                pe.wait_ge(p_ready, m * NCH + NCH)
                TR(bank(6)[0:16, 0:R], P[0:R, GA:GA + 16], ident[0:R, 0:R]).then_inc(aT_tp, 1)
                if i is not None:
                    for n, c in enumerate((KC, VC)):
                        last = MM(bank(4)[0:64, 2 * n:2 * n + 2], P[:, c:c + 64], K("ind2"), start=True, stop=True)
                    last.then_inc(km_done, 1)
                pe.wait_ge(aT_ready, m + 1)
                MM(bank(6)[0:R, 128:256], aT[:, 0:R], gate_up[:, :], start=True, stop=False)
                MM(bank(6)[0:R, 128:256], K("ones", 1)[:, 0:R], gate_b[:, :], start=False, stop=True).then_inc(pre_done, 1)
                pe.wait_ge(qn_ready, m + 1)
                if i is not None:
                    for a, (src, c) in enumerate(((P, SBQ), (P, SBQ + 128), (P, SBK), (P, SBK + 128), (QN, 0),
                                                  (QN, 128), (QN, QNS), (QN, QNW))):
                        TR(bank(0, 2)[:, a * 128:(a + 1) * 128], src[:, c:c + 128], ident)
                    for a in range(2):
                        TR(bank(7)[:, a * 128:(a + 1) * 128], QN[:, QNM + a * 128:QNM + (a + 1) * 128], ident)
                TR(bank(7)[:, 256:256 + R], P[0:R, GQ:GQ + 128], ident[0:R, 0:R])
                TR(bank(7)[:, 384:384 + R], P[0:R, GK:GK + 128], ident[0:R, 0:R]).then_inc(qn_tp, 1)
                pe.wait_ge(sp_ready, m + 1)
                pe.wait_ge(slots_ready, m + 1)
                if i is not None:
                    MM(bank(7)[:, 0:128], sp[:, :], K("gm_mid"), start=True, stop=True)
                    MM(bank(7)[:, 128:256], sp[:, :], K("gm_cum"), start=True, stop=True)
                    MM(bank(7)[:, 256:384], K("gm_suf"), sp[:, :], start=True, stop=True).then_inc(cum_done, 1)
                    pe.wait_ge(gl_ready, m + 1)
                    MM(bank(5), k1T[:, :], q1bd[:, :, :].rearrange("p a b -> p (a b)"), start=True,
                       stop=True).then_inc(att_done, 1)
                    pe.wait_ge(attm_ready, i + 1)
                    for c in range(2):
                        last = MM(bank(5)[:, c * 256:(c + 1) * 256], k4[:, c, :], P[:, GV:GV + 256], start=True, stop=True)
                    last.then_inc(upd_done, 1)
                    oc = bank(6)[:, 0:256]
                    pe.wait_ge(sa_ready, m)
                    MM(oc, q3[:, 0, :], Sa[:, :], start=True, stop=False, skip_group_check=True)
                    for h in range(4):
                        MM(oc[:, h * 64:(h + 1) * 64], attm[:, h, :], P[:, GV + h * 64:GV + (h + 1) * 64],
                           start=False, stop=False, skip_group_check=True)
                    pe.wait_ge(sb_ready, i + 1)
                    MM(oc, q3[:, 1, :], Sb[:, :], start=False, stop=True, skip_group_check=True).then_inc(oc_done, 1)
                    pe.wait_ge(oc_ready, m + 1)
                    for h in range(4):
                        last = MM(bank(5, 2)[:, h * 256:(h + 1) * 256], mq[:, h // 2, h % 2, :], mkT[:, h // 2, :],
                                  start=True, stop=True)
                    last.then_inc(msc_done, 1)
                    pe.wait_ge(mp_ready, i + 1)
                    for a in range(8):
                        last = TR(bank(0, 2)[:, a * 128:(a + 1) * 128], mp[:, a // 2, (a % 2) * 128:(a % 2 + 1) * 128], ident)
                    last.then_inc(mpt_tp, 1)
                    pe.wait_ge(mpt_evac, i + 1)
                    for h in range(4):
                        for u in range(2):
                            last = MM(bank(7)[:, h * 64:(h + 1) * 64], mpT[:, 2 * h + u, :],
                                      mv[:, u, h * 64:(h + 1) * 64], start=(u == 0), stop=(u == 1))
                    last.then_inc(mo_done, 1)
                    pe.wait_ge(om_ready, i + 1)
                    for a in range(4):
                        last = TR(bank(7)[:, a * 128:(a + 1) * 128], oCM[:, a * 128:(a + 1) * 128], ident)
                    last.then_inc(ot_tp, 1)
                else:
                    TR(bank(7)[:, 0:R], sp[0:R, :], ident[0:R, 0:R]).then_inc(seT_done, 1)
                    pe.wait_ge(gl_ready, 1)
                    for b in range(NB):
                        if b:
                            pe.wait_ge(supd_used, b)
                        MM(bank(5)[:, 0:256], km8[:, b, :], P[0:8, GV:GV + 256], start=True, stop=True).then_inc(supd_done, 1)
                        pe.wait_ge(sbd_ready, b + 1)
                        last = MM(bank(6)[0:8, 0:256], qTm[:, b, :], Sb[:, :], start=(b == 0), stop=(b == NB - 1))
                        if b < NB - 1:
                            last.then_inc(seT_done, 1)
                    last.then_inc(oc_done, 1)
                    pe.wait_ge(oc_ready, 1)
                    for a in range(2):
                        last = TR(bank(7)[:, a * 128:a * 128 + R], oCM[0:R, a * 128:(a + 1) * 128], ident[0:R, 0:R])
                    last.then_inc(ot_tp, 1)
                pe.wait_ge(ot_evac, m + 1)

            tile(None, NB)
            with pe.Fori(0, NT) as i:
                tile(i, 128)

        stage1.close()
        stage_over()

        acur = [late_w]

        def big(*dims, r=128):
            n = int(np.prod(dims))
            v = arena[0:r, acur[0]:acur[0] + n]
            acur[0] += n
            assert acur[0] <= KD * NP1, acur[0]
            if len(dims) == 2:
                return v.rearrange("p (a b) -> p a b", a=dims[0])
            if len(dims) == 3:
                return v.rearrange("p (a b c) -> p a b c", a=dims[0], b=dims[1])
            return v

        bsel = big(NSEL, 4)
        bwin = big(NWIN, 4)
        bcmp = big(64)
        keep = acur[0]
        BS = big(4, SEQ)
        WB = big(4, 640)
        bc = big(30, 4)
        vc01 = big(30, 4)
        kcT = big(16)
        kcr = big(128, r=16)
        kcs = big(64, r=16)
        vcbd = big(256, r=64)
        kn1, kn2 = big(1, r=16), big(1, r=16)
        kn2j = big(64, r=16)
        ind_col = K("ind2", 64)[:, 0:1]
        after_bias = acur[0]
        OH = big(OHC + 128 * (NSEL + NWIN) + 64 + NEAR, r=33)
        near = big(4, NEAR)
        acur[0] = after_bias
        QAbd = [big(2, 2, 128) for _ in range(2)]
        QBbd = [big(2, 2, 128) for _ in range(2)]
        zab = [big(512) for _ in range(2)]
        spu = [big(512) for _ in range(2)]
        Rsum = [big(512) for _ in range(3)]
        au = [big(512) for _ in range(2)]
        oAs = big(256)
        cursor[0] = 0
        sB = [tmp(1024) for _ in range(2)]
        pB = [tmp(1024) for _ in range(2)]
        pTB = [tmp(1024) for _ in range(2)]
        nmB = [tmp(1) for _ in range(2)]
        lB = tmp(2, 12)
        cB = tmp(2, 12)
        lcm, pcm, pcT = tmp(4, 16), tmp(4, 16), tmp(128, r=64)
        nmc = tmp(4)
        gB = tmp(NT, 12)
        oBs, oB2 = tmp(256), tmp(256)

        names = ("c2_in", "oh_in", "near_ps", "near_ready", "skew_out", "skew_in", "bias_ps", "bias_used", "bias_ready", "pm_done", "pm_ready", "km2_ready", "kc_done",
                 "kc_sq", "kc_r", "kc_n", "kc_tp", "kc_ready", "bd_zero", "bdA", "bdB", "z_done", "l_ready", "spA_ready",
                 "tri_done", "a_ready", "R_ready", "av_done", "oAs_ready", "oA_tp", "oA_evac", "sc_done",
                 "s_ready", "p_ready2", "pt_tp", "pt_evac", "o_done", "gB_e", "gB_ready", "lc_done", "lc_ready",
                 "pc_exp", "pc_ready", "pc_tp", "pc_evac", "oc2_done", "oB_ready", "oB_tp", "oB_evac", "ch2A", "ch2V",
                 "ch2P")
        S2 = {n: sem(n) for n in names}
        units = [(t, kb) for t in range(NT) for kb in range(t, -1, -1)]
        jobs = [(t, h, kind) for t in range(NT) for kind in (0, 1) for h in range(4)]

        def span(t, kind):
            n = t + 1 if kind == 0 else min(t + 1, 5)
            return t + 1 - n, n

        stage2 = ExitStack()
        block = stage2.enter_context(nc.Block())

        @block.sync
        def _(sy):
            sy.dma_start(late, C_d[:, c_early:c_late]).then_inc(S2["c2_in"], 16)
            sy.dma_start(OH[:, :], OH_d).then_inc(S2["oh_in"], 16)
            sy.wait_ge(S2["near_ready"], 1)
            sy.dma_start(skew_d.ap(), near).then_inc(S2["skew_out"], 16)
            sy.wait_ge(S2["skew_out"], 16)
            sy.dma_start(BS[:, :, 768:1024], bass.AP(skew_d, 127, [[4 * NEAR - 1, 128], [NEAR, 4], [1, 256]]))\
              .then_inc(S2["skew_in"], 16)

        @block.gpsimd
        def _(pool):
            G = nc.gpsimd
            pool.wait_ge(S2["bias_ready"], 1)
            for b in QAbd + QBbd:
                last = G.memset(b[:, :, :, :], 0.0)
            last.then_inc(S2["bd_zero"], 1)
            pool.wait_ge(S2["bd_zero"], 1)
            for t in range(NT):
                cols = slice(t * 128, t * 128 + 128)
                if t >= 2:
                    pool.wait_ge(S2["z_done"], sum(1 for u in units if u[0] <= t - 2))
                for a in range(2):
                    for hh in range(2):
                        r = slice(64 * hh, 64 * hh + 64)
                        last = G.tensor_scalar(QAbd[t % 2][r, a, hh, :], TT[r, a, cols], 0.125, None, ALU.mult)
                last.then_inc(S2["bdA"], 1)
            for t in range(NT):
                cols = slice(t * 128, t * 128 + 128)
                if t >= 2:
                    pool.wait_ge(S2["sc_done"], 8 * (t - 1))
                    pool.wait_ge(S2["lc_done"], t - 1)
                for a in range(2):
                    for hh in range(2):
                        r = slice(64 * hh, 64 * hh + 64)
                        last = G.tensor_copy(QBbd[t % 2][r, a, hh, :], TT[r, 4 + a, cols])
                last.then_inc(S2["bdB"], 1)

        @block.tensor
        def _(pe):
            MM, TR = nc.tensor.matmul, nc.tensor.transpose
            ident = K("ident")
            pe.wait_ge(S2["oh_in"], 16)
            o = OHC + 128 * (NSEL + NWIN) + 64
            for h in range(4):
                last = MM(bank(h)[:, 0:NEAR], tab[:, h:h + 1].broadcast_to([33, 128]), OH[:, o:o + NEAR], start=True, stop=True)
            last.then_inc(S2["near_ps"], 1)
            for j in range(30):
                MM(bank(4)[:, 4 * j:4 * j + 4], OH[:, 1856 - 64 * j:1984 - 64 * j], tab[:, :], start=True, stop=True)
            for r in range(NSEL + NWIN):
                o = OHC + 128 * r
                MM(bank(4)[:, 120 + 4 * r:124 + 4 * r], OH[:, o:o + 128], tab[:, :], start=True, stop=True)
            o = OHC + 128 * (NSEL + NWIN)
            MM(bank(5)[0:4, 64:128], tab[:, :], OH[:, o:o + 64], start=True, stop=True)
            for n in range(2):
                last = MM(bank(5)[0:64, n:n + 1], pe_kv[:, n, :], ind_col, start=True, stop=True)
            last.then_inc(S2["bias_ps"], 1)
            pe.wait_ge(S2["km2_ready"], 1)
            for n in range(2):
                last = MM(bank(6)[0:16, 64 * n:64 * n + 64], kmT[:, n, :], phi_kv[:, n, :], start=True, stop=True)
            last.then_inc(S2["kc_done"], 1)
            pe.wait_ge(S2["kc_n"], 1)
            TR(bank(7)[:, 0:16], kcr[:, :], ident[0:16, 0:16])
            MM(bank(7)[0:64, 64:128], K("rep16", 16), kcs[:, :], start=True, stop=True).then_inc(S2["kc_tp"], 1)
            pe.wait_ge(S2["kc_ready"], 1)

            for u in range(len(units) + 2):
                if u < len(units):
                    t, kb = units[u]
                    z = bank(u % 2)
                    pe.wait_ge(S2["bdA"], t + 1)
                    if u >= 2:
                        pe.wait_ge(S2["a_ready"], u - 1)
                    for a in range(2):
                        last = MM(z[:, a * 256:a * 256 + 256], TT[:, 2 + a, kb * 128:kb * 128 + 128],
                                  QAbd[t % 2][:, a, :, :].rearrange("p a b -> p (a b)"), start=(a == 0), stop=False,
                                  skip_group_check=True)
                    if kb == t:
                        last = MM(z.rearrange("p (a b) -> p a b", a=4), ident, K("causalneg")[:, None, :].broadcast_to([128, 4, 128]),
                                  start=False, stop=False, skip_group_check=True)
                    last.then_inc(S2["z_done"], 1)
                v = u - 1
                if 0 <= v < len(units):
                    t, kb = units[v]
                    pe.wait_ge(S2["spA_ready"], v + 1)
                    last = MM(bank(v % 2), K("negtri"), spu[v % 2], start=False, stop=True, skip_group_check=True)
                    if kb < t:
                        pe.wait_ge(S2["R_ready"], v)
                        last = MM(bank(v % 2), K("negones"), Rsum[(v - 1) % 3], start=False, stop=True,
                                  skip_group_check=True)
                    last.then_inc(S2["tri_done"], 1)
                w = u - 2
                if 0 <= w:
                    t, kb = units[w]
                    pe.wait_ge(S2["a_ready"], w + 1)
                    if kb == t and t >= 2:
                        pe.wait_ge(S2["oAs_ready"], t - 1)
                    for h in range(4):
                        last = MM(bank(2 + t % 2)[:, h * 64:h * 64 + 64], au[w % 2][:, h * 128:h * 128 + 128],
                                  VA[:, kb, h * 64:h * 64 + 64], start=(kb == t and h == 0), stop=(kb == 0),
                                  skip_group_check=True)
                    last.then_inc(S2["av_done"], 1)
                    if kb == 0:
                        pe.wait_ge(S2["oAs_ready"], t + 1)
                        if t:
                            pe.wait_ge(S2["oA_evac"], t)
                        for a in range(2):
                            last = TR(bank(4)[:, a * 128:a * 128 + 128], oAs[:, a * 128:a * 128 + 128], ident)
                        last.then_inc(S2["oA_tp"], 1)

            pe.wait_ge(S2["oA_evac"], NT)
            for j in range(len(jobs) + 3):
                if j < len(jobs):
                    t, h, kind = jobs[j]
                    k0, n = span(t, kind)
                    pe.wait_ge(S2["bdB"], t + 1)
                    if j >= 2:
                        pe.wait_ge(S2["s_ready"], j - 1)
                    for c in range(0, n * 128, 512):
                        w = min(512, n * 128 - c)
                        last = MM(bank(2 * (j % 2), 2)[:, c:c + w], QBbd[t % 2][:, h // 2, h % 2, :],
                                  TT[:, 6 + kind, k0 * 128 + c:k0 * 128 + c + w], start=True, stop=True)
                    last.then_inc(S2["sc_done"], 1)
                v = j - 1
                if 0 <= v < len(jobs):
                    t, h, kind = jobs[v]
                    k0, n = span(t, kind)
                    pe.wait_ge(S2["p_ready2"], v + 1)
                    if v:
                        pe.wait_ge(S2["pt_evac"], v)
                    for b in range(n):
                        last = TR(bank(4, 2)[:, b * 128:b * 128 + 128], pB[v % 2][:, b * 128:b * 128 + 128], ident)
                    last.then_inc(S2["pt_tp"], 1)
                w = j - 2
                if 0 <= w < len(jobs):
                    t, h, kind = jobs[w]
                    k0, n = span(t, kind)
                    pe.wait_ge(S2["pt_evac"], w + 1)
                    if w % 8 == 0 and t:
                        pe.wait_ge(S2["oB_ready"], t)
                    vals = VSt if kind == 0 else VWt
                    o = bank(6)[:, (kind * 4 + h) * 64:(kind * 4 + h) * 64 + 64]
                    for b in range(n):
                        last = MM(o, pTB[w % 2][:, b * 128:b * 128 + 128], vals[:, k0 + b, :], start=(b == 0),
                                  stop=(b == n - 1))
                    last.then_inc(S2["o_done"], 1)
                t, step = j // 8, j % 8
                if step == 1 and t >= 1:
                    pe.wait_ge(S2["oB_ready"], t)
                    for a in range(2):
                        last = TR(bank(7)[:, a * 128:a * 128 + 128], oBs[:, a * 128:a * 128 + 128], ident)
                    last.then_inc(S2["oB_tp"], 1)
                if t < NT and step == 2:
                    if t:
                        pe.wait_ge(S2["oB_evac"], t)
                    for h in range(4):
                        last = MM(bank(7)[:, h * 16:h * 16 + 16], QBbd[t % 2][:, h // 2, h % 2, :], kcT, start=True, stop=True)
                    last.then_inc(S2["lc_done"], 1)
                if t < NT and step == 4:
                    pe.wait_ge(S2["pc_ready"], t + 1)
                    TR(bank(7)[0:64, 64:192], pcm.rearrange("p a b -> p (a b)"), ident).then_inc(S2["pc_tp"], 1)
                if t < NT and step == 6:
                    pe.wait_ge(S2["pc_evac"], t + 1)
                    MM(bank(7)[:, 192:448], pcT, vcbd, start=True, stop=True).then_inc(S2["oc2_done"], 1)

        @block.scalar
        def _(act):
            A = nc.scalar.activation
            chain = Chain(act, S2["ch2A"])
            nc.scalar.preload_act_table_set("natural_log_exp_and_others")
            act.wait_ge(S2["kc_done"], 1)
            chain(A(kn2j, bank(6)[0:16, 0:64], ACT.Square, accum_out=kn1[:, :]))
            chain(A(kn2[:, :], kn1[:, :], ACT.Ln, bias=eps[0:16, :], scale=1.0 / 64))
            A(kn2[:, :], kn2[:, :], ACT.Exp, scale=-0.5).then_inc(S2["kc_r"], 1)
            A(gB[:, :, :], NGt[:, :, :], ACT.Exp, scale=-1.0).then_inc(S2["gB_e"], 1)
            act.wait_ge(S2["bias_ready"], 1)
            for u in range(len(units) + 2):
                if u < len(units):
                    z, buf = bank(u % 2), zab[u % 2]
                    act.wait_ge(S2["z_done"], u + 1)
                    if u >= 2:
                        act.wait_ge(S2["spA_ready"], u - 1)
                    chain(A(buf, z, ACT.Abs))
                    chain(A(buf, buf, ACT.Exp, scale=-1.0))
                    A(buf, buf, ACT.Ln, bias=one[:, :]).then_inc(S2["l_ready"], 1)
                v = u - 1
                if 0 <= v < len(units):
                    act.wait_ge(S2["tri_done"], v + 1)
                    if v >= 2:
                        act.wait_ge(S2["av_done"], v - 1)
                    A(au[v % 2], bank(v % 2), ACT.Exp).then_inc(S2["a_ready"], 1)
                w = u - 2
                if 0 <= w and units[w][1] == 0:
                    t = units[w][0]
                    act.wait_ge(S2["oA_tp"], t + 1)
                    A(OT[:, 0:2, t * 128:t * 128 + 128], bank(4)[:, 0:256].rearrange("p (a b) -> p a b", a=2),
                      ACT.Copy).then_inc(S2["oA_evac"], 1)
            for j in range(len(jobs) + 3):
                if j < len(jobs):
                    t, h, kind = jobs[j]
                    k0, n = span(t, kind)
                    act.wait_ge(S2["s_ready"], j + 1)
                    if j >= 2:
                        act.wait_ge(S2["pt_tp"], j - 1)
                    if j % 8 == 0 and t >= 2:
                        act.wait_ge(S2["oB_ready"], t - 1)
                    A(pB[j % 2][:, 0:n * 128], sB[j % 2][:, 0:n * 128], ACT.Exp, bias=nmB[j % 2],
                      accum_out=lB[:, t % 2, 4 + kind * 4 + h:5 + kind * 4 + h]).then_inc(S2["p_ready2"], 1)
                v = j - 1
                if 0 <= v < len(jobs):
                    t, h, kind = jobs[v]
                    n = span(t, kind)[1]
                    act.wait_ge(S2["pt_tp"], v + 1)
                    if v >= 2:
                        act.wait_ge(S2["o_done"], v - 1)
                    A(pTB[v % 2][:, 0:n * 128], bank(4, 2)[:, 0:n * 128], ACT.Copy).then_inc(S2["pt_evac"], 1)
                t, step = j // 8, j % 8
                if step == 1 and t >= 1:
                    act.wait_ge(S2["oB_tp"], t)
                    A(OT[:, 2:4, (t - 1) * 128:t * 128], bank(7)[:, 0:256].rearrange("p (a b) -> p a b", a=2),
                      ACT.Copy).then_inc(S2["oB_evac"], 1)
                if t < NT and step == 2:
                    act.wait_ge(S2["lc_ready"], t + 1)
                    A(pcm, lcm, ACT.Exp).then_inc(S2["pc_exp"], 1)
                if t < NT and step == 4:
                    act.wait_ge(S2["pc_tp"], t + 1)
                    A(pcT, bank(7)[0:64, 64:192], ACT.Copy).then_inc(S2["pc_evac"], 1)

        @block.vector
        def _(dve):
            V = nc.vector
            chain = Chain(dve, S2["ch2V"])
            dve.wait_ge(S2["near_ps"], 1)
            V.tensor_copy(near, PS[:, 0:2048].rearrange("p (h x) -> p h x", h=4)[:, :, 0:NEAR]).then_inc(S2["near_ready"], 1)
            dve.wait_ge(S2["bias_ps"], 1)
            dve.wait_ge(S2["c2_in"], 16)
            chain(V.tensor_copy(pe_mean[:, :], bank(5)[0:64, 0:2]))
            for n in range(2):
                last = V.tensor_scalar(kmT[:, n, :], kmT[:, n, :], pe_mean[:, n:n + 1], None, ALU.add)
            last.then_inc(S2["km2_ready"], 1)
            dve.wait_ge(S2["skew_in"], 16)
            chain(V.tensor_copy(BS[:, :, 0:768], BS[:, :, 768:769].broadcast_to([128, 4, 768])))
            chain(V.tensor_copy(WB[:, :, :], BS[:, :, 384:1024]))
            V.tensor_tensor(WB[:, :, 0:128], WB[:, :, 0:128], K("winneg")[:, None, :].broadcast_to([128, 4, 128]), ALU.add)
            chain(V.tensor_copy(bc[:, :, :], bank(4)[:, 0:120].rearrange("p (a b) -> p a b", b=4)))
            V.tensor_scalar(vc01[:, :, :], bc[:, :, :], -1e29, None, ALU.is_gt)
            V.tensor_copy(bsel[:, :, :], bank(4)[:, 120:120 + 4 * NSEL].rearrange("p (a b) -> p a b", b=4))
            V.tensor_copy(bwin[:, :, :], bank(4)[:, 120 + 4 * NSEL:120 + 4 * (NSEL + NWIN)].rearrange("p (a b) -> p a b", b=4))
            V.tensor_copy(bcmp[0:4, :], bank(5)[0:4, 64:128]).then_inc(S2["bias_ready"], 1)
            dve.wait_ge(S2["kc_r"], 1)
            V.tensor_copy(kcs[:, :], bank(6)[0:16, 64:128])
            chain(V.scalar_tensor_tensor(kcr[:, 0:64], bank(6)[0:16, 0:64], kn2[:, :], kn_cmp[0:16, :], ALU.mult, ALU.mult))
            V.tensor_copy(kcr[:, 64:128], kcr[:, 0:64]).then_inc(S2["kc_n"], 1)
            dve.wait_ge(S2["gB_e"], 1)
            chain(V.tensor_scalar(gB[:, :, :], gB[:, :, :], 1.0, None, ALU.add))
            chain(V.reciprocal(gB[:, :, :], gB[:, :, :]))
            dve.wait_ge(S2["kc_tp"], 1)
            V.tensor_copy(kcT[:, :], bank(7)[:, 0:16])
            V.tensor_tensor(vcbd.rearrange("p (a b) -> p a b", a=4), bank(7)[0:64, None, 64:128].broadcast_to([64, 4, 64]),
                            K("cbd", 64).rearrange("p (a b) -> p a b", a=4), ALU.mult).then_inc(S2["kc_ready"], 1)
            for u in range(len(units) + 2):
                if u < len(units):
                    t, kb = units[u]
                    dve.wait_ge(S2["l_ready"], u + 1)
                    if u >= 2:
                        dve.wait_ge(S2["tri_done"], u - 1)
                    V.scalar_tensor_tensor(spu[u % 2], bank(u % 2), 0.0, zab[u % 2], ALU.max, ALU.add)\
                        .then_inc(S2["spA_ready"], 1)
                    dve.wait_ge(S2["spA_ready"], u + 1)
                    if kb == t:
                        V.tensor_copy(Rsum[u % 3], spu[u % 2]).then_inc(S2["R_ready"], 1)
                    else:
                        dve.wait_ge(S2["R_ready"], u)
                        V.tensor_tensor(Rsum[u % 3], Rsum[(u - 1) % 3], spu[u % 2], ALU.add).then_inc(S2["R_ready"], 1)
                w = u - 2
                if 0 <= w and units[w][1] == 0:
                    t = units[w][0]
                    dve.wait_ge(S2["av_done"], w + 1)
                    if t:
                        dve.wait_ge(S2["oA_tp"], t)
                    V.tensor_copy(oAs, bank(2 + t % 2)[:, 0:256]).then_inc(S2["oAs_ready"], 1)

            def heads(ap):
                return ap.rearrange("p (a b) -> p a b", b=64)

            for j in range(len(jobs) + 3):
                if j < len(jobs):
                    t, h, kind = jobs[j]
                    k0, n = span(t, kind)
                    dve.wait_ge(S2["sc_done"], j + 1)
                    if j >= 2:
                        dve.wait_ge(S2["p_ready2"], j - 1)
                    strip = BS[:, h, 1024 - n * 128:1024] if kind == 0 or t < 4 else WB[:, h, :]
                    chain(V.tensor_tensor(sB[j % 2][:, 0:n * 128], bank(2 * (j % 2), 2)[:, 0:n * 128], strip, ALU.add))
                    V.tensor_reduce(nmB[j % 2], sB[j % 2][:, 0:n * 128], AX.X, ALU.max, negate=True).then_inc(S2["s_ready"], 1)
                t, step = j // 8, j % 8
                if step == 1 and t >= 1:
                    T = t - 1
                    dve.wait_ge(S2["o_done"], 8 * t)
                    dve.wait_ge(S2["p_ready2"], 8 * t)
                    dve.wait_ge(S2["oc2_done"], t)
                    if T:
                        dve.wait_ge(S2["oB_tp"], T)
                    chain(V.tensor_scalar(cB[:, T % 2, :], lB[:, T % 2, :], 1e-30, None, ALU.max))
                    chain(V.reciprocal(cB[:, T % 2, :], cB[:, T % 2, :]))
                    chain(V.tensor_tensor(cB[:, T % 2, :].rearrange("p (b h) -> p b h", b=3),
                                          cB[:, T % 2, :].rearrange("p (b h) -> p b h", b=3),
                                          gB[:, T, :].rearrange("p (h b) -> p b h", b=3), ALU.mult))
                    src = (bank(7)[:, 192:448], bank(6)[:, 0:256], bank(6)[:, 256:512])
                    for b in range(3):
                        dst = oBs if b == 0 else oB2
                        chain(V.tensor_tensor(heads(dst), heads(src[b]),
                                              cB[:, T % 2, 4 * b:4 * b + 4][:, :, None].broadcast_to([128, 4, 64]), ALU.mult))
                        if b:
                            last = V.tensor_tensor(oBs, oBs, oB2, ALU.add)
                            if b == 1:
                                chain(last)
                    last.then_inc(S2["oB_ready"], 1)
                if t < NT and step == 2:
                    dve.wait_ge(S2["lc_done"], t + 1)
                    if t:
                        dve.wait_ge(S2["pc_tp"], t)
                    j0 = 14 - 2 * t
                    chain(V.tensor_tensor(lcm, bank(7)[:, 0:64].rearrange("p (a b) -> p a b", a=4),
                                          bc[:, j0:j0 + 16, :].rearrange("p j h -> p h j"), ALU.add))
                    chain(V.tensor_reduce(nmc, lcm, AX.X, ALU.max))
                    V.tensor_tensor(lcm, lcm, nmc[:, :, None].broadcast_to([128, 4, 16]), ALU.subtract)\
                        .then_inc(S2["lc_ready"], 1)
                if t < NT and step == 3:
                    dve.wait_ge(S2["pc_exp"], t + 1)
                    j0 = 14 - 2 * t
                    chain(V.tensor_tensor(pcm, pcm, vc01[:, j0:j0 + 16, :].rearrange("p j h -> p h j"), ALU.mult))
                    V.tensor_reduce(lB[:, t % 2, 0:4], pcm, AX.X, ALU.add).then_inc(S2["pc_ready"], 1)

        stage2.close()
        stage_over()

        acur[0] = keep
        NR = 32
        tpool = [TT[:, :, :].rearrange("p a b -> p (a b)"), 0]

        def tt(*dims, r=128):
            n = int(np.prod(dims))
            v = tpool[0][0:r, tpool[1]:tpool[1] + n]
            tpool[1] += n
            assert tpool[1] <= 8 * SEQ, tpool[1]
            return v if len(dims) == 1 else v.rearrange("p (a b) -> p a b", a=dims[0])

        kring = [tt(4, 256) for _ in range(4)]
        vring = [tt(4, 256) for _ in range(4)]
        Ks = [big(NSEL, 64) for _ in range(2)]
        Vs = [big(NSEL, 64) for _ in range(2)]
        CK = [big(NR, 64) for _ in range(2)]
        CV = [big(NR, 64) for _ in range(2)]
        cursor[0] = 0
        WK = [tmp(NWIN, 64) for _ in range(2)]
        WV = [tmp(NWIN, 64) for _ in range(2)]
        MK = [tmp(2, 256) for _ in range(2)]
        MV = [tmp(2, 256) for _ in range(2)]
        qrow = [tmp(3, 256) for _ in range(2)]
        qTs = [tmp(4, r=64) for _ in range(2)]
        gs = [tmp(3, r=4) for _ in range(2)]
        prod = [tmp(2112) for _ in range(1)] * 2
        gtj = tmp(64, r=64)
        zAs = [tmp(4, NR) for _ in range(2)]
        labs, spS, Csuf, wA, aA = (tmp(4, NR) for _ in range(5))
        SCs = [tmp(4, 40) for _ in range(2)]
        pSC = tmp(4, 40)
        ksums = [tmp(2, 64) for _ in range(2)]
        kmTs = tmp(2, 64, r=64)
        kcn, vcn, kcTs = (tmp(64, r=64) for _ in range(3))
        kq, kr = tmp(1, r=64), tmp(1, r=64)
        lcs, pcs = tmp(64, r=4), tmp(64, r=4)
        nml, lcl, rcl = tmp(1, r=4), tmp(1, r=4), tmp(1, r=4)
        srw, gtw = tmp(64, r=64), tmp(64, r=64)
        scol, rk1, rk2 = tmp(1, r=64), tmp(1, r=64), tmp(1, r=64)
        pcTs = tmp(4, r=64)
        mx12 = tmp(12)
        mcol = tmp(1, r=12)
        dg12 = tmp(12, r=12)
        lp12 = tmp(12)
        rl3, gg3 = tmp(3, r=4), tmp(3, r=4)
        om4 = tmp(256, r=4)
        orow = tmp(3, 64, r=4)
        samrows = big(1024, r=8)
        idxf = tmp(NB)
        idx_pt = small[:, cursor[0]:cursor[0] + NB].bitcast(I32)
        cursor[0] += NB
        idx_c = small[:, cursor[0]:cursor[0] + 9].bitcast(I32)
        cursor[0] += 9
        idx_all = small[:, cursor[0]:cursor[0] + 9 * NB].bitcast(I32)
        cursor[0] += 9 * NB
        slot_k, slot_v = ([small[:, cursor[0] + 9 * n:cursor[0] + 9 * n + 9].bitcast(I32) for n in m] for m in ((0, 1), (2, 3)))
        cursor[0] += 36
        assert cursor[0] <= SMALL

        names = ("pt_in", "idx_f", "idx_ready", "slot_ready", "zeroS", "kA_used", "vA_used", "z_all", "lS_ready",
                 "spS_ready", "suf_ready", "X_done", "w_ready", "aS_ready", "sum_ready", "km_doneS",
                 "km_readyS", "kcS_done", "kcS_sq", "kcS_ready", "kcT_done", "kcT_ready", "lcS_done", "lcS_ready", "pcS_exp",
                 "pcS_ready", "imp_done", "rank_ready", "exp_done", "mx_ready", "mxT_done", "mxc_ready", "mxb_done",
                 "scS_ready", "pS_ready", "lpS_ready", "lS_done", "AB_done", "gs_e", "orow_ready", "orow_out", "sel_scored",
                 "samT_in", "gather_go", "samT_done", "samT_ready", "pcT_ready", "chSA", "chSV")
        S3 = {n: sem(n) for n in names}
        ks_in = [sem(f"kring_in{n}") for n in range(4)]
        vs_in = [sem(f"vring_in{n}") for n in range(4)]
        sel_in = [sem(f"sel_in{n}") for n in range(2)]
        row_in = [sem(f"row_in{n}") for n in range(2)]
        NSMALL = 11

        sbk = I["cache_sb_k"][0].rearrange("n (s r) h d -> (n s) (r h d)", r=4)
        sbv = I["cache_sb_v"][0].rearrange("n (s r) h d -> (n s) (r h d)", r=4)
        small_caches = [I[n][0].rearrange("n (s r) d -> (n s) (r d)", r=NR)
                        for n in ("cache_nsa_sel_k", "cache_nsa_sel_v", "cache_nsa_cmp_k", "cache_nsa_cmp_v")]

        stageS = ExitStack()
        block = stageS.enter_context(nc.Block())

        @block.sync
        def _(sy):
            sy.dma_start(idx_c, RO_d).then_inc(S3["pt_in"], 16)
            for s in range(4):
                sy.dma_start(idx_pt[s:128:4, :], I["page_table"].rearrange("b j -> j b")).then_inc(S3["pt_in"], 16)

            def seq(b, par, i):
                def load(dst, src):
                    sy.dma_start(dst, src).then_inc(row_in[par], 16)
                one = bass.ds(b, 1)
                row = lambda c, w: srow_d[one, c:c + w]
                load(qrow[par].rearrange("p a b -> p (a b)"), row(RQA, 768).broadcast_to([128, 768]))
                load(Ks[par][0:1, NR, :], row(RKS, 64))
                load(Vs[par][0:1, NR, :], row(RVS, 64))
                load(WK[par][0:1, 4, :], row(RKW, 64))
                load(WV[par][0:1, 4, :], row(RVW, 64))
                load(WK[par][:, 0:4, :], I["cache_nsa_win_k"][0, one].rearrange("a (p r) d -> p (a r) d", r=4))
                load(WV[par][:, 0:4, :], I["cache_nsa_win_v"][0, one].rearrange("a (p r) d -> p (a r) d", r=4))
                load(MK[par][:, :, :], I["cache_mem_k"][0, one].rearrange("a (p r) h d -> p (a r) (h d)", r=2))
                load(MV[par][:, :, :], I["cache_mem_v"][0, one].rearrange("a (p r) h d -> p (a r) (h d)", r=2))
                load(qTs[par], srow_d[one, RQB:RQB + 256].rearrange("a (h d) -> d (a h)", d=64))
                load(gs[par], srow_d[one, RG:RG + 12].rearrange("a (h g) -> h (a g)", g=3))

            def store(b):
                sy.wait_ge(S3["orow_ready"], b + 1)
                for n, c in ((0, 0), (1, 256), (2, 768)):
                    sy.dma_start(osam_d[bass.ds(b, 1), c:c + 256].rearrange("a (h d) -> h (a d)", d=64),
                                 orow[:, n, :]).then_inc(S3["orow_out"], 16)

            sy.wait_ge(S3["zeroS"], 1)
            for par in range(2):
                seq(par, par, 0)
            with sy.Fori(0, NB // 2 - 1) as pair:
                i = pair * 2
                for par in range(2):
                    store(i + par)
                    seq(i + par + 2, par, i)
            for b in range(NB - 2, NB):
                store(b)
            sy.wait_ge(S3["orow_out"], 16 * 3 * NB)
            for c in (0, 256, 768):
                sy.dma_start(samrows[:, c:c + 256], osam_d[:, c:c + 256]).then_inc(S3["samT_in"], 16)

        @block.gpsimd
        def _(pool):
            G = nc.gpsimd
            for par in range(2):
                for x in (Ks, Vs):
                    G.memset(x[par][:, NR, :], 0.0)
                for x in (WK, WV):
                    last = G.memset(x[par][:, 4, :], 0.0)
            last.then_inc(S3["zeroS"], 1)
            pool.wait_ge(S3["idx_ready"], 1)

            def wait(s, v):
                pool.wait_ge(s, v)
                pool.sem_inc(S3["gather_go"], 1)

            def gather(dst, src, slot, c, s):
                G.indirect_dma_start(dst, None, src, bass.IndirectOffsetOnAxis(ap=slot.bitcast(U32)[:, c:c + 1], axis=0)).then_inc(s, 16)

            def rows(slot, b, used, n):
                if used is not None:
                    wait(*used)
                G.tensor_copy(slot, idx_all[:, bass.ds(b * 9, 9)]).then_inc(S3["slot_ready"], 1)
                wait(S3["slot_ready"], n)

            def keys(b, par, cs, first=False):
                for c in cs:
                    if not first:
                        wait(S3["kA_used"], 8 * b + (c - 3))
                    gather(kring[c % 4].rearrange("p a b -> p (a b)"), sbk, slot_k[par], c, ks_in[c % 4])

            def values(b, par, cs, first=False):
                for c in cs:
                    if not first:
                        wait(S3["vA_used"], 8 * b + (c - 3))
                    gather(vring[c % 4].rearrange("p a b -> p (a b)"), sbv, slot_v[par], c, vs_in[c % 4])

            def small_pages(b, par):
                for n, x in enumerate((Ks, Vs, CK, CV)):
                    gather(x[par][:, 0:NR, :].rearrange("p a b -> p (a b)"), small_caches[n], slot_k[par], 8, sel_in[par])

            def step(b, par, kind):
                if kind != 7:
                    rows(slot_k[1 - par], b + 1, None if kind == 0 else (S3["kA_used"], 8 * b), 2 * b + 2)
                    keys(b + 1, 1 - par, range(4))
                rows(slot_v[par], b, None if kind < 2 else (S3["vA_used"], 8 * b - 8), (2 * b + 3) if kind != 7 else 2 * NB)
                values(b, par, range(4), first=(kind == 0))
                if kind != 7:
                    if kind:
                        wait(S3["orow_ready"], b)
                    small_pages(b + 1, 1 - par)
                    keys(b + 1, 1 - par, range(4, 8))
                values(b, par, range(4, 8))

            rows(slot_k[0], 0, None, 1)
            keys(0, 0, range(4), first=True)
            small_pages(0, 0)
            keys(0, 0, range(4, 8))
            step(0, 0, 0)
            step(1, 1, 1)
            with pool.Fori(1, NB // 2 - 1) as pair:
                for par in range(2):
                    step(pair * 2 + par, par, 2)
            step(NB - 2, 0, 2)
            step(NB - 1, 1, 7)

        @block.vector
        def _(dve):
            V = nc.vector
            chain = Chain(dve, S3["chSV"])
            dve.wait_ge(S3["pt_in"], 80)
            chain(V.tensor_scalar(idxf, idx_pt, 32.0, None, ALU.mult))
            for b in range(NB):
                last = V.tensor_scalar(idx_all[:, 9 * b:9 * b + 8], idx_c[:, 0:8], idxf[:, b:b + 1], None, ALU.add)
            chain(last)
            chain(V.tensor_scalar(idxf, idx_pt, 4.0, None, ALU.mult))
            for b in range(NB):
                last = V.tensor_scalar(idx_all[:, 9 * b + 8:9 * b + 9], idx_c[:, 8:9], idxf[:, b:b + 1], None, ALU.add)
            last.then_inc(S3["idx_ready"], 1)

            def score(b, par, i, n):
                zA, SC, ksum = zAs[par], SCs[par], ksums[par]
                qA, qB, qM = (qrow[par][:, a, :] for a in range(3))
                if n == 0:
                    dve.wait_ge(row_in[par], i * (8 * NSMALL) + 16 * NSMALL)
                if n < 8:
                    c = n
                    pr = prod[0][:, (c % 2) * 1024:(c % 2) * 1024 + 1024]
                    if not (isinstance(b, int) and b == 0 and c < 2):
                        dve.wait_ge(S3["kA_used"], 8 * b + (c - 1))
                    dve.wait_ge(ks_in[c % 4], b * 32 + 16 * (c // 4 + 1))
                    chain(V.tensor_tensor(pr.rearrange("p (r x) -> p r x", r=4), kring[c % 4],
                                          qA[:, None, :].broadcast_to([128, 4, 256]), ALU.mult))
                    V.tensor_reduce(zA[:, :, 4 * c:4 * c + 4].rearrange("p h r -> p r h"),
                                    pr.rearrange("p (r h d) -> p r h d", r=4, h=4), AX.X, ALU.add).then_inc(S3["kA_used"], 1)
                elif n < 12:
                    h = n - 8
                    if h == 0:
                        dve.wait_ge(S3["kA_used"], 8 * b + 8)
                        V.tensor_scalar(zA, zA, 0.125, None, ALU.mult).then_inc(S3["z_all"], 1)
                        dve.wait_ge(sel_in[par], i * 32 + 64)
                    pr = prod[0][:, 0:NSEL * 64].rearrange("p (a b) -> p a b", b=64)
                    chain(V.tensor_tensor(pr, Ks[par], qB[:, None, h * 64:h * 64 + 64].broadcast_to([128, NSEL, 64]), ALU.mult))
                    chain(V.tensor_reduce(SC[:, h, 0:NSEL], pr, AX.X, ALU.add))
                elif n == 12:
                    pr = prod[0][:, 0:1280].rearrange("p (h r d) -> p h r d", h=4, r=NWIN)
                    for h in range(4):
                        last = V.tensor_tensor(pr[:, h], WK[par], qB[:, None, h * 64:h * 64 + 64].broadcast_to([128, NWIN, 64]), ALU.mult)
                    chain(last)
                    chain(V.tensor_reduce(SC[:, :, 33:38], pr, AX.X, ALU.add))
                elif n == 13:
                    pr = prod[0][:, 0:512]
                    chain(V.tensor_tensor(pr.rearrange("p (r x) -> p r x", r=2), MK[par], qM[:, None, :].broadcast_to([128, 2, 256]), ALU.mult))
                    chain(V.tensor_reduce(SC[:, :, 38:40].rearrange("p h r -> p r h"),
                                          pr.rearrange("p (r h d) -> p r h d", r=2, h=4), AX.X, ALU.add))
                elif n == 14:
                    chain(V.tensor_reduce(ksum[:, 0, :], CK[par].rearrange("p r d -> p d r"), AX.X, ALU.add))
                    V.tensor_tensor(SC[:, :, 0:33], SC[:, :, 0:33], bsel.rearrange("p r h -> p h r"), ALU.add)
                else:
                    chain(V.tensor_tensor(SC[:, :, 33:38], SC[:, :, 33:38], bwin.rearrange("p r h -> p h r"), ALU.add))
                    V.tensor_reduce(ksum[:, 1, :], CV[par].rearrange("p r d -> p d r"), AX.X, ALU.add).then_inc(S3["sum_ready"], 1)

            def seq(b, par, i, following=True):
                zA, SC = zAs[par], SCs[par]

                def nxt(n):
                    if following:
                        score(b + 1, 1 - par, i + 2 * par, n)

                nxt(0)
                dve.wait_ge(S3["lS_ready"], b + 1)
                chain(V.scalar_tensor_tensor(spS, zA, 0.0, labs, ALU.max, ALU.add))
                chain(V.tensor_tensor_scan(Csuf.rearrange("p a b -> p (a b)")[:, ::-1], K("restart")[:, ::-1],
                                           spS.rearrange("p a b -> p (a b)")[:, ::-1], 0.0, ALU.mult, ALU.add))
                V.tensor_tensor(wA, zA, Csuf, ALU.subtract).then_inc(S3["suf_ready"], 1)
                dve.wait_ge(S3["suf_ready"], b + 1)
                nxt(1)
                dve.wait_ge(S3["X_done"], b + 1)
                V.tensor_tensor(wA, wA, bank(2)[:, 260:264][:, :, None].broadcast_to([128, 4, NR]), ALU.subtract)\
                    .then_inc(S3["w_ready"], 1)
                dve.wait_ge(S3["km_doneS"], b + 1)
                for n in range(2):
                    last = V.tensor_scalar(kmTs[:, n, :], bank(0)[0:64, 64 * n:64 * n + 64], pe_mean[:, n:n + 1], None, ALU.add)
                last.then_inc(S3["km_readyS"], 1)
                nxt(2)
                dve.wait_ge(S3["kcS_sq"], b + 1)
                V.tensor_copy(vcn, bank(1)[0:64, 64:128])
                V.scalar_tensor_tensor(kcn, bank(1)[0:64, 0:64], kr, kn_cmp[0:64, :], ALU.mult, ALU.mult).then_inc(S3["kcS_ready"], 1)
                nxt(3)
                dve.wait_ge(S3["kcT_done"], b + 1)
                V.tensor_copy(kcTs, bank(1)[0:64, 128:192]).then_inc(S3["kcT_ready"], 1)
                nxt(4)
                dve.wait_ge(S3["lcS_done"], b + 1)
                chain(V.tensor_tensor(lcs, bank(1)[0:4, 256:320], bcmp[0:4, :], ALU.add))
                V.tensor_reduce(nml, lcs, AX.X, ALU.max, negate=True).then_inc(S3["lcS_ready"], 1)
                nxt(5)
                dve.wait_ge(S3["pcS_exp"], b + 1)
                chain(V.tensor_scalar(rcl, lcl, 1e-30, None, ALU.max))
                chain(V.reciprocal(rcl, rcl))
                V.tensor_scalar(pcs, pcs, rcl, None, ALU.mult).then_inc(S3["pcS_ready"], 1)
                nxt(6)
                dve.wait_ge(S3["imp_done"], b + 1)
                V.tensor_copy(pcTs, bank(2)[0:64, 64:68]).then_inc(S3["pcT_ready"], 1)
                chain(V.tensor_tensor(srw, bank(2)[0:64, 0:64], K("forced", 64), ALU.max))
                chain(V.tensor_tensor(gtw, srw, K("ident", 64)[:, 0:64], ALU.mult))
                chain(V.tensor_reduce(scol, gtw, AX.X, ALU.add))
                chain(V.tensor_scalar(gtw, srw, scol, None, ALU.is_gt))
                chain(V.tensor_reduce(rk1, gtw, AX.X, ALU.add))
                chain(V.scalar_tensor_tensor(gtw, srw, scol, K("jlti", 64), ALU.is_equal, ALU.mult))
                chain(V.tensor_reduce(rk2, gtw, AX.X, ALU.add))
                chain(V.tensor_tensor(rk1, rk1, rk2, ALU.add))
                chain(V.tensor_scalar(rk1, rk1, 14.5, None, ALU.is_lt))
                V.tensor_scalar(rk1, rk1, -1.0, 1e30, ALU.add, ALU.mult).then_inc(S3["rank_ready"], 1)
                nxt(7)
                dve.wait_ge(S3["exp_done"], b + 1)
                chain(V.tensor_scalar(SC[:, :, 0:32], SC[:, :, 0:32], bank(2)[:, 256:257], None, ALU.add))
                segs = ((0, 33), (33, 38), (38, 40))
                for n, (a, c) in enumerate(segs):
                    last = V.tensor_reduce(mx12[:, 4 * n:4 * n + 4], SC[:, :, a:c], AX.X, ALU.max)
                last.then_inc(S3["mx_ready"], 1)
                nxt(8)
                dve.wait_ge(S3["mxT_done"], b + 1)
                chain(V.tensor_reduce(mcol, bank(3)[0:12, 0:128], AX.X, ALU.max))
                V.tensor_scalar(dg12, K("ident", 12)[:, 0:12], mcol, None, ALU.mult).then_inc(S3["mxc_ready"], 1)
                nxt(9)
                dve.wait_ge(S3["mxb_done"], b + 1)
                for n, (a, c) in enumerate(segs):
                    last = V.tensor_tensor(SC[:, :, a:c], SC[:, :, a:c],
                                           bank(3)[:, 128 + 4 * n:132 + 4 * n][:, :, None].broadcast_to([128, 4, c - a]), ALU.subtract)
                last.then_inc(S3["scS_ready"], 1)
                nxt(10)
                dve.wait_ge(S3["pS_ready"], b + 1)
                for n, (a, c) in enumerate(segs):
                    last = V.tensor_reduce(lp12[:, 4 * n:4 * n + 4], pSC[:, :, a:c], AX.X, ALU.add)
                last.then_inc(S3["lpS_ready"], 1)
                nxt(11)
                dve.wait_ge(S3["gs_e"], b + 1)
                chain(V.tensor_scalar(gg3, gg3, 1.0, None, ALU.add))
                chain(V.reciprocal(gg3, gg3))
                dve.wait_ge(S3["lS_done"], b + 1)
                chain(V.reciprocal(rl3, bank(3)[0:4, 144:147]))
                chain(V.tensor_tensor(gg3[:, 1:3], gg3[:, 1:3], rl3[:, 0:2], ALU.mult))
                for n in (12, 13, 14):
                    nxt(n)
                dve.wait_ge(S3["AB_done"], b + 1)
                if not (isinstance(b, int) and b == 0):
                    dve.wait_ge(S3["orow_out"], b * 48)
                chain(V.tensor_scalar(orow[:, 1, :], bank(7)[0:4, 0:64], gg3[:, 0:1], None, ALU.mult))
                chain(V.scalar_tensor_tensor(orow[:, 1, :], bank(5)[0:4, 0:64], gg3[:, 1:2], orow[:, 1, :], ALU.mult, ALU.add))
                chain(V.scalar_tensor_tensor(orow[:, 1, :], bank(5)[0:4, 64:128], gg3[:, 2:3], orow[:, 1, :], ALU.mult, ALU.add))
                chain(V.scalar_tensor_tensor(om4, bank(6)[0:4, 0:256], rl3[:, 2:3], K("blk4", 4), ALU.mult, ALU.mult))
                chain(V.tensor_reduce(orow[:, 2, :], om4.rearrange("p (h d) -> p d h", h=4), AX.X, ALU.add))
                nxt(15)
                dve.wait_ge(S3["vA_used"], 8 * b + 8)
                chain(V.tensor_tensor(om4, bank(4)[0:4, 0:256], K("blk4", 4), ALU.mult))
                V.tensor_reduce(orow[:, 0, :], om4.rearrange("p (h d) -> p d h", h=4), AX.X, ALU.add).then_inc(S3["orow_ready"], 1)

            for n in range(16):
                score(0, 0, 0, n)
            for b in range(2):
                n0 = chain.n
                seq(b, b, 0)
            CHAIN_VS = chain.n - n0
            with dve.Fori(1, NB // 2 - 1) as pair:
                i = pair * 2
                chain.enter(i - 2, CHAIN_VS)
                for par in range(2):
                    seq(i + par, par, i)
            chain.leave(NB - 4, 2)
            seq(NB - 2, 0, NB - 2)
            seq(NB - 1, 1, NB - 2, following=False)

        @block.scalar
        def _(act):
            A = nc.scalar.activation
            chain = Chain(act, S3["chSA"])
            nc.scalar.preload_act_table_set("natural_log_exp_and_others")

            def seq(b, par, i):
                zA, SC = zAs[par], SCs[par]
                act.wait_ge(S3["z_all"], b + 1)
                chain(A(labs, zA, ACT.Abs))
                chain(A(labs, labs, ACT.Exp, scale=-1.0))
                A(labs, labs, ACT.Ln, bias=one[:, :]).then_inc(S3["lS_ready"], 1)
                act.wait_ge(S3["w_ready"], b + 1)
                if not (isinstance(b, int) and b == 0):
                    act.wait_ge(S3["vA_used"], 8 * b)
                A(aA, wA, ACT.Exp).then_inc(S3["aS_ready"], 1)
                act.wait_ge(S3["kcS_done"], b + 1)
                chain(A(gtj, bank(1)[0:64, 0:64], ACT.Square, accum_out=kq))
                chain(A(kr, kq, ACT.Ln, bias=eps[0:64, :], scale=1.0 / 64))
                A(kr, kr, ACT.Exp, scale=-0.5).then_inc(S3["kcS_sq"], 1)
                act.wait_ge(S3["lcS_ready"], b + 1)
                A(pcs, lcs, ACT.Exp, bias=nml, accum_out=lcl).then_inc(S3["pcS_exp"], 1)
                act.wait_ge(row_in[par], i * (8 * NSMALL) + 16 * NSMALL)
                A(gg3, gs[par], ACT.Exp, scale=-1.0).then_inc(S3["gs_e"], 1)
                act.wait_ge(S3["scS_ready"], b + 1)
                A(pSC, SC, ACT.Exp).then_inc(S3["pS_ready"], 1)

            for b in range(2):
                n0 = chain.n
                seq(b, b, 0)
            CHAIN_AS = chain.n - n0
            with act.Fori(1, NB // 2) as pair:
                i = pair * 2
                chain.enter(i - 2, CHAIN_AS)
                for par in range(2):
                    seq(i + par, par, i)
            chain.leave(NB - 2, 2)
            act.wait_ge(S3["samT_done"], 1)
            samT = bank(7)[:, 0:64].rearrange("p (a b) -> p a b", b=8)
            A(OT[:, 0:4, SEQ:NCOL], samT[:, 0:4, :], ACT.Copy)
            A(OT[:, 6:8, SEQ:NCOL], samT[:, 6:8, :], ACT.Copy).then_inc(S3["samT_ready"], 1)

        @block.tensor
        def _(pe):
            MM, TR = nc.tensor.matmul, nc.tensor.transpose
            ident = K("ident")

            def wait(s, v):
                at = v if isinstance(v, int) else pe.snap(v)
                pe.wait_ge(S3["zeroS"], 1)
                pe.wait_ge(s, at)

            def seq(b, par, i):
                if not (isinstance(b, int) and b == 0):
                    wait(S3["orow_ready"], b)
                wait(row_in[par], i * (8 * NSMALL) + 16 * NSMALL)
                wait(S3["sum_ready"], b + 1)
                for n in range(2):
                    last = MM(bank(0)[0:64, 64 * n:64 * n + 64], ksums[par][:, n, :], K("pair"), start=True, stop=True)
                last.then_inc(S3["km_doneS"], 1)
                wait(S3["suf_ready"], b + 1)
                MM(bank(2)[:, 260:264], K("strict"), Csuf[:, :, 0], start=True, stop=True).then_inc(S3["X_done"], 1)
                wait(S3["km_readyS"], b + 1)
                for n in range(2):
                    last = MM(bank(1)[0:64, 64 * n:64 * n + 64], kmTs[:, n, :], phi_kv[:, n, :], start=True, stop=True)
                last.then_inc(S3["kcS_done"], 1)
                wait(S3["kcS_ready"], b + 1)
                TR(bank(1)[0:64, 128:192], kcn, ident[0:64, 0:64]).then_inc(S3["kcT_done"], 1)
                wait(S3["kcT_ready"], b + 1)
                MM(bank(1)[0:4, 256:320], qTs[par], kcTs, start=True, stop=True).then_inc(S3["lcS_done"], 1)
                wait(S3["pcS_ready"], b + 1)
                MM(bank(2)[0:64, 0:64], K("ones", 4)[:, 0:64], pcs, start=True, stop=True)
                TR(bank(2)[0:64, 64:68], pcs, ident[0:4, 0:4]).then_inc(S3["imp_done"], 1)
                wait(S3["pcT_ready"], b + 1)
                MM(bank(7)[0:4, 0:64], pcTs, vcn, start=True, stop=True)
                wait(S3["rank_ready"], b + 1)
                MM(bank(2)[:, 256:257], K("expand", 64), rk1, start=True, stop=True).then_inc(S3["exp_done"], 1)
                wait(S3["mx_ready"], b + 1)
                TR(bank(3)[0:12, 0:128], mx12, ident).then_inc(S3["mxT_done"], 1)
                wait(S3["mxc_ready"], b + 1)
                MM(bank(3)[:, 128:140], K("ones", 12), dg12, start=True, stop=True).then_inc(S3["mxb_done"], 1)
                wait(S3["lpS_ready"], b + 1)
                for n in range(3):
                    last = MM(bank(3)[0:4, 144 + n:145 + n], lp12[:, 4 * n:4 * n + 4], K("ones")[:, 0:1], start=True, stop=True)
                last.then_inc(S3["lS_done"], 1)
                wait(sel_in[par], i * 32 + 64)
                for r in range(NSEL):
                    MM(bank(5)[0:4, 0:64], pSC[:, :, r], Vs[par][:, r, :], start=(r == 0), stop=(r == NSEL - 1))
                for r in range(NWIN):
                    MM(bank(5)[0:4, 64:128], pSC[:, :, 33 + r], WV[par][:, r, :], start=(r == 0), stop=(r == NWIN - 1))
                for r in range(2):
                    last = MM(bank(6)[0:4, 0:256], pSC[:, :, 38 + r], MV[par][:, r, :], start=(r == 0), stop=(r == 1))
                last.then_inc(S3["AB_done"], 1)
                wait(S3["aS_ready"], b + 1)
                for c in range(8):
                    wait(vs_in[c % 4], b * 32 + 16 * (c // 4 + 1))
                    for r in range(4):
                        last = MM(bank(4)[0:4, 0:256], aA[:, :, 4 * c + r], vring[c % 4][:, r, :],
                                  start=(c == 0 and r == 0), stop=(c == 7 and r == 3))
                    last.then_inc(S3["vA_used"], 1)

            for b in range(2):
                seq(b, b, 0)
            with pe.Fori(1, NB // 2) as pair:
                i = pair * 2
                for par in range(2):
                    seq(i + par, par, i)
            pe.wait_ge(S3["samT_in"], 48)
            for a in (0, 1, 2, 3, 6, 7):
                last = TR(bank(7)[:, 8 * a:8 * a + 8], samrows[:, a * 128:a * 128 + 128], ident[0:8, 0:8])
            last.then_inc(S3["samT_done"], 1)

        stageS.close()
        stage_over()

        TC = NCOL // 3
        hT = arena[:, 0:KD * NCOL].rearrange("p (j t) -> p j t", j=KD)
        mT = arena[:, KD * NP1 - KD * NCOL:KD * NP1].rearrange("p (j t) -> p j t", j=KD)
        wout = TT[:, :, :]
        cursor[0] = 0
        wgate = [tmp(KD, 128) for _ in range(2)]
        wbr = [tmp(2, 128) for _ in range(2)]
        sgm = [tmp(TC) for _ in range(2)]
        mtmp = tmp(TC)
        hT_in, out_in = sem("hT_in"), sem("w_out_in")
        gate_in = [sem(f"gate_in{n}") for n in range(2)]
        gu_done, sg_ready, mrg_done, mtmp_ready = (sem(n) for n in ("gu_done", "sg_ready", "mrg_done", "mtmp_ready"))
        NG_U = 12
        br_d = I["w_branch"][0].rearrange("n (a p) d -> n p a d", p=128)

        stage3 = ExitStack()
        block = stage3.enter_context(nc.Block())

        @block.sync
        def _(sy):
            def load(j, n):
                cols = bass.ds(j * 128 + (NP1 + n * D), 128)
                sy.dma_start(wgate[n % 2], W1_d[:, :, cols]).then_inc(gate_in[n % 2], 16)
                sy.dma_start(wbr[n % 2], br_d[n][:, :, bass.ds(j * 128, 128)]).then_inc(gate_in[n % 2], 16)

            load(0, 0)
            for j in range(KD):
                sy.dma_start(hT[:, j, 0:SEQ], hT_d[:, j, :]).then_inc(hT_in, 16)
            load(0, 1)
            sy.dma_start(wout, I["w_out"][0].rearrange("(k p) n -> p k n", p=128)).then_inc(out_in, 16)
            with sy.Fori(0, KD - 1) as j:
                for n in range(4):
                    sy.wait_ge(gu_done, j * NG_U + 3 * (n + 1))
                    load(j + (n + 2) // 4, (n + 2) % 4)
            for n in range(2):
                sy.wait_ge(gu_done, (KD - 1) * NG_U + 3 * (n + 1))
                load(KD - 1, n + 2)

        @block.tensor
        def _(pe):
            MM = nc.tensor.matmul

            def channels(j, first=False):
                for n in range(4):
                    pe.wait_ge(gate_in[n % 2], j * 64 + 32 * (n // 2 + 1))
                    for c in range(3):
                        u = 3 * n + c
                        if not (first and u < 4):
                            pe.wait_ge(mrg_done, j * NG_U + (u - 3))
                        cols = slice(c * TC, c * TC + TC)
                        G, U = bank(2 * (u % 4))[:, 0:TC], bank(2 * (u % 4) + 1)[:, 0:TC]
                        for k in range(KD):
                            MM(G, wgate[n % 2][:, k, :], hT[:, k, cols], start=(k == 0), stop=(k == KD - 1))
                        for a in range(2):
                            last = MM(U, wbr[n % 2][:, a, :], OT[:, 2 * n + a, cols], start=(a == 0), stop=(a == 1))
                        last.then_inc(gu_done, 1)

            pe.wait_ge(hT_in, 16 * KD + 1)
            channels(0, True)
            with pe.Fori(1, KD) as j:
                channels(j)

        @block.scalar
        def _(act):
            nc.scalar.preload_act_table(ACT.Sigmoid)

            def channels(j, first=False):
                for u in range(NG_U):
                    act.wait_ge(gu_done, j * NG_U + (u + 1))
                    if not (first and u < 2):
                        act.wait_ge(mrg_done, j * NG_U + (u - 1))
                    nc.scalar.activation(sgm[u % 2], bank(2 * (u % 4))[:, 0:TC], ACT.Sigmoid).then_inc(sg_ready, 1)

            channels(0, True)
            with act.Fori(1, KD) as j:
                channels(j)

        @block.vector
        def _(dve):
            V = nc.vector
            V.tensor_copy(hT[:, :, SEQ:NCOL], hT_s[:, :, :]).then_inc(hT_in, 1)

            def channels(j, first=False):
                for u in range(NG_U):
                    n, c = u // 3, u % 3
                    U = bank(2 * (u % 4) + 1)[:, 0:TC]
                    dst = mT[:, bass.ds(j, 1), c * TC:c * TC + TC]
                    dve.wait_ge(sg_ready, j * NG_U + (u + 1))
                    if n == 0:
                        V.tensor_tensor(dst, sgm[u % 2][:, None, :], U[:, None, :], ALU.mult).then_inc(mrg_done, 1)
                    else:
                        dve.wait_ge(mrg_done, j * NG_U + u)
                        V.tensor_tensor(mtmp, sgm[u % 2], U, ALU.mult).then_inc(mtmp_ready, 1)
                        dve.wait_ge(mtmp_ready, j * 9 + (u - 2))
                        V.tensor_tensor(dst, dst, mtmp[:, None, :], ALU.add).then_inc(mrg_done, 1)

            channels(0, True)
            with dve.Fori(1, KD) as j:
                channels(j)

        @block.gpsimd
        def _(pool):
            pool.wait_ge(out_in, 16)

        stage3.close()
        stage_over()

        NTS = NT + 1
        x2 = arena[:, 0:NTS * D].rearrange("p (t n) -> p t n", t=NTS)
        a4 = NTS * D
        comb = arena[:, a4:a4 + NTS * NE].rearrange("p (t e) -> p t e", t=NTS)
        csl = [arena[:, a4 + NTS * NE + NTS * n:a4 + NTS * NE + NTS * (n + 1)] for n in range(2)]
        assert a4 + NTS * (NE + 2) <= KD * NP1 - KD * NCOL
        tT = OT
        cursor[0] = 0
        xr = [tmp(D) for _ in range(2)]
        xm = tmp(D)
        sqj = tmp(D)
        wr = tmp(KD, 20)
        rbias = tmp(20)
        lg = tmp(NTS, 20)
        q1, q2 = tmp(1), tmp(1)
        gmx, gsum = tmp(NTS), tmp(NTS)
        e4, oh, eq = tmp(NTS, 4), tmp(NTS, 4), tmp(NTS, 4)
        cov = tmp(NTS)
        t16 = tmp(NTS, 16)
        le, le2, ee, o1, o2 = (tmp(NTS, 4) for _ in range(5))
        m1, s1 = tmp(NTS), tmp(NTS)
        NM4 = ("xr_in", "wr_in", "op_done", "x2_ready", "rs_ready", "xm_ready", "xm_tp", "tT_ready", "rt_done", "lg_ready",
               "ex_in", "ex_out", "ex2_in", "ex2_out", "ch4A", "ch4V")
        S4 = {n: sem(n) for n in NM4}
        R_ = lambda t: 128 if t < NT else NB
        C_ = lambda t: slice(t * 128, t * 128 + R_(t))

        stage4 = ExitStack()
        block = stage4.enter_context(nc.Block())

        @block.sync
        def _(sy):
            sy.dma_start(wr[:, :, 0:4], I["w_grp"][0].rearrange("(p j) n -> p j n", j=KD)).then_inc(S4["wr_in"], 16)
            sy.dma_start(wr[:, :, 4:20], I["w_rt"][0].rearrange("(p j) n -> p j n", j=KD)).then_inc(S4["wr_in"], 16)
            sy.dma_start(rbias[:, 0:4], I["b_grp"][0:1].broadcast_to([128, 4])).then_inc(S4["wr_in"], 16)
            sy.dma_start(rbias[:, 4:20], I["b_rt"][0:1].broadcast_to([128, 16])).then_inc(S4["wr_in"], 16)
            for t in range(NTS):
                if t >= 1:
                    sy.wait_ge(S4["x2_ready"], t)
                src = x_p[t * 128:t * 128 + 128, :] if t < NT else x_s
                sy.dma_start(xr[t % 2][0:R_(t), :], src).then_inc(S4["xr_in"], 16)

        @block.tensor
        def _(pe):
            MM, TR = nc.tensor.matmul, nc.tensor.transpose
            ident = K("ident")

            def project(t):
                R = R_(t)
                if t >= 2:
                    pe.wait_ge(S4["x2_ready"], t - 1)
                for half in range(2):
                    for k in range(KD):
                        last = MM(bank(2 * (t % 2) + half)[0:R, :], mT[:, k, C_(t)], wout[:, k, half * 512:half * 512 + 512],
                                  start=(k == 0), stop=(k == KD - 1))
                last.then_inc(S4["op_done"], 1)

            def route(t):
                R = R_(t)
                pe.wait_ge(S4["xm_ready"], t + 1)
                if t:
                    pe.wait_ge(S4["tT_ready"], t)
                for k in range(KD):
                    last = TR(bank(4, 2)[:, k * 128:k * 128 + R], xm[0:R, k:D:KD], ident[0:R, 0:R])
                last.then_inc(S4["xm_tp"], 1)
                pe.wait_ge(S4["tT_ready"], t + 1)
                if t:
                    pe.wait_ge(S4["lg_ready"], t)
                for k in range(KD):
                    last = MM(bank(6)[0:R, 0:20], tT[:, k, C_(t)], wr[:, k, :], start=(k == 0), stop=(k == KD - 1))
                last.then_inc(S4["rt_done"], 1)

            project(0)
            pe.wait_ge(S4["wr_in"], 64)
            for t in range(NTS):
                if t + 1 < NTS:
                    project(t + 1)
                route(t)

        @block.scalar
        def _(act):
            A = nc.scalar.activation
            chain = Chain(act, S4["ch4A"])
            nc.scalar.preload_act_table_set("natural_log_exp_and_others")
            for t in range(NTS):
                R = R_(t)
                act.wait_ge(S4["x2_ready"], t + 1)
                chain(A(sqj[0:R, :], x2[0:R, t, :], ACT.Square, accum_out=q1[0:R, :]))
                chain(A(q1[0:R, :], q1[0:R, :], ACT.Ln, bias=eps[0:R, :], scale=1.0 / D))
                if t:
                    act.wait_ge(S4["xm_ready"], t)
                A(q2[0:R, :], q1[0:R, :], ACT.Exp, scale=-0.5).then_inc(S4["rs_ready"], 1)
            act.wait_ge(S4["ex_in"], 1)
            A(e4, e4, ACT.Exp).then_inc(S4["ex_out"], 1)
            act.wait_ge(S4["ex2_in"], 1)
            A(ee, ee, ACT.Exp).then_inc(S4["ex2_out"], 1)

        @block.vector
        def _(dve):
            V = nc.vector
            chain = Chain(dve, S4["ch4V"])
            chain(V.memset(lg[:, NT, :], 0.0))
            dve.wait_ge(S4["wr_in"], 64)

            def residual(t):
                R = R_(t)
                dve.wait_ge(S4["xr_in"], 16 * (t + 1))
                dve.wait_ge(S4["op_done"], t + 1)
                V.tensor_tensor(x2[0:R, t, :], bank(2 * (t % 2), 2)[0:R, :], xr[t % 2][0:R, :], ALU.add)\
                    .then_inc(S4["x2_ready"], 1)

            residual(0)
            for t in range(NTS):
                R = R_(t)
                dve.wait_ge(S4["rs_ready"], t + 1)
                if t:
                    dve.wait_ge(S4["xm_tp"], t)
                V.tensor_scalar(xm[0:R, :], x2[0:R, t, :], q2[0:R, :], None, ALU.mult).then_inc(S4["xm_ready"], 1)
                if t + 1 < NTS:
                    residual(t + 1)
                dve.wait_ge(S4["xm_tp"], t + 1)
                V.tensor_tensor(tT[:, :, C_(t)], bank(4, 2).rearrange("p (j t) -> p j t", j=KD)[:, :, 0:R],
                                g_ffn[:, :, None].broadcast_to([128, KD, R]), ALU.mult).then_inc(S4["tT_ready"], 1)
                dve.wait_ge(S4["rt_done"], t + 1)
                V.tensor_tensor(lg[0:R, t, :], bank(6)[0:R, 0:20], rbias[0:R, :], ALU.add).then_inc(S4["lg_ready"], 1)
            dve.wait_ge(S4["lg_ready"], NTS)
            wide = lambda v: v[:, :, None].broadcast_to([128, NTS, 4])

            def first_max(x, mx, out):
                chain(V.tensor_tensor(eq, x, wide(mx), ALU.is_equal))
                V.tensor_copy(out[:, :, 0], eq[:, :, 0])
                chain(V.tensor_copy(cov, eq[:, :, 0]))
                for n in range(1, 4):
                    chain(V.scalar_tensor_tensor(out[:, :, n], cov, 0.5, eq[:, :, n], ALU.is_lt, ALU.mult))
                    if n < 3:
                        chain(V.tensor_tensor(cov, cov, eq[:, :, n], ALU.max))

            grp = lg[:, :, 0:4]
            chain(V.tensor_reduce(gmx, grp, AX.X, ALU.max))
            V.tensor_tensor(e4, grp, wide(gmx), ALU.subtract).then_inc(S4["ex_in"], 1)
            first_max(grp, gmx, oh)
            chain(V.tensor_tensor(t16.rearrange("p t (e g) -> p t e g", e=4), lg[:, :, 4:20].rearrange("p t (g e) -> p t e g", g=4),
                                  oh[:, :, None, :].broadcast_to([128, NTS, 4, 4]), ALU.mult))
            chain(V.tensor_reduce(le, t16.rearrange("p t (e g) -> p t e g", e=4), AX.X, ALU.add))
            chain(V.tensor_reduce(m1, le, AX.X, ALU.max))
            V.tensor_tensor(ee, le, wide(m1), ALU.subtract).then_inc(S4["ex2_in"], 1)
            first_max(le, m1, o1)
            chain(V.scalar_tensor_tensor(le2, o1, NEG, le, ALU.mult, ALU.add))
            chain(V.tensor_reduce(m1, le2, AX.X, ALU.max))
            first_max(le2, m1, o2)
            chain(V.tensor_tensor(o1, o1, o2, ALU.add))
            dve.wait_ge(S4["ex2_out"], 1)
            chain(V.tensor_tensor(ee, ee, o1, ALU.mult))
            chain(V.tensor_reduce(s1, ee, AX.X, ALU.add))
            dve.wait_ge(S4["ex_out"], 1)
            chain(V.tensor_reduce(gsum, e4, AX.X, ALU.add))
            chain(V.tensor_tensor(s1, s1, gsum, ALU.mult))
            chain(V.reciprocal(s1, s1))
            chain(V.tensor_tensor(ee, ee, wide(s1), ALU.mult))
            chain(V.tensor_tensor(comb.rearrange("p t (g e) -> p t g e", g=4), oh[:, :, :, None].broadcast_to([128, NTS, 4, 4]),
                                  ee[:, :, None, :].broadcast_to([128, NTS, 4, 4]), ALU.mult))

        stage4.close()
        stage_over()

        flatTT = TT[:, :, :].rearrange("p a b -> p (a b)")
        weg = [flatTT[:, n * 4096:n * 4096 + 2048].rearrange("p (k f) -> p k f", k=KD) for n in range(2)]
        weu = [flatTT[:, n * 4096 + 2048:n * 4096 + 4096].rearrange("p (k f) -> p k f", k=KD) for n in range(2)]
        cursor[0] = 0
        wed = [tmp(2, D) for _ in range(2)]
        hid = [tmp(2, NCOL) for _ in range(2)]
        sil5 = [tmp(TC) for _ in range(2)]
        NM5 = ("up_done", "silu_ready", "hid_ready", "dn_done", "acc_done", "cs_ready", "y_out")
        S5 = {n: sem(n) for n in NM5}
        gu_in = [sem(f"gu_in{n}") for n in range(2)]
        dn_in = [sem(f"dn_in{n}") for n in range(2)]
        NU, NDN = 6, 2 * NTS

        stage5 = ExitStack()
        block = stage5.enter_context(nc.Block())

        @block.sync
        def _(sy):
            eg_d = I["w_eg"][0].rearrange("e (p j) f -> p e j f", j=KD)
            eu_d = I["w_eu"][0].rearrange("e (p j) f -> p e j f", j=KD)
            ed_d = I["w_ed"][0].rearrange("e (a p) d -> p e a d", p=128)

            def load_up(e, par):
                sy.dma_start(weg[par][:, None], eg_d[:, bass.ds(e, 1)]).then_inc(gu_in[par], 16)
                sy.dma_start(weu[par][:, None], eu_d[:, bass.ds(e, 1)]).then_inc(gu_in[par], 16)

            def load_down(e, par):
                sy.dma_start(wed[par][:, None], ed_d[:, bass.ds(e, 1)]).then_inc(dn_in[par], 16)

            for par in range(2):
                load_up(par, par)
                load_down(par, par)
            with sy.Fori(0, NE // 2 - 1) as pair:
                for par in range(2):
                    sy.wait_ge(S5["up_done"], pair * (2 * NU) + NU * (par + 1))
                    load_up(pair * 2 + (par + 2), par)
                    sy.wait_ge(S5["dn_done"], pair * (2 * NDN) + NDN * (par + 1))
                    load_down(pair * 2 + (par + 2), par)
            for t in range(NTS):
                sy.wait_ge(S5["acc_done"], NDN * (NE - 1) + 2 * (t + 1))
                dst = O[0][0, t * 128:t * 128 + 128, :] if t < NT else O[1][:, 0, :]
                sy.dma_start(dst, x2[0:R_(t), t, :]).then_inc(S5["y_out"], 16)
            sy.wait_ge(S5["y_out"], 16 * NTS)

        @block.tensor
        def _(pe):
            MM = nc.tensor.matmul

            def expert(pair, par, first=False):
                pe.wait_ge(gu_in[par], pair * 32 + 32)
                for u in range(NU):
                    c, f = u // 2, u % 2
                    if not (first and u < 2):
                        pe.wait_ge(S5["hid_ready"], pair * (2 * NU) + (NU * par + u - 1))
                    cols = slice(c * TC, c * TC + TC)
                    for w, b in ((weg, 2 * (u % 2)), (weu, 2 * (u % 2) + 1)):
                        for k in range(KD):
                            last = MM(bank(b)[:, 0:TC], w[par][:, k, f * 128:f * 128 + 128], tT[:, k, cols],
                                      start=(k == 0), stop=(k == KD - 1))
                    last.then_inc(S5["up_done"], 1)
                pe.wait_ge(dn_in[par], pair * 16 + 16)
                for v in range(NDN):
                    t, half = v // 2, v % 2
                    R = R_(t)
                    if half == 0:
                        need = 2 * ((t * 128 + R - 1) // TC + 1)
                        pe.wait_ge(S5["hid_ready"], pair * (2 * NU) + (NU * par + need))
                    if not (first and v < 4):
                        pe.wait_ge(S5["acc_done"], pair * (2 * NDN) + (NDN * par + v - 3))
                    for f in range(2):
                        last = MM(bank(4 + (2 * par + v) % 4)[0:R, :], hid[par][:, f, C_(t)],
                                  wed[par][:, f, half * 512:half * 512 + 512], start=(f == 0), stop=(f == 1))
                    last.then_inc(S5["dn_done"], 1)

            expert(0, 0, True)
            expert(0, 1)
            with pe.Fori(1, NE // 2) as pair:
                for par in range(2):
                    expert(pair, par)

        @block.scalar
        def _(act):
            nc.scalar.preload_act_table(ACT.Silu)

            def expert(pair, par, first=False):
                for u in range(NU):
                    act.wait_ge(S5["up_done"], pair * (2 * NU) + (NU * par + u + 1))
                    if not (first and u < 2):
                        act.wait_ge(S5["hid_ready"], pair * (2 * NU) + (NU * par + u - 1))
                    nc.scalar.activation(sil5[u % 2], bank(2 * (u % 2))[:, 0:TC], ACT.Silu).then_inc(S5["silu_ready"], 1)

            expert(0, 0, True)
            expert(0, 1)
            with act.Fori(1, NE // 2) as pair:
                for par in range(2):
                    expert(pair, par)

        @block.vector
        def _(dve):
            V = nc.vector

            def expert(pair, par, first=False):
                V.tensor_copy(csl[par][:, :, None], comb[:, :, bass.ds(pair * 2 + par, 1)]).then_inc(S5["cs_ready"], 1)
                for u in range(NU):
                    c, f = u // 2, u % 2
                    dve.wait_ge(S5["silu_ready"], pair * (2 * NU) + (NU * par + u + 1))
                    V.tensor_tensor(hid[par][:, f, c * TC:c * TC + TC], sil5[u % 2], bank(2 * (u % 2) + 1)[:, 0:TC],
                                    ALU.mult).then_inc(S5["hid_ready"], 1)
                dve.wait_ge(S5["cs_ready"], pair * 2 + (par + 1))
                for v in range(NDN):
                    t, half = v // 2, v % 2
                    R = R_(t)
                    dve.wait_ge(S5["dn_done"], pair * (2 * NDN) + (NDN * par + v + 1))
                    acc = x2[0:R, t, half * 512:half * 512 + 512]
                    V.scalar_tensor_tensor(acc, bank(4 + (2 * par + v) % 4)[0:R, :], csl[par][0:R, t:t + 1], acc,
                                           ALU.mult, ALU.add).then_inc(S5["acc_done"], 1)

            expert(0, 0, True)
            expert(0, 1)
            with dve.Fori(1, NE // 2) as pair:
                for par in range(2):
                    expert(pair, par)

        stage5.close()


INPUTS = ['x_prompt', 'x_sample', 'mem_prompt', 'cache_sb_k', 'cache_sb_v', 'cache_nsa_cmp_k', 'cache_nsa_cmp_v',
          'cache_nsa_sel_k', 'cache_nsa_sel_v', 'cache_nsa_win_k', 'cache_nsa_win_v', 'state_gla', 'cache_mem_k',
          'cache_mem_v', 'page_table', 'norm_mix_g', 'norm_ffn_g', 'norm_mem_g', 'w_in', 'gla_gate_up', 'gla_gate_b',
          'gla_norm_g', 'nsa_pe_k', 'nsa_pe_v', 'nsa_phi_k', 'nsa_phi_v', 'nsa_qn_g', 'nsa_kn_g', 'mem_qn_g',
          'mem_kn_g', 'w_mem_kv', 'w_branch', 'w_out', 'rel_bias', 'w_grp', 'b_grp', 'w_rt', 'b_rt', 'w_eg', 'w_eu',
          'w_ed']
OUTPUTS = [(1, SEQ, D), (NB, 1, D), (1, 1, SEQ, 4, 64), (1, 1, SEQ, 4, 64), (1, 1, SEQ, 64), (1, 1, SEQ, 64),
           (1, 1, SEQ, 64), (1, 1, SEQ, 64), (1, 1, 512, 64), (1, 1, 512, 64), (1, 1, 4, 32, 64),
           (1, 1, MEM, 4, 64), (1, 1, MEM, 4, 64), (1, NB, 1, 4, 64), (1, NB, 1, 4, 64), (1, NB, 1, 64),
           (1, NB, 1, 64), (1, NB, 1, 64), (1, NB, 1, 64), (1, NB, 512, 64), (1, NB, 512, 64), (1, NB, 4, 32, 64)]


def kernel(**inputs):
    import concourse.bacc as bacc
    from concourse.bass_utils import run_bass_kernel_spmd

    nc = bacc.Bacc("TRN2", target_bir_lowering=False, num_devices=1)
    at, table = shape_constants()
    arrays = {n: np.ascontiguousarray(inputs[n]) for n in INPUTS}
    arrays.update(shape_table=table, distance_table=distance_onehots(), row_table=row_offsets())
    aps = {n: nc.dram_tensor("in_" + n, a.shape, mybir.dt.from_np(a.dtype), kind="ExternalInput").ap()
           for n, a in arrays.items()}
    outs = [nc.dram_tensor(f"out_{i}", s, F32, kind="ExternalOutput").ap() for i, s in enumerate(OUTPUTS)]
    build(nc, aps, outs, at, aps["shape_table"], aps["distance_table"], aps["row_table"], None)
    r = run_bass_kernel_spmd(nc, [{"in_" + n: a for n, a in arrays.items()}], core_ids=[0])
    return tuple(r.results[0][f"out_{i}"] for i in range(len(OUTPUTS)))
```

```python
import math
from contextlib import ExitStack

import numpy as np

import concourse.bass as bass
from concourse import mybir

F32 = mybir.dt.float32
F32R = mybir.dt.float32r
I32 = mybir.dt.int32
U32 = mybir.dt.uint32
ALU = mybir.AluOpType
ACT = mybir.ActivationFunctionType
AX = mybir.AxisListType

D = 1024
KD = D // 128
SEQ = 1024
NT = SEQ // 128
NB = 8
NCOL = SEQ + NB
MEM = 256
PAST = 4096
PAGE = 128
NPAGE = PAST // PAGE
NP1 = 2460
CH = 492
NCH = NP1 // CH
EPS = 1e-6
NEG = -1e30
NE = 16
DE = 256
NSLOT = (2 * NCOL + NE * 127) // 128
(SBQ, SBK, SBV, NQ, KC, VC, KS, VS, KW, VW, NG, GQ, GK, GV, GA, GR, MQ) = (
    0, 256, 512, 768, 1024, 1088, 1152, 1216, 1280, 1344, 1408, 1420, 1548, 1676, 1932, 1948, 2204)
QNB, QNM, QNS, QNW = 0, 256, 512, 640
(RQA, RQB, RQM, RKS, RVS, RKW, RVW, RG, RW) = (0, 256, 512, 768, 832, 896, 960, 1024, 1036)


def bucket(dist):
    n = np.maximum(dist, 0)
    nf = np.maximum(n, 1).astype(np.float32)
    large = 16 + (np.log(nf / np.float32(16)) / np.float32(math.log(8)) * np.float32(16)).astype(np.int32)
    return np.where(n < 16, n, np.minimum(large, 31))


def onehot(dist):
    row = np.where(dist < 0, 32, bucket(dist))
    return (np.arange(33).reshape((33,) + (1,) * dist.ndim) == row[None]).astype(np.float32)


OHC = 1984
NEAR = 384
NSEL, NWIN = 33, 5


def shape_constants():
    p = np.arange(128)
    a, b = p[:, None], p[None, :]
    same = (a // 64) == (b // 64)
    mid = (b // 64) * 64 + 31
    c = {}
    c["ident"] = (a == b)
    c["ones"] = np.ones((128, 128))
    c["gm_mid"] = -(1.0 * (a <= b) * same - 1.0 * (a <= mid) * same) / 16.0
    c["gm_cum"] = -1.0 * (a <= b) * same / 16.0
    c["gm_suf"] = -1.0 * (a > b) * same / 16.0
    c["glamask"] = 1.0 * (a <= b) * same
    c["bd256"] = 1.0 * ((a // 32) == (np.arange(256)[None, :] // 64))
    c["ind2"] = ((a // 64) == np.arange(2)[None, :]) / 64.0
    c["hcol"] = np.stack([p < 64, p >= 64], 1)
    c["eye88"] = 1.0 * np.broadcast_to((np.arange(64) // 8) == (np.arange(64) % 8), (128, 64))
    c["negtri"] = -1.0 * (a >= b)
    c["negones"] = -np.ones((128, 128))
    c["causal01"] = 1.0 * (a < b)
    c["causalneg"] = NEG * (a >= b)
    c["winneg"] = NEG * (b < a)
    c["strict"] = 1.0 * (a > b)
    c["blk4"] = 1.0 * (a == (np.arange(256)[None, :] // 64))
    c["pair"] = ((a // 2) == np.arange(64)[None, :]) / 64.0
    c["rep16"] = 1.0 * (a == (np.arange(64)[None, :] % 16))
    c["cbd"] = 1.0 * ((a // 16) == (np.arange(256)[None, :] // 64))
    c["restart"] = np.broadcast_to(1.0 * ((np.arange(128) % 32) != 31), (128, 128))
    c["expand"] = 1.0 * (a == (b // 2))
    c["jlti"] = 1.0 * (np.arange(64)[None, :] < a)
    forced = 1e9 * np.isin(np.arange(64), (0, 63)).astype(np.float64)
    c["forced"] = np.broadcast_to(forced, (128, 64))
    c["onehot8"] = 1.0 * (a == (np.arange(1024)[None, :] // 128))
    t = np.arange(NT + 1)[None, :]
    valid = (t < NT) | (a < NB)
    c["iota"] = np.arange(128)[None, :] - 128.0
    c["slot_lo"] = 128.0 * np.arange(NSLOT + 1)[None, :]
    c["slot_id"] = 1.0 * np.arange(NSLOT)[None, :]
    c["valid"] = 1.0 * valid
    c["token"] = (t * 128 + a) * valid
    c["upto"] = 1.0 * (np.arange(NE)[None, :] <= np.arange(NE)[:, None]).reshape(1, -1)
    c["row"] = 1.0 * a
    at, out, cols = {}, [], 0
    for name, v in c.items():
        v = np.broadcast_to(v, (128, v.shape[1])).astype(np.float32)
        at[name] = (cols, v.shape[1])
        cols += v.shape[1]
        out.append(v)
    return at, np.ascontiguousarray(np.concatenate(out, 1))


def distance_onehots():
    p = np.arange(128)
    parts = [onehot(np.arange(OHC) - 1023)]
    r = np.arange(NSEL)[:, None]
    parts.append(onehot(np.where(r < 32, PAST - 32 * p[None] - r, np.where(p[None] == 0, 0, -1))).reshape(33, -1))
    r = np.arange(NWIN)[:, None]
    parts.append(onehot(np.where(r < 4, 512 - 4 * p[None] - r, np.where(p[None] == 0, 0, -1))).reshape(33, -1))
    parts.append(onehot(PAST - 64 * np.arange(64) - 63))
    parts.append(onehot(255 - np.arange(NEAR)))
    return np.ascontiguousarray(np.concatenate(parts, 1))


def row_offsets():
    p = np.arange(128)[:, None]
    return np.ascontiguousarray(np.concatenate([(p % 4) * 8 + np.arange(8)[None], p % 4], 1).astype(np.int32))


class Chain:

    def __init__(self, eng, sem):
        self.eng, self.sem, self.base, self.n = eng, sem, 0, 0

    def __call__(self, ins):
        self.n += 1
        ins.then_inc(self.sem, 1)
        self.eng.wait_ge(self.sem, self.base + self.n)

    def enter(self, i, per):
        self.start = self.base + self.n
        self.base, self.n, self.per = self.start + i * per, 0, per

    def leave(self, trips, unrolled=1):
        assert self.n == self.per * unrolled, f"chain {self.sem}: {self.n} steps in the body"
        self.base, self.n = self.start + trips * self.per, 0


CHAIN_V1, CHAIN_A1 = 11, 6
SMALL = 10240


def build(nc, I, O, consts_at, C_d, OH_d, RO_d, stages):
    ctx = ExitStack()
    with ctx:
        ctx.enter_context(nc.allow_non_contiguous_dma(reason="small gains and biases"))

        def sb(name, shape, dt=F32):
            return ctx.enter_context(nc.sbuf_tensor(name, shape, dt))

        def sem(name):
            live.append(nc.alloc_semaphore(name))
            return live[-1]

        live = []

        def stage_over():
            nc.clear_and_free_semaphores(live)
            live.clear()
            nc.all_engine_barrier()

        hT_d = nc.dram_tensor("hT_scratch", [128, KD, SEQ], F32).ap()
        srow_d = nc.dram_tensor("sample_rows", [NB, RW], F32).ap()
        skew_d = nc.dram_tensor("near_bias", [128, 4, NEAR], F32)
        osam_d = nc.dram_tensor("sample_branch_rows", [NB, 1024], F32).ap()
        xm_d = nc.dram_tensor("normed_rows", [NCOL, D], F32).ap()
        slots_d = nc.dram_tensor("slot_rows", [NSLOT * 128, D], F32).ap()

        c_early, c_late = consts_at["negtri"][0], consts_at["onehot8"][0]
        cst = sb("cst", [128, c_early])

        def K(name, r=128):
            a, w = consts_at[name]
            return cst[0:r, a:a + w] if a < c_early else late[0:r, a - c_early:a - c_early + w]

        eps = sb("eps", [128, 1])
        one = sb("one", [128, 1])
        g_mix, g_ffn, g_mem = sb("g_mix", [128, KD]), sb("g_ffn", [128, KD]), sb("g_mem", [128, KD])
        qn_gain = sb("qn_gain", [128, 640])
        kn_mem = sb("kn_mem", [128, 64])
        kn_cmp = sb("kn_cmp", [128, 64])
        g_gla = sb("g_gla", [128, 64])
        pe_kv = sb("pe_kv", [64, 2, 64])
        phi_kv = sb("phi_kv", [64, 2, 64])
        pe_mean = sb("pe_mean", [64, 2])
        gate_up = sb("gate_up", [16, 128])
        gate_b = sb("gate_b", [1, 128])
        tab = sb("tab", [33, 4])
        TT = sb("TT", [128, 8, SEQ])
        OT = sb("OT", [128, 8, NCOL])
        kmT = sb("kmT", [64, 2, 16])
        hT_s = sb("hT_s", [128, KD, NB])
        small = sb("small", [128, SMALL])
        first_stages = ctx.enter_context(ExitStack())

        def sb1(name, shape):
            return first_stages.enter_context(nc.sbuf_tensor(name, shape, F32))

        VA = sb1("VA", [128, NT, 256])
        VSt = sb1("VSt", [128, NT, 64])
        VWt = sb1("VWt", [128, NT, 64])
        KWt = sb1("KWt", [128, NT, 64])
        NGt = sb1("NGt", [128, NT, 12])
        arena = sb1("arena", [128, KD * NP1])
        W1 = arena[:, :].rearrange("p (j n) -> p j n", j=KD)
        wmem = TT[:, 0:4, :].rearrange("p a b -> p (a b)").rearrange("p (j n) -> p j n", j=KD)
        early = OT[:, 0:4, :].rearrange("p a b -> p (a b)")
        xt = early[:, 0:1024]
        xn = early[:, 1024:2048]
        hTs = early[:, 2048:3072].rearrange("p (j t) -> p j t", j=KD)
        sqx = early[:, 3072:4096]
        late_w = c_late - c_early
        late = arena[:, 0:late_w]
        cursor, room = [0], [small]

        def tmp(*dims, r=128):
            n = int(np.prod(dims))
            v = room[0][0:r, cursor[0]:cursor[0] + n]
            cursor[0] += n
            assert cursor[0] <= SMALL, cursor[0]
            if len(dims) == 2:
                return v.rearrange("p (a b) -> p a b", a=dims[0])
            if len(dims) == 3:
                return v.rearrange("p (a b c) -> p a b c", a=dims[0], b=dims[1])
            return v

        P = tmp(NP1)
        sq = tmp(768)
        QN = tmp(768)
        ss, r10 = tmp(10), tmp(10)
        ssq, lnx, rstd = tmp(1), tmp(1), tmp(1)
        mq = tmp(2, 2, 128)
        mkT = tmp(2, MEM)
        mv = tmp(2, 256)
        mp = sqx.rearrange("p (a b) -> p a b", a=4)
        mpT = xn.rearrange("p (a b) -> p a b", a=8)
        nmx, lm, rlm = tmp(4), tmp(4), tmp(4)
        gqT, gkT = tmp(128), tmp(128)
        aT = tmp(128, r=16)
        pab, pln, sp = tmp(128), tmp(128), tmp(128)
        cclip = tmp(128)
        Emid, Eimid, Ecum, Esuf = (sq[:, n * 128:(n + 1) * 128] for n in range(4))
        q1bd = tmp(4, 128)
        k1T = tmp(128)
        q3 = tmp(2, 128)
        k4 = tmp(2, 128)
        attm = tmp(4, 128)
        updm = tmp(2, 256)
        Sa, Sb = tmp(256), tmp(256)
        er = tmp(256)
        sil = er
        oCM = tmp(512)
        sq2 = sq[:, 512:768]
        s4, l4, r4 = tmp(4), tmp(4), tmp(4)
        km8 = TT[0:8, 5, :].rearrange("p (a b) -> p a b", a=8)
        oh8 = TT[0:8, 6, :].rearrange("p (a b) -> p a b", a=8)
        S0s = TT[:, 4, 0:512].rearrange("p (a b) -> p a b", a=8)
        S1s = TT[:, 4, 512:1024].rearrange("p (a b) -> p a b", a=8)
        qTm = tmp(8, 8)
        PS = ctx.enter_context(nc.psum_tensor("PS", [128, 4096], F32))

        def bank(b, n=1):
            return PS[:, b * 512:(b + n) * 512]

        (c_in, w_in_s, x_in, hT_out, rows_out, kv_out, const_ready, rstd_ready, xn_ready, xn_tp, hts_ready,
         kv_done, kv_p, proj_done, p_ready, sq_ready, ss_ready, r_ready, qn_ready, qn_tp, tt_evac, slots_ready,
         kv_tp, mk_ready, km_done, km_evac, aT_tp, aT_ready, pre_done, ln_ready, sp_ready, cum_done, clip_ready,
         exps_ready, gl_ready, att_done, attm_ready, upd_done, sb_ready, oc_done, sa_ready, sq2_ready, s4_ready,
         r4_ready, er_ready, oc_ready, msc_done, nmx_ready, mp_ready, mpt_tp, mpt_evac, mo_done, om_ready, ot_tp,
         ot_evac, pool_done, seT_done, seT_ready, supd_done, supd_used, sbd_ready, chA, chV, w_done, gla_out) = (
            sem(n) for n in (
                "c_in", "w_in_s", "x_in", "hT_out", "rows_out", "kv_out", "const_ready", "rstd_ready", "xn_ready",
                "xn_tp", "hts_ready", "kv_done", "kv_p", "proj_done", "p_ready", "sq_ready", "ss_ready", "r_ready",
                "qn_ready", "qn_tp", "tt_evac", "slots_ready", "kv_tp", "mk_ready", "km_done", "km_evac", "aT_tp",
                "aT_ready", "pre_done", "ln_ready", "sp_ready", "cum_done", "clip_ready", "exps_ready", "gl_ready",
                "att_done", "attm_ready", "upd_done", "sb_ready", "oc_done", "sa_ready", "sq2_ready", "s4_ready",
                "r4_ready", "er_ready", "oc_ready", "msc_done", "nmx_ready", "mp_ready", "mpt_tp", "mpt_evac",
                "mo_done", "om_ready", "ot_tp", "ot_evac", "pool_done", "seT_done", "seT_ready", "supd_done",
                "supd_used", "sbd_ready", "chA", "chV", "w_done", "gla_out"))

        w_in = I["w_in"][0]
        W1_d = w_in.rearrange("(p j) n -> p j n", j=KD)
        x_p = I["x_prompt"][0]
        x_s = I["x_sample"][:, 0, :]
        mem_d = I["mem_prompt"][0]
        stage1 = ExitStack()
        block = stage1.enter_context(nc.Block())
        CIN = [0]
        PBANK = (2, 3, 4, 2, 3)
        ROWS_S, ROWS_P = 15, 6

        def wait_min(eng, s, v):
            if not (isinstance(v, int) and v <= 0):
                eng.wait_ge(s, v)

        @block.sync
        def _(sp_e):
            def load(dst, src, s=c_in):
                sp_e.dma_start(dst, src).then_inc(s, 16)
                if s is c_in:
                    CIN[0] += 16

            load(xt, mem_d[0:128, :], x_in)
            load(cst[:, :], C_d[:, 0:c_early])
            load(TT[0:8, 6, :], C_d[0:8, c_late:c_late + 1024])
            for g, n in ((g_mix, "norm_mix_g"), (g_ffn, "norm_ffn_g"), (g_mem, "norm_mem_g")):
                load(g[:, :], I[n][0].rearrange("(p j) -> p j", j=KD))
            load(wmem, I["w_mem_kv"][0].rearrange("(p j) n -> p j n", j=KD))
            for h in range(4):
                load(qn_gain[:, h * 64:(h + 1) * 64], I["nsa_qn_g"][0:1].broadcast_to([128, 64]))
                load(qn_gain[:, 256 + h * 64:256 + (h + 1) * 64], I["mem_qn_g"][0:1].broadcast_to([128, 64]))
            load(qn_gain[:, 512:576], I["nsa_kn_g"][0, 1:2].broadcast_to([128, 64]))
            load(qn_gain[:, 576:640], I["nsa_kn_g"][0, 2:3].broadcast_to([128, 64]))
            load(kn_cmp[:, :], I["nsa_kn_g"][0, 0:1].broadcast_to([128, 64]))
            load(kn_mem[:, :], I["mem_kn_g"][0:1].broadcast_to([128, 64]))
            load(g_gla[:, :], I["gla_norm_g"][0:1].broadcast_to([128, 64]))
            for n, (a, b) in enumerate((("nsa_pe_k", "nsa_phi_k"), ("nsa_pe_v", "nsa_phi_v"))):
                load(pe_kv[:, n, :], I[a][0])
                load(phi_kv[:, n, :], I[b][0])
            load(gate_up[:, :], I["gla_gate_up"][0])
            load(gate_b[:, :], I["gla_gate_b"][0:1])
            load(tab[0:32, :], I["rel_bias"])
            load(S0s[:, :, :], I["state_gla"][0].rearrange("b h k v -> (h k) b v"))
            load(W1, W1_d[:, :, 0:NP1], w_in_s)
            load(O[19][0, :, 0:511, :], I["cache_nsa_win_k"][0, :, 1:512, :], rows_out)
            load(O[20][0, :, 0:511, :], I["cache_nsa_win_v"][0, :, 1:512, :], hT_out)

            sp_e.wait_ge(xn_ready, 1)
            load(xt, mem_d[128:256, :], x_in)
            for u in range(2):
                sp_e.wait_ge(mk_ready, u + 1)
                load(O[11][0, 0, u * 128:(u + 1) * 128].rearrange("t h d -> t (h d)"), QN[:, 0:256], kv_out)
                load(O[12][0, 0, u * 128:(u + 1) * 128].rearrange("t h d -> t (h d)"), mv[:, u, :], kv_out)
            sp_e.wait_ge(xn_ready, 2)
            load(xt[0:8, :], x_s, x_in)
            sp_e.wait_ge(xn_ready, 3)
            load(xt, x_p[0:128, :], x_in)
            sp_e.wait_ge(p_ready, NCH)
            for c, w, o in ((SBK, 256, 13), (SBV, 256, 14)):
                load(O[o][0, :, 0].rearrange("t h d -> t (h d)"), P[0:8, c:c + w], rows_out)
            for c, o in ((KC, 15), (VC, 16), (VS, 18)):
                load(O[o][0, :, 0, :], P[0:8, c:c + 64], rows_out)
            load(O[20][0, :, 511, :], P[0:8, VW:VW + 64], rows_out)
            load(srow_d[:, RQA:RQA + 256], P[0:8, SBQ:SBQ + 256], rows_out)
            load(srow_d[:, RVS:RVS + 64], P[0:8, VS:VS + 64], rows_out)
            load(srow_d[:, RVW:RVW + 64], P[0:8, VW:VW + 64], rows_out)
            load(srow_d[:, RG:RG + 12], P[0:8, NG:NG + 12], rows_out)
            sp_e.wait_ge(qn_ready, 1)
            load(O[17][0, :, 0, :], QN[0:8, QNS:QNS + 64], rows_out)
            load(O[19][0, :, 511, :], QN[0:8, QNW:QNW + 64], rows_out)
            load(srow_d[:, RQB:RQB + 512], QN[0:8, 0:512], rows_out)
            load(srow_d[:, RKS:RKS + 64], QN[0:8, QNS:QNS + 64], rows_out)
            load(srow_d[:, RKW:RKW + 64], QN[0:8, QNW:QNW + 64], rows_out)

            def tile(i, last=False):
                rows = bass.ds(i * 128, 128)
                sp_e.wait_ge(hts_ready, i + 4)
                sp_e.dma_start(hT_d[:, :, rows], hTs).then_inc(hT_out, 16)
                if not last:
                    sp_e.wait_ge(xn_ready, i + 4)
                    sp_e.dma_start(xt, x_p[bass.ds(i * 128 + 128, 128), :]).then_inc(x_in, 16)
                sp_e.wait_ge(p_ready, i * NCH + 2 * NCH)
                for c, o in ((SBK, 2), (SBV, 3)):
                    sp_e.dma_start(O[o][0, 0, rows].rearrange("t h d -> t (h d)"),
                                   P[:, c:c + 256]).then_inc(rows_out, 16)
                for c, o in ((KC, 4), (VC, 5), (VS, 7)):
                    sp_e.dma_start(O[o][0, 0, rows, :], P[:, c:c + 64]).then_inc(rows_out, 16)
                sp_e.wait_ge(qn_ready, i + 2)
                sp_e.dma_start(O[6][0, 0, rows, :], QN[:, QNS:QNS + 64]).then_inc(rows_out, 16)

            sp_e.wait_ge(sbd_ready, 8)
            load(O[21][0].rearrange("b h k v -> (h k) b v"), S1s, gla_out)
            with sp_e.Fori(0, NT - 1) as i:
                tile(i)
            tile(NT - 1, last=True)
            sp_e.wait_ge(pool_done, NT + 1)
            sp_e.dma_start(O[8][0, 0].rearrange("(j p) d -> p j d", p=128), KWt[:, 4:8, :]).then_inc(rows_out, 16)
            sp_e.dma_start(O[9][0, 0].rearrange("(j p) d -> p j d", p=128), VWt[:, 4:8, :]).then_inc(rows_out, 16)
            sp_e.wait_ge(sa_ready, NT + 1)
            for h in range(4):
                sp_e.dma_start(O[10][0, 0, h], Sa[32 * h:32 * h + 32, 64 * h:64 * h + 64]).then_inc(gla_out, 16)
            sp_e.wait_ge(gla_out, 80)
            sp_e.wait_ge(hT_out, 16 * NT + 16)
            sp_e.wait_ge(kv_out, 64)
            sp_e.wait_ge(rows_out, 16 * (1 + ROWS_S + ROWS_P * NT + 2))
            sp_e.wait_ge(ot_evac, NT + 1)

        @block.gpsimd
        def _(pool):
            def tile(i):
                for dst, src, w in ((VA, SBV, 256), (VSt, VS, 64), (VWt, VW, 64), (NGt, NG, 12)):
                    if dst is VA:
                        pool.wait_ge(p_ready, i * NCH + 2 * NCH)
                    nc.gpsimd.tensor_copy(dst[:, bass.ds(i, 1), :], P[:, None, src:src + w])
                pool.wait_ge(qn_ready, i + 2)
                nc.gpsimd.tensor_copy(KWt[:, bass.ds(i, 1), :], QN[:, None, QNW:QNW + 64]).then_inc(pool_done, 1)

            nc.gpsimd.memset(NGt[:, :, :], 0.0).then_inc(pool_done, 1)
            pool.wait_ge(pool_done, 1)
            with pool.Fori(0, NT) as i:
                tile(i)

        @block.scalar
        def _(act):
            chain = Chain(act, chA)
            A = nc.scalar.activation

            def norm(k, R):
                act.wait_ge(x_in, 16 * (k + 1))
                chain(A(sqx[0:R, :], xt[0:R, :], ACT.Square, accum_out=ssq[0:R, :]))
                chain(A(lnx[0:R, :], ssq[0:R, :], ACT.Ln, bias=eps[0:R, :], scale=1.0 / D))
                wait_min(act, xn_ready, k)
                A(rstd[0:R, :], lnx[0:R, :], ACT.Exp, scale=-0.5).then_inc(rstd_ready, 1)

            def head_rstd(k, R, n):
                act.wait_ge(ss_ready, k + 1)
                chain(A(r10[0:R, 0:n], ss[0:R, 0:n], ACT.Ln, bias=eps[0:R, :], scale=1.0 / 64))
                A(r10[0:R, 0:n], r10[0:R, 0:n], ACT.Exp, scale=-0.5).then_inc(r_ready, 1)

            act.wait_ge(const_ready, 1)
            nc.scalar.preload_act_table_set("natural_log_exp_and_others")
            for u in range(2):
                norm(u, 128)
                act.wait_ge(kv_done, u + 1)
                if u:
                    act.wait_ge(kv_tp, 1)
                    act.wait_ge(mk_ready, 1)
                chain(A(P[:, 0:512], bank(2), ACT.Copy))
                chain(A(mv[:, u, :], P[:, 256:512], ACT.Copy))
                A(sq[:, 0:256], P[:, 0:256], ACT.Square).then_inc(sq_ready, 1)
                head_rstd(u, 128, 4)
                act.wait_ge(kv_tp, u + 1)
                A(mkT[:, :, u * 128:(u + 1) * 128], bank(7)[:, 0:256].rearrange("p (a b) -> p a b", a=2),
                  ACT.Copy).then_inc(kv_p, 1)

            def evacuate(i, R, cs):
                m = 0 if i is None else i + 1
                if i is not None and 0 in cs:
                    act.wait_ge(oc_done, m)
                    act.wait_ge(pool_done, i + 1)
                    act.wait_ge(rows_out, 16 * (1 + ROWS_S) + i * (16 * ROWS_P))
                for c in cs:
                    act.wait_ge(proj_done, m * NCH + (c + 1))
                    A(P[0:R, c * CH:(c + 1) * CH], bank(PBANK[c])[0:R, 0:CH], ACT.Copy).then_inc(p_ready, 1)

            def tile(i, R, ahead=False):
                k, m = (2, 0) if i is None else (i + 3, i + 1)
                nx = 0 if i is None else i + 1
                if ahead:
                    norm(k + 1, 128)
                act.wait_ge(p_ready, m * NCH + NCH)
                A(sq[0:R, 0:256], P[0:R, NQ:NQ + 256], ACT.Square)
                A(sq[0:R, 256:512], P[0:R, MQ:MQ + 256], ACT.Square)
                A(sq[0:R, 512:576], P[0:R, KS:KS + 64], ACT.Square)
                A(sq[0:R, 576:640], P[0:R, KW:KW + 64], ACT.Square).then_inc(sq_ready, 1)
                A(er[0:R, :], P[0:R, GR:GR + 256], ACT.Exp, scale=-1.0).then_inc(er_ready, 1)
                act.wait_ge(aT_tp, m + 1)
                A(aT[:, 0:R], bank(6)[0:16, 0:R], ACT.Copy).then_inc(aT_ready, 1)
                head_rstd(k, R, 10)
                act.wait_ge(pre_done, m + 1)
                pre = bank(6)[0:R, 128:256]
                chain(A(pab[0:R, :], pre, ACT.Abs))
                chain(A(pab[0:R, :], pab[0:R, :], ACT.Exp, scale=-1.0))
                A(pln[0:R, :], pab[0:R, :], ACT.Ln, bias=one[0:R, :]).then_inc(ln_ready, 1)
                if i is not None:
                    cols = bass.ds(i * 128, 128)
                    act.wait_ge(qn_tp, m + 1)
                    A(TT[:, 0:8, cols], bank(0, 2).rearrange("p (a b) -> p a b", a=8), ACT.Copy)
                    A(mq[0:64, :, 0, :], bank(7)[0:64, 0:256].rearrange("p (a b) -> p a b", a=2), ACT.Copy)
                    A(mq[64:128, :, 1, :], bank(7)[64:128, 0:256].rearrange("p (a b) -> p a b", a=2),
                      ACT.Copy).then_inc(tt_evac, 1)
                else:
                    act.wait_ge(qn_tp, m + 1)
                A(gqT[:, 0:R], bank(7)[:, 256:256 + R], ACT.Copy, scale=32 ** -0.5)
                A(gkT[:, 0:R], bank(7)[:, 384:384 + R], ACT.Copy).then_inc(slots_ready, 1)
                if i is not None:
                    act.wait_ge(km_done, i + 1)
                    A(kmT[:, :, bass.ds(i * 2, 2)], bank(4)[0:64, 0:4].rearrange("p (a b) -> p a b", a=2),
                      ACT.Copy).then_inc(km_evac, 1)
                    act.wait_ge(clip_ready, i + 1)
                    A(Emid[:, :], cclip[:, :], ACT.Exp)
                    A(Eimid[:, :], cclip[:, :], ACT.Exp, scale=-1.0)
                    A(Ecum[:, :], bank(7)[:, 128:256], ACT.Exp)
                    A(Esuf[:, :], bank(7)[:, 256:384], ACT.Exp).then_inc(exps_ready, 1)
                else:
                    act.wait_ge(seT_done, 1)
                    A(Ecum[:, 0:R], bank(7)[:, 0:R], ACT.Exp, scale=-1.0 / 16).then_inc(seT_ready, 1)
                act.wait_ge(oc_done, m + 1)
                A(sq2[0:R, :], bank(6)[0:R, 0:256], ACT.Square).then_inc(sq2_ready, 1)
                if ahead:
                    evacuate(nx, 128, (0, 1))
                act.wait_ge(s4_ready, m + 1)
                chain(A(l4[0:R, :], s4[0:R, :], ACT.Ln, bias=eps[0:R, :], scale=1.0 / 64))
                A(r4[0:R, :], l4[0:R, :], ACT.Exp, scale=-0.5).then_inc(r4_ready, 1)
                if ahead:
                    evacuate(nx, 128, (2,))
                if i is not None:
                    act.wait_ge(nmx_ready, i + 1)
                    for h in range(4):
                        last = A(mp[:, h, :], bank(5, 2)[:, h * 256:(h + 1) * 256], ACT.Exp, bias=nmx[:, h:h + 1],
                                 accum_out=lm[:, h:h + 1])
                    last.then_inc(mp_ready, 1)
                    if ahead:
                        evacuate(nx, 128, (3,))
                    act.wait_ge(mpt_tp, i + 1)
                    A(mpT[:, :, :], bank(0, 2).rearrange("p (a b) -> p a b", a=8), ACT.Copy).then_inc(mpt_evac, 1)
                    act.wait_ge(ot_tp, m + 1)
                    A(OT[:, 4:8, cols], bank(7).rearrange("p (a b) -> p a b", a=4), ACT.Copy).then_inc(ot_evac, 1)
                    if ahead:
                        evacuate(nx, 128, (4,))
                else:
                    act.wait_ge(ot_tp, 1)
                    A(OT[:, 4:6, SEQ:NCOL], bank(7)[:, 0:256].rearrange("p (a b) -> p a b", a=2)[:, :, 0:8],
                      ACT.Copy).then_inc(ot_evac, 1)
                    evacuate(nx, 128, (3, 4))

            norm(2, NB)
            evacuate(None, NB, range(NCH))
            tile(None, NB, ahead=True)
            act.wait_ge(gla_out, 16)
            with act.Fori(0, NT - 1) as i:
                chain.enter(i, CHAIN_A1)
                tile(i, 128, ahead=True)
            chain.leave(NT - 1)
            tile(NT - 1, 128)

        @block.vector
        def _(dve):
            chain = Chain(dve, chV)
            V = nc.vector
            V.memset(eps[:, :], EPS)
            V.memset(mq[:, :, :, :], 0.0)
            V.memset(q1bd[:, :, :], 0.0)
            V.memset(q3[:, :, :], 0.0)
            V.memset(tab[32:33, :], NEG)
            chain(V.memset(one[:, :], 1.0))
            dve.wait_ge(c_in, CIN[0])
            V.tensor_scalar(qn_gain[:, 0:512], qn_gain[:, 0:512], 0.125, None, ALU.mult)
            V.memset(Sa[:, :], 0.0).then_inc(const_ready, 1)
            dve.wait_ge(const_ready, 1)

            def norm(k, R, gain):
                dve.wait_ge(rstd_ready, k + 1)
                wait_min(dve, xn_tp, k)
                V.tensor_scalar(xn[0:R, :], xt[0:R, :], rstd[0:R, :], None, ALU.mult).then_inc(xn_ready, 1)
                dve.wait_ge(xn_tp, k + 1)
                V.tensor_tensor(hTs[:, :, 0:R], bank(0, 2).rearrange("p (j t) -> p j t", j=KD)[:, :, 0:R],
                                gain[:, :, None].broadcast_to([128, KD, R]), ALU.mult).then_inc(hts_ready, 1)

            def groups(k, R, n):
                dve.wait_ge(sq_ready, k + 1)
                V.tensor_reduce(ss[0:R, 0:n], sq[0:R, 0:64 * n].rearrange("p (a b) -> p a b", b=64), AX.X,
                                ALU.add).then_inc(ss_ready, 1)
                dve.wait_ge(r_ready, k + 1)

            for u in range(2):
                norm(u, 128, g_mem)
                groups(u, 128, 4)
                if u:
                    dve.wait_ge(kv_out, 32)
                    dve.wait_ge(kv_tp, 1)
                chain(V.tensor_tensor(QN[:, 0:256].rearrange("p (a b) -> p a b", b=64),
                                      P[:, 0:256].rearrange("p (a b) -> p a b", b=64),
                                      r10[:, 0:4, None].broadcast_to([128, 4, 64]), ALU.mult))
                V.tensor_tensor(QN[:, 0:256].rearrange("p (a b) -> p a b", b=64),
                                QN[:, 0:256].rearrange("p (a b) -> p a b", b=64),
                                kn_mem[:, None, :].broadcast_to([128, 4, 64]), ALU.mult).then_inc(mk_ready, 1)

            def normed(i, R):
                if i is None:
                    dve.wait_ge(kv_done, 2)
                else:
                    dve.wait_ge(proj_done, (i + 1) * NCH)
                    dve.wait_ge(hT_out, i * 16 + 16)
                norm(2 if i is None else i + 3, R, g_mix)

            def tile(i, R, ahead=False):
                k, m = (2, 0) if i is None else (i + 3, i + 1)
                if i is None:
                    dve.wait_ge(hts_ready, 3)
                    V.tensor_copy(hT_s[:, :, :], hTs[:, :, 0:8])
                if ahead:
                    normed(0 if i is None else i + 1, 128)
                groups(k, R, 10)
                if i is None:
                    dve.wait_ge(kv_out, 64)
                    dve.wait_ge(kv_tp, 2)
                else:
                    dve.wait_ge(qn_tp, m)
                    dve.wait_ge(pool_done, i + 1)
                    dve.wait_ge(rows_out, 16 * (1 + ROWS_S) + i * (16 * ROWS_P))
                def part(dst, src, r, n):
                    return V.tensor_tensor(QN[0:R, dst:dst + 64 * n].rearrange("p (a b) -> p a b", b=64),
                                           P[0:R, src:src + 64 * n].rearrange("p (a b) -> p a b", b=64),
                                           r10[0:R, r:r + n, None].broadcast_to([R, n, 64]), ALU.mult)
                part(QNB, NQ, 0, 4)
                part(QNM, MQ, 4, 4)
                part(QNS, KS, 8, 1)
                chain(part(QNW, KW, 9, 1))
                V.tensor_tensor(QN[0:R, 0:512], QN[0:R, 0:512], qn_gain[0:R, 0:512], ALU.mult)
                chain(V.tensor_tensor(QN[0:R, 512:768].rearrange("p (a b) -> p a b", b=128)[:, :, 0:64],
                                QN[0:R, 512:768].rearrange("p (a b) -> p a b", b=128)[:, :, 0:64],
                                qn_gain[0:R, 512:640].rearrange("p (a b) -> p a b", b=64), ALU.mult))
                V.tensor_copy(QN[0:R, 512:768].rearrange("p (a b) -> p a b", b=128)[:, :, 64:128],
                              QN[0:R, 512:768].rearrange("p (a b) -> p a b", b=128)[:, :, 0:64]).then_inc(qn_ready, 1)
                dve.wait_ge(ln_ready, m + 1)
                chain(V.tensor_scalar(sp[0:R, :], bank(6)[0:R, 128:256], -1.0, 0.0, ALU.mult, ALU.max))
                V.tensor_tensor(sp[0:R, :], sp[0:R, :], pln[0:R, :], ALU.add).then_inc(sp_ready, 1)
                dve.wait_ge(er_ready, m + 1)
                chain(V.tensor_scalar(sil[0:R, :], er[0:R, :], 1.0, None, ALU.add))
                chain(V.reciprocal(sil[0:R, :], sil[0:R, :]))
                chain(V.tensor_tensor(sil[0:R, :], sil[0:R, :], P[0:R, GR:GR + 256], ALU.mult))
                chain(V.tensor_tensor(sil[0:R, :].rearrange("p (a b) -> p a b", b=64),
                                      sil[0:R, :].rearrange("p (a b) -> p a b", b=64),
                                      g_gla[0:R, None, :].broadcast_to([R, 4, 64]), ALU.mult))
                if i is not None:
                    dve.wait_ge(cum_done, i + 1)
                    V.tensor_scalar(cclip[:, :], bank(7)[:, 0:128], -40.0, 40.0, ALU.max, ALU.min).then_inc(clip_ready, 1)
                    dve.wait_ge(slots_ready, m + 1)
                    dve.wait_ge(exps_ready, i + 1)
                    for h in range(4):
                        r = slice(32 * h, 32 * h + 32)
                        V.tensor_tensor(q1bd[r, h, :], gqT[r, :], Emid[r, :], ALU.mult)
                    V.tensor_tensor(k1T[:, :], gkT[:, :], Eimid[:, :], ALU.mult)
                    for c in range(2):
                        V.tensor_tensor(q3[:, c, c * 64:c * 64 + 64], gqT[:, c * 64:c * 64 + 64],
                                        Ecum[:, c * 64:c * 64 + 64], ALU.mult)
                        last = V.scalar_tensor_tensor(k4[:, c, :], P[:, GK:GK + 128], K("hcol")[:, c:c + 1],
                                                      Esuf[:, :], ALU.mult, ALU.mult)
                    last.then_inc(gl_ready, 1)
                    dve.wait_ge(att_done, i + 1)
                    chain(V.tensor_scalar(attm[:, :, :].rearrange("p a b -> p (a b)"), bank(5), -1e30, 1e30, ALU.max, ALU.min))
                    V.tensor_tensor(attm[:, :, :], attm[:, :, :], K("glamask")[:, None, :].broadcast_to([128, 4, 128]),
                                    ALU.mult).then_inc(attm_ready, 1)
                    dve.wait_ge(upd_done, i + 1)
                    chain(V.tensor_tensor(updm[:, :, :], bank(5).rearrange("p (a b) -> p a b", a=2),
                                          K("bd256")[:, None, :].broadcast_to([128, 2, 256]), ALU.mult))
                    V.scalar_tensor_tensor(Sb[:, :], Sa[:, :], Ecum[:, 63:64], updm[:, 0, :], ALU.mult,
                                           ALU.add).then_inc(sb_ready, 1)
                    dve.wait_ge(sb_ready, i + 1)
                    dve.wait_ge(oc_done, m + 1)
                    V.scalar_tensor_tensor(Sa[:, :], Sb[:, :], Ecum[:, 127:128], updm[:, 1, :], ALU.mult,
                                           ALU.add).then_inc(sa_ready, 1)
                else:
                    dve.wait_ge(slots_ready, 1)
                    dve.wait_ge(seT_ready, 1)
                    V.tensor_tensor(qTm[:, :, :], gqT[:, None, 0:8].broadcast_to([128, 8, 8]),
                                    K("eye88").rearrange("p (a b) -> p a b", a=8), ALU.mult)
                    V.tensor_tensor(km8[:, :, :], P[0:8, None, GK:GK + 128].broadcast_to([8, 8, 128]),
                                    oh8, ALU.mult).then_inc(gl_ready, 1)
                    for b in range(NB):
                        dve.wait_ge(supd_done, b + 1)
                        chain(V.tensor_tensor(updm[:, 0, :], bank(5)[:, 0:256], K("bd256"), ALU.mult))
                        chain(V.tensor_reduce(updm[:, 1, 0:64], updm[:, 0, :].rearrange("p (h v) -> p v h", h=4),
                                              AX.X, ALU.add))
                        V.scalar_tensor_tensor(S1s[:, b, :], S0s[:, b, :], Ecum[:, b:b + 1], updm[:, 1, 0:64],
                                               ALU.mult, ALU.add).then_inc(supd_used, 1)
                        dve.wait_ge(supd_used, b + 1)
                        if b:
                            dve.wait_ge(seT_done, b + 1)
                        V.tensor_tensor(Sb[:, :].rearrange("p (h v) -> p h v", h=4),
                                        S1s[:, b:b + 1, :].broadcast_to([128, 4, 64]),
                                        K("bd256").rearrange("p (h v) -> p h v", h=4), ALU.mult).then_inc(sbd_ready, 1)
                    dve.wait_ge(oc_done, 1)
                    V.memset(updm[:, 0, 0:1], 0.0).then_inc(sa_ready, 1)
                dve.wait_ge(sq2_ready, m + 1)
                V.tensor_reduce(s4[0:R, :], sq2[0:R, :].rearrange("p (a b) -> p a b", b=64), AX.X,
                                ALU.add).then_inc(s4_ready, 1)
                dve.wait_ge(r4_ready, m + 1)
                chain(V.tensor_tensor(oCM[0:R, 0:256].rearrange("p (a b) -> p a b", b=64),
                                      bank(6)[0:R, 0:256].rearrange("p (a b) -> p a b", b=64),
                                      r4[0:R, :, None].broadcast_to([R, 4, 64]), ALU.mult))
                V.tensor_tensor(oCM[0:R, 0:256], oCM[0:R, 0:256], sil[0:R, :], ALU.mult).then_inc(oc_ready, 1)
                if i is not None:
                    dve.wait_ge(msc_done, i + 1)
                    V.tensor_reduce(nmx[:, :], bank(5, 2).rearrange("p (a b) -> p a b", a=4), AX.X, ALU.max,
                                    negate=True).then_inc(nmx_ready, 1)
                    dve.wait_ge(mp_ready, i + 1)
                    chain(V.reciprocal(rlm[:, :], lm[:, :]))
                    dve.wait_ge(mo_done, i + 1)
                    V.tensor_tensor(oCM[:, 256:512].rearrange("p (a b) -> p a b", b=64),
                                    bank(7)[:, 0:256].rearrange("p (a b) -> p a b", b=64),
                                    rlm[:, :, None].broadcast_to([128, 4, 64]), ALU.mult).then_inc(om_ready, 1)

            normed(None, NB)
            tile(None, NB, ahead=True)
            with dve.Fori(0, NT - 1) as i:
                chain.enter(i, CHAIN_V1)
                tile(i, 128, ahead=True)
            chain.leave(NT - 1)
            tile(NT - 1, 128)

        @block.tensor
        def _(pe):
            MM, TR = nc.tensor.matmul, nc.tensor.transpose
            ident = K("ident")

            def transposes(k, R):
                pe.wait_ge(xn_ready, k + 1)
                for j in range(KD):
                    last = TR(bank(0, 2)[:, j * 128:j * 128 + R], xn[0:R, j:D:KD], ident[0:R, 0:R])
                last.then_inc(xn_tp, 1)

            pe.wait_ge(const_ready, 1)
            for u in range(2):
                transposes(u, 128)
                pe.wait_ge(hts_ready, u + 1)
                for j in range(KD):
                    last = MM(bank(2), hTs[:, j, :], wmem[:, j, :], start=(j == 0), stop=(j == KD - 1))
                last.then_inc(kv_done, 1)
                pe.wait_ge(mk_ready, u + 1)
                for a in range(2):
                    last = TR(bank(7)[:, a * 128:(a + 1) * 128], QN[:, a * 128:(a + 1) * 128], ident)
                last.then_inc(kv_tp, 1)
                pe.wait_ge(kv_p, u + 1)
            pe.wait_ge(w_in_s, 16)

            def project(i, R, *halves):
                k, m = (2, 0) if i is None else (i + 3, i + 1)
                for h in halves:
                    c = h // 2
                    if h == 0:
                        pe.wait_ge(hts_ready, k + 1)
                    if h == 4 and i is not None:
                        wait_min(pe, km_evac, i)
                    if h in (6, 8):
                        pe.wait_ge(p_ready, m * NCH + (c - 2))
                    for j in range(4 * (h % 2), 4 * (h % 2) + 4):
                        last = MM(bank(PBANK[c])[0:R, 0:CH], hTs[:, j, 0:R], W1[:, j, c * CH:(c + 1) * CH],
                                  start=(j == 0), stop=(j == KD - 1))
                    if h % 2:
                        last.then_inc(proj_done, 1)

            def tile(i, R, ahead=False):
                k, m = (2, 0) if i is None else (i + 3, i + 1)

                def fill(*halves):
                    if ahead:
                        project(0 if i is None else i + 1, 128, *halves)

                pe.wait_ge(p_ready, m * NCH + NCH)
                TR(bank(6)[0:16, 0:R], P[0:R, GA:GA + 16], ident[0:R, 0:R]).then_inc(aT_tp, 1)
                if i is not None:
                    for n, c in enumerate((KC, VC)):
                        last = MM(bank(4)[0:64, 2 * n:2 * n + 2], P[:, c:c + 64], K("ind2"), start=True, stop=True)
                    last.then_inc(km_done, 1)
                if ahead:
                    transposes(k + 1, 128)
                pe.wait_ge(aT_ready, m + 1)
                MM(bank(6)[0:R, 128:256], aT[:, 0:R], gate_up[:, :], start=True, stop=False)
                MM(bank(6)[0:R, 128:256], K("ones", 1)[:, 0:R], gate_b[:, :], start=False, stop=True).then_inc(pre_done, 1)
                fill(0, 1)
                pe.wait_ge(qn_ready, m + 1)
                if i is not None:
                    pe.wait_ge(ot_evac, m)
                    for a, (src, c) in enumerate(((P, SBQ), (P, SBQ + 128), (P, SBK), (P, SBK + 128), (QN, 0),
                                                  (QN, 128), (QN, QNS), (QN, QNW))):
                        TR(bank(0, 2)[:, a * 128:(a + 1) * 128], src[:, c:c + 128], ident)
                    for a in range(2):
                        TR(bank(7)[:, a * 128:(a + 1) * 128], QN[:, QNM + a * 128:QNM + (a + 1) * 128], ident)
                TR(bank(7)[:, 256:256 + R], P[0:R, GQ:GQ + 128], ident[0:R, 0:R])
                TR(bank(7)[:, 384:384 + R], P[0:R, GK:GK + 128], ident[0:R, 0:R]).then_inc(qn_tp, 1)
                fill(2)
                pe.wait_ge(sp_ready, m + 1)
                pe.wait_ge(slots_ready, m + 1)
                if i is not None:
                    MM(bank(7)[:, 0:128], sp[:, :], K("gm_mid"), start=True, stop=True)
                    MM(bank(7)[:, 128:256], sp[:, :], K("gm_cum"), start=True, stop=True)
                    MM(bank(7)[:, 256:384], K("gm_suf"), sp[:, :], start=True, stop=True).then_inc(cum_done, 1)
                    fill(3, 4)
                    pe.wait_ge(gl_ready, m + 1)
                    MM(bank(5), k1T[:, :], q1bd[:, :, :].rearrange("p a b -> p (a b)"), start=True,
                       stop=True).then_inc(att_done, 1)
                    fill(5)
                    pe.wait_ge(attm_ready, i + 1)
                    for c in range(2):
                        last = MM(bank(5)[:, c * 256:(c + 1) * 256], k4[:, c, :], P[:, GV:GV + 256], start=True, stop=True)
                    last.then_inc(upd_done, 1)
                    oc = bank(6)[:, 0:256]
                    pe.wait_ge(sa_ready, m)
                    MM(oc, q3[:, 0, :], Sa[:, :], start=True, stop=False, skip_group_check=True)
                    for h in range(4):
                        MM(oc[:, h * 64:(h + 1) * 64], attm[:, h, :], P[:, GV + h * 64:GV + (h + 1) * 64],
                           start=False, stop=False, skip_group_check=True)
                    pe.wait_ge(sb_ready, i + 1)
                    MM(oc, q3[:, 1, :], Sb[:, :], start=False, stop=True, skip_group_check=True).then_inc(oc_done, 1)
                    fill(6)
                    pe.wait_ge(oc_ready, m + 1)
                    for h in range(4):
                        last = MM(bank(5, 2)[:, h * 256:(h + 1) * 256], mq[:, h // 2, h % 2, :], mkT[:, h // 2, :],
                                  start=True, stop=True)
                    last.then_inc(msc_done, 1)
                    fill(7)
                    pe.wait_ge(mp_ready, i + 1)
                    for a in range(8):
                        last = TR(bank(0, 2)[:, a * 128:(a + 1) * 128], mp[:, a // 2, (a % 2) * 128:(a % 2 + 1) * 128], ident)
                    last.then_inc(mpt_tp, 1)
                    fill(8)
                    pe.wait_ge(mpt_evac, i + 1)
                    for h in range(4):
                        for u in range(2):
                            last = MM(bank(7)[:, h * 64:(h + 1) * 64], mpT[:, 2 * h + u, :],
                                      mv[:, u, h * 64:(h + 1) * 64], start=(u == 0), stop=(u == 1))
                    last.then_inc(mo_done, 1)
                    fill(9)
                    pe.wait_ge(om_ready, i + 1)
                    for a in range(4):
                        last = TR(bank(7)[:, a * 128:(a + 1) * 128], oCM[:, a * 128:(a + 1) * 128], ident)
                    last.then_inc(ot_tp, 1)
                else:
                    TR(bank(7)[:, 0:R], sp[0:R, :], ident[0:R, 0:R]).then_inc(seT_done, 1)
                    pe.wait_ge(gl_ready, 1)
                    for b in range(NB):
                        if b:
                            pe.wait_ge(supd_used, b)
                        MM(bank(5)[:, 0:256], km8[:, b, :], P[0:8, GV:GV + 256], start=True, stop=True).then_inc(supd_done, 1)
                        pe.wait_ge(sbd_ready, b + 1)
                        last = MM(bank(6)[0:8, 0:256], qTm[:, b, :], Sb[:, :], start=(b == 0), stop=(b == NB - 1))
                        if b < NB - 1:
                            last.then_inc(seT_done, 1)
                        if b < 3:
                            fill(b + 3)
                    last.then_inc(oc_done, 1)
                    fill(6, 7)
                    pe.wait_ge(oc_ready, 1)
                    for a in range(2):
                        last = TR(bank(7)[:, a * 128:a * 128 + R], oCM[0:R, a * 128:(a + 1) * 128], ident[0:R, 0:R])
                    last.then_inc(ot_tp, 1)
                    fill(8, 9)

            transposes(2, NB)
            project(None, NB, *range(2 * NCH))
            tile(None, NB, ahead=True)
            with pe.Fori(0, NT - 1) as i:
                tile(i, 128, ahead=True)
            tile(NT - 1, 128)

        stage1.close()
        stage_over()

        acur = [late_w]

        def big(*dims, r=128):
            n = int(np.prod(dims))
            v = arena[0:r, acur[0]:acur[0] + n]
            acur[0] += n
            assert acur[0] <= KD * NP1, acur[0]
            if len(dims) == 2:
                return v.rearrange("p (a b) -> p a b", a=dims[0])
            if len(dims) == 3:
                return v.rearrange("p (a b c) -> p a b c", a=dims[0], b=dims[1])
            return v

        bsel = big(NSEL, 4)
        bwin = big(NWIN, 4)
        bcmp = big(64)
        keep = acur[0]
        BS = big(4, SEQ)
        WB = big(4, 640)
        bc = big(30, 4)
        vc01 = big(30, 4)
        kcT = big(16)
        kcr = big(128, r=16)
        kcs = big(64, r=16)
        vcbd = big(256, r=64)
        kn1, kn2 = big(1, r=16), big(1, r=16)
        kn2j = big(64, r=16)
        ind_col = K("ind2", 64)[:, 0:1]
        after_bias = acur[0]
        OH = big(OHC + 128 * (NSEL + NWIN) + 64 + NEAR, r=33)
        near = big(4, NEAR)
        acur[0] = after_bias
        QAbd = [big(2, 2, 128) for _ in range(2)]
        QBbd = [big(2, 2, 128) for _ in range(2)]
        zab = [big(512) for _ in range(2)]
        spu = [big(512) for _ in range(2)]
        Rsum = [big(512) for _ in range(3)]
        au = [big(512) for _ in range(2)]
        oAs = big(256)
        cursor[0] = 0
        sB = [tmp(1024) for _ in range(2)]
        pB = [tmp(1024) for _ in range(2)]
        pTB = [tmp(1024) for _ in range(2)]
        nmB = [tmp(1) for _ in range(2)]
        lB = tmp(2, 12)
        cB = tmp(2, 12)
        lcm, pcm, pcT = tmp(4, 16), tmp(4, 16), tmp(128, r=64)
        nmc = tmp(4)
        gB = tmp(NT, 12)
        oBs, oB2 = tmp(256), tmp(256)

        names = ("c2_in", "oh_in", "near_ps", "near_ready", "skew_out", "skew_in", "bias_ps", "bias_used", "bias_ready", "pm_done", "pm_ready", "km2_ready", "kc_done",
                 "kc_sq", "kc_r", "kc_n", "kc_tp", "kc_ready", "bd_zero", "bdA", "bdB", "z_done", "l_ready", "spA_ready",
                 "tri_done", "a_ready", "R_ready", "av_done", "oAs_ready", "oA_tp", "oA_evac", "sc_done",
                 "s_ready", "p_ready2", "pt_tp", "pt_evac", "o_done", "gB_e", "gB_ready", "lc_done", "lc_ready",
                 "pc_exp", "pc_ready", "pc_tp", "pc_evac", "oc2_done", "oB_ready", "oB_tp", "oB_evac", "ch2A", "ch2V",
                 "ch2P")
        S2 = {n: sem(n) for n in names}
        units = [(t, kb) for t in range(NT) for kb in range(t, -1, -1)]
        jobs = [(t, h, kind) for t in range(NT) for kind in (0, 1) for h in range(4)]

        zbank = lambda u: bank((0, 1, 5)[u % 3])

        def span(t, kind):
            n = t + 1 if kind == 0 else min(t + 1, 5)
            return t + 1 - n, n

        stage2 = ExitStack()
        block = stage2.enter_context(nc.Block())

        @block.sync
        def _(sy):
            sy.dma_start(late, C_d[:, c_early:c_late]).then_inc(S2["c2_in"], 16)
            sy.dma_start(OH[:, :], OH_d).then_inc(S2["oh_in"], 16)
            sy.wait_ge(S2["near_ready"], 1)
            sy.dma_start(skew_d.ap(), near).then_inc(S2["skew_out"], 16)
            sy.wait_ge(S2["skew_out"], 16)
            sy.dma_start(BS[:, :, 768:1024], bass.AP(skew_d, 127, [[4 * NEAR - 1, 128], [NEAR, 4], [1, 256]]))\
              .then_inc(S2["skew_in"], 16)

        @block.gpsimd
        def _(pool):
            G = nc.gpsimd
            pool.wait_ge(S2["bias_ready"], 1)
            for b in QAbd + QBbd:
                last = G.memset(b[:, :, :, :], 0.0)
            last.then_inc(S2["bd_zero"], 1)
            pool.wait_ge(S2["bd_zero"], 1)
            for t in range(NT):
                cols = slice(t * 128, t * 128 + 128)
                if t >= 2:
                    pool.wait_ge(S2["z_done"], sum(1 for u in units if u[0] <= t - 2))
                for a in range(2):
                    for hh in range(2):
                        r = slice(64 * hh, 64 * hh + 64)
                        last = G.tensor_scalar(QAbd[t % 2][r, a, hh, :], TT[r, a, cols], 0.125, None, ALU.mult)
                last.then_inc(S2["bdA"], 1)
            for t in range(NT):
                cols = slice(t * 128, t * 128 + 128)
                if t >= 2:
                    pool.wait_ge(S2["sc_done"], 8 * (t - 1))
                    pool.wait_ge(S2["lc_done"], t - 1)
                for a in range(2):
                    for hh in range(2):
                        r = slice(64 * hh, 64 * hh + 64)
                        last = G.tensor_copy(QBbd[t % 2][r, a, hh, :], TT[r, 4 + a, cols])
                last.then_inc(S2["bdB"], 1)

        @block.tensor
        def _(pe):
            MM, TR = nc.tensor.matmul, nc.tensor.transpose
            ident = K("ident")
            pe.wait_ge(S2["oh_in"], 16)
            o = OHC + 128 * (NSEL + NWIN) + 64
            for h in range(4):
                last = MM(bank(h)[:, 0:NEAR], tab[:, h:h + 1].broadcast_to([33, 128]), OH[:, o:o + NEAR], start=True, stop=True)
            last.then_inc(S2["near_ps"], 1)
            for j in range(30):
                MM(bank(4)[:, 4 * j:4 * j + 4], OH[:, 1856 - 64 * j:1984 - 64 * j], tab[:, :], start=True, stop=True)
            for r in range(NSEL + NWIN):
                o = OHC + 128 * r
                MM(bank(4)[:, 120 + 4 * r:124 + 4 * r], OH[:, o:o + 128], tab[:, :], start=True, stop=True)
            o = OHC + 128 * (NSEL + NWIN)
            MM(bank(5)[0:4, 64:128], tab[:, :], OH[:, o:o + 64], start=True, stop=True)
            for n in range(2):
                last = MM(bank(5)[0:64, n:n + 1], pe_kv[:, n, :], ind_col, start=True, stop=True)
            last.then_inc(S2["bias_ps"], 1)
            pe.wait_ge(S2["km2_ready"], 1)
            for n in range(2):
                last = MM(bank(6)[0:16, 64 * n:64 * n + 64], kmT[:, n, :], phi_kv[:, n, :], start=True, stop=True)
            last.then_inc(S2["kc_done"], 1)
            pe.wait_ge(S2["kc_n"], 1)
            TR(bank(7)[:, 0:16], kcr[:, :], ident[0:16, 0:16])
            MM(bank(7)[0:64, 64:128], K("rep16", 16), kcs[:, :], start=True, stop=True).then_inc(S2["kc_tp"], 1)
            pe.wait_ge(S2["kc_ready"], 1)

            for x in range(len(units) + 3):
                u = x - 1
                if x < len(units):
                    t, kb = units[x]
                    z = zbank(x)
                    pe.wait_ge(S2["bdA"], t + 1)
                    if x >= 3:
                        pe.wait_ge(S2["a_ready"], x - 2)
                    for a in range(2):
                        last = MM(z[:, a * 256:a * 256 + 256], TT[:, 2 + a, kb * 128:kb * 128 + 128],
                                  QAbd[t % 2][:, a, :, :].rearrange("p a b -> p (a b)"), start=(a == 0), stop=False,
                                  skip_group_check=True)
                    if kb == t:
                        last = MM(z.rearrange("p (a b) -> p a b", a=4), ident, K("causalneg")[:, None, :].broadcast_to([128, 4, 128]),
                                  start=False, stop=False, skip_group_check=True)
                    last.then_inc(S2["z_done"], 1)
                v = u - 1
                if 0 <= v < len(units):
                    t, kb = units[v]
                    pe.wait_ge(S2["spA_ready"], v + 1)
                    last = MM(zbank(v), K("negtri"), spu[v % 2], start=False, stop=True, skip_group_check=True)
                    if kb < t:
                        pe.wait_ge(S2["R_ready"], v)
                        last = MM(zbank(v), K("negones"), Rsum[(v - 1) % 3], start=False, stop=True,
                                  skip_group_check=True)
                    last.then_inc(S2["tri_done"], 1)
                w = u - 2
                if 0 <= w:
                    t, kb = units[w]
                    pe.wait_ge(S2["a_ready"], w + 1)
                    if kb == t and t >= 2:
                        pe.wait_ge(S2["oAs_ready"], t - 1)
                    for h in range(4):
                        last = MM(bank(2 + t % 2)[:, h * 64:h * 64 + 64], au[w % 2][:, h * 128:h * 128 + 128],
                                  VA[:, kb, h * 64:h * 64 + 64], start=(kb == t and h == 0), stop=(kb == 0),
                                  skip_group_check=True)
                    last.then_inc(S2["av_done"], 1)
                    if kb == 0:
                        pe.wait_ge(S2["oAs_ready"], t + 1)
                        if t:
                            pe.wait_ge(S2["oA_evac"], t)
                        for a in range(2):
                            last = TR(bank(4)[:, a * 128:a * 128 + 128], oAs[:, a * 128:a * 128 + 128], ident)
                        last.then_inc(S2["oA_tp"], 1)

            pe.wait_ge(S2["oA_evac"], NT)
            for j in range(len(jobs) + 3):
                if j < len(jobs):
                    t, h, kind = jobs[j]
                    k0, n = span(t, kind)
                    pe.wait_ge(S2["bdB"], t + 1)
                    if j >= 2:
                        pe.wait_ge(S2["s_ready"], j - 1)
                    for c in range(0, n * 128, 512):
                        w = min(512, n * 128 - c)
                        last = MM(bank(2 * (j % 2), 2)[:, c:c + w], QBbd[t % 2][:, h // 2, h % 2, :],
                                  TT[:, 6 + kind, k0 * 128 + c:k0 * 128 + c + w], start=True, stop=True)
                    last.then_inc(S2["sc_done"], 1)
                v = j - 2
                if 0 <= v < len(jobs):
                    t, h, kind = jobs[v]
                    k0, n = span(t, kind)
                    pe.wait_ge(S2["p_ready2"], v + 1)
                    if v:
                        pe.wait_ge(S2["pt_evac"], v)
                    for b in range(n):
                        last = TR(bank(4, 2)[:, b * 128:b * 128 + 128], pB[v % 2][:, b * 128:b * 128 + 128], ident)
                    last.then_inc(S2["pt_tp"], 1)
                w = j - 3
                if 0 <= w < len(jobs):
                    t, h, kind = jobs[w]
                    k0, n = span(t, kind)
                    pe.wait_ge(S2["pt_evac"], w + 1)
                    if w % 8 == 0 and t:
                        pe.wait_ge(S2["oB_ready"], t)
                    vals = VSt if kind == 0 else VWt
                    o = bank(6)[:, (kind * 4 + h) * 64:(kind * 4 + h) * 64 + 64]
                    for b in range(n):
                        last = MM(o, pTB[w % 2][:, b * 128:b * 128 + 128], vals[:, k0 + b, :], start=(b == 0),
                                  stop=(b == n - 1))
                    last.then_inc(S2["o_done"], 1)
                t, step = j // 8, j % 8
                if step == 2 and t >= 1:
                    pe.wait_ge(S2["oB_ready"], t)
                    for a in range(2):
                        last = TR(bank(7)[:, a * 128:a * 128 + 128], oBs[:, a * 128:a * 128 + 128], ident)
                    last.then_inc(S2["oB_tp"], 1)
                if t < NT and step == 3:
                    if t:
                        pe.wait_ge(S2["oB_evac"], t)
                    for h in range(4):
                        last = MM(bank(7)[:, h * 16:h * 16 + 16], QBbd[t % 2][:, h // 2, h % 2, :], kcT, start=True, stop=True)
                    last.then_inc(S2["lc_done"], 1)
                if t < NT and step == 5:
                    pe.wait_ge(S2["pc_ready"], t + 1)
                    TR(bank(7)[0:64, 64:192], pcm.rearrange("p a b -> p (a b)"), ident).then_inc(S2["pc_tp"], 1)
                if t < NT and step == 7:
                    pe.wait_ge(S2["pc_evac"], t + 1)
                    MM(bank(7)[:, 192:448], pcT, vcbd, start=True, stop=True).then_inc(S2["oc2_done"], 1)

        @block.scalar
        def _(act):
            A = nc.scalar.activation
            chain = Chain(act, S2["ch2A"])
            nc.scalar.preload_act_table_set("natural_log_exp_and_others")
            act.wait_ge(S2["kc_done"], 1)
            chain(A(kn2j, bank(6)[0:16, 0:64], ACT.Square, accum_out=kn1[:, :]))
            chain(A(kn2[:, :], kn1[:, :], ACT.Ln, bias=eps[0:16, :], scale=1.0 / 64))
            A(kn2[:, :], kn2[:, :], ACT.Exp, scale=-0.5).then_inc(S2["kc_r"], 1)
            A(gB[:, :, :], NGt[:, :, :], ACT.Exp, scale=-1.0).then_inc(S2["gB_e"], 1)
            act.wait_ge(S2["bias_ready"], 1)
            for u in range(len(units) + 2):
                if u < len(units):
                    z, buf = zbank(u), zab[u % 2]
                    act.wait_ge(S2["z_done"], u + 1)
                    if u >= 2:
                        act.wait_ge(S2["spA_ready"], u - 1)
                    chain(A(buf, z, ACT.Abs))
                    chain(A(buf, buf, ACT.Exp, scale=-1.0))
                    A(buf, buf, ACT.Ln, bias=one[:, :]).then_inc(S2["l_ready"], 1)
                v = u - 1
                if 0 <= v < len(units):
                    act.wait_ge(S2["tri_done"], v + 1)
                    if v >= 2:
                        act.wait_ge(S2["av_done"], v - 1)
                    A(au[v % 2], zbank(v), ACT.Exp).then_inc(S2["a_ready"], 1)
                w = u - 2
                if 0 <= w and units[w][1] == 0:
                    t = units[w][0]
                    act.wait_ge(S2["oA_tp"], t + 1)
                    A(OT[:, 0:2, t * 128:t * 128 + 128], bank(4)[:, 0:256].rearrange("p (a b) -> p a b", a=2),
                      ACT.Copy).then_inc(S2["oA_evac"], 1)
            for j in range(len(jobs) + 3):
                v = j - 2
                if 0 <= v < len(jobs):
                    t, h, kind = jobs[v]
                    n = span(t, kind)[1]
                    act.wait_ge(S2["pt_tp"], v + 1)
                    if v >= 2:
                        act.wait_ge(S2["o_done"], v - 1)
                    A(pTB[v % 2][:, 0:n * 128], bank(4, 2)[:, 0:n * 128], ACT.Copy).then_inc(S2["pt_evac"], 1)
                if j < len(jobs):
                    t, h, kind = jobs[j]
                    k0, n = span(t, kind)
                    act.wait_ge(S2["s_ready"], j + 1)
                    if j >= 2:
                        act.wait_ge(S2["pt_tp"], j - 1)
                    if j % 8 == 0 and t >= 2:
                        act.wait_ge(S2["oB_ready"], t - 1)
                    A(pB[j % 2][:, 0:n * 128], sB[j % 2][:, 0:n * 128], ACT.Exp, bias=nmB[j % 2],
                      accum_out=lB[:, t % 2, 4 + kind * 4 + h:5 + kind * 4 + h]).then_inc(S2["p_ready2"], 1)
                t, step = j // 8, j % 8
                if step == 2 and t >= 1:
                    act.wait_ge(S2["oB_tp"], t)
                    A(OT[:, 2:4, (t - 1) * 128:t * 128], bank(7)[:, 0:256].rearrange("p (a b) -> p a b", a=2),
                      ACT.Copy).then_inc(S2["oB_evac"], 1)
                if t < NT and step == 3:
                    act.wait_ge(S2["lc_ready"], t + 1)
                    A(pcm, lcm, ACT.Exp).then_inc(S2["pc_exp"], 1)
                if t < NT and step == 5:
                    act.wait_ge(S2["pc_tp"], t + 1)
                    A(pcT, bank(7)[0:64, 64:192], ACT.Copy).then_inc(S2["pc_evac"], 1)

        @block.vector
        def _(dve):
            V = nc.vector
            chain = Chain(dve, S2["ch2V"])
            dve.wait_ge(S2["near_ps"], 1)
            V.tensor_copy(near, PS[:, 0:2048].rearrange("p (h x) -> p h x", h=4)[:, :, 0:NEAR]).then_inc(S2["near_ready"], 1)
            dve.wait_ge(S2["bias_ps"], 1)
            dve.wait_ge(S2["c2_in"], 16)
            chain(V.tensor_copy(pe_mean[:, :], bank(5)[0:64, 0:2]))
            for n in range(2):
                last = V.tensor_scalar(kmT[:, n, :], kmT[:, n, :], pe_mean[:, n:n + 1], None, ALU.add)
            last.then_inc(S2["km2_ready"], 1)
            dve.wait_ge(S2["skew_in"], 16)
            chain(V.tensor_copy(BS[:, :, 0:768], BS[:, :, 768:769].broadcast_to([128, 4, 768])))
            chain(V.tensor_copy(WB[:, :, :], BS[:, :, 384:1024]))
            V.tensor_tensor(WB[:, :, 0:128], WB[:, :, 0:128], K("winneg")[:, None, :].broadcast_to([128, 4, 128]), ALU.add)
            chain(V.tensor_copy(bc[:, :, :], bank(4)[:, 0:120].rearrange("p (a b) -> p a b", b=4)))
            V.tensor_scalar(vc01[:, :, :], bc[:, :, :], -1e29, None, ALU.is_gt)
            V.tensor_copy(bsel[:, :, :], bank(4)[:, 120:120 + 4 * NSEL].rearrange("p (a b) -> p a b", b=4))
            V.tensor_copy(bwin[:, :, :], bank(4)[:, 120 + 4 * NSEL:120 + 4 * (NSEL + NWIN)].rearrange("p (a b) -> p a b", b=4))
            V.tensor_copy(bcmp[0:4, :], bank(5)[0:4, 64:128]).then_inc(S2["bias_ready"], 1)
            dve.wait_ge(S2["kc_r"], 1)
            V.tensor_copy(kcs[:, :], bank(6)[0:16, 64:128])
            chain(V.scalar_tensor_tensor(kcr[:, 0:64], bank(6)[0:16, 0:64], kn2[:, :], kn_cmp[0:16, :], ALU.mult, ALU.mult))
            V.tensor_copy(kcr[:, 64:128], kcr[:, 0:64]).then_inc(S2["kc_n"], 1)
            dve.wait_ge(S2["gB_e"], 1)
            chain(V.tensor_scalar(gB[:, :, :], gB[:, :, :], 1.0, None, ALU.add))
            chain(V.reciprocal(gB[:, :, :], gB[:, :, :]))
            dve.wait_ge(S2["kc_tp"], 1)
            V.tensor_copy(kcT[:, :], bank(7)[:, 0:16])
            V.tensor_tensor(vcbd.rearrange("p (a b) -> p a b", a=4), bank(7)[0:64, None, 64:128].broadcast_to([64, 4, 64]),
                            K("cbd", 64).rearrange("p (a b) -> p a b", a=4), ALU.mult).then_inc(S2["kc_ready"], 1)
            for u in range(len(units) + 2):
                if u < len(units):
                    t, kb = units[u]
                    dve.wait_ge(S2["l_ready"], u + 1)
                    if u >= 2:
                        dve.wait_ge(S2["tri_done"], u - 1)
                    V.scalar_tensor_tensor(spu[u % 2], zbank(u), 0.0, zab[u % 2], ALU.max, ALU.add)\
                        .then_inc(S2["spA_ready"], 1)
                    dve.wait_ge(S2["spA_ready"], u + 1)
                    if kb == t:
                        V.tensor_copy(Rsum[u % 3], spu[u % 2]).then_inc(S2["R_ready"], 1)
                    else:
                        dve.wait_ge(S2["R_ready"], u)
                        V.tensor_tensor(Rsum[u % 3], Rsum[(u - 1) % 3], spu[u % 2], ALU.add).then_inc(S2["R_ready"], 1)
                w = u - 2
                if 0 <= w and units[w][1] == 0:
                    t = units[w][0]
                    dve.wait_ge(S2["av_done"], w + 1)
                    if t:
                        dve.wait_ge(S2["oA_tp"], t)
                    V.tensor_copy(oAs, bank(2 + t % 2)[:, 0:256]).then_inc(S2["oAs_ready"], 1)

            def heads(ap):
                return ap.rearrange("p (a b) -> p a b", b=64)

            for j in range(len(jobs) + 3):
                if j < len(jobs):
                    t, h, kind = jobs[j]
                    k0, n = span(t, kind)
                    dve.wait_ge(S2["sc_done"], j + 1)
                    if j >= 2:
                        dve.wait_ge(S2["p_ready2"], j - 1)
                    strip = BS[:, h, 1024 - n * 128:1024] if kind == 0 or t < 4 else WB[:, h, :]
                    chain(V.tensor_tensor(sB[j % 2][:, 0:n * 128], bank(2 * (j % 2), 2)[:, 0:n * 128], strip, ALU.add))
                    V.tensor_reduce(nmB[j % 2], sB[j % 2][:, 0:n * 128], AX.X, ALU.max, negate=True).then_inc(S2["s_ready"], 1)
                t, step = j // 8, j % 8
                if step == 2 and t >= 1:
                    T = t - 1
                    dve.wait_ge(S2["o_done"], 8 * t)
                    dve.wait_ge(S2["p_ready2"], 8 * t)
                    dve.wait_ge(S2["oc2_done"], t)
                    if T:
                        dve.wait_ge(S2["oB_tp"], T)
                    chain(V.tensor_scalar(cB[:, T % 2, :], lB[:, T % 2, :], 1e-30, None, ALU.max))
                    chain(V.reciprocal(cB[:, T % 2, :], cB[:, T % 2, :]))
                    chain(V.tensor_tensor(cB[:, T % 2, :].rearrange("p (b h) -> p b h", b=3),
                                          cB[:, T % 2, :].rearrange("p (b h) -> p b h", b=3),
                                          gB[:, T, :].rearrange("p (h b) -> p b h", b=3), ALU.mult))
                    src = (bank(7)[:, 192:448], bank(6)[:, 0:256], bank(6)[:, 256:512])
                    for b in range(3):
                        dst = oBs if b == 0 else oB2
                        chain(V.tensor_tensor(heads(dst), heads(src[b]),
                                              cB[:, T % 2, 4 * b:4 * b + 4][:, :, None].broadcast_to([128, 4, 64]), ALU.mult))
                        if b:
                            last = V.tensor_tensor(oBs, oBs, oB2, ALU.add)
                            if b == 1:
                                chain(last)
                    last.then_inc(S2["oB_ready"], 1)
                if t < NT and step == 3:
                    dve.wait_ge(S2["lc_done"], t + 1)
                    if t:
                        dve.wait_ge(S2["pc_tp"], t)
                    j0 = 14 - 2 * t
                    chain(V.tensor_tensor(lcm, bank(7)[:, 0:64].rearrange("p (a b) -> p a b", a=4),
                                          bc[:, j0:j0 + 16, :].rearrange("p j h -> p h j"), ALU.add))
                    chain(V.tensor_reduce(nmc, lcm, AX.X, ALU.max))
                    V.tensor_tensor(lcm, lcm, nmc[:, :, None].broadcast_to([128, 4, 16]), ALU.subtract)\
                        .then_inc(S2["lc_ready"], 1)
                if t < NT and step == 4:
                    dve.wait_ge(S2["pc_exp"], t + 1)
                    j0 = 14 - 2 * t
                    chain(V.tensor_tensor(pcm, pcm, vc01[:, j0:j0 + 16, :].rearrange("p j h -> p h j"), ALU.mult))
                    V.tensor_reduce(lB[:, t % 2, 0:4], pcm, AX.X, ALU.add).then_inc(S2["pc_ready"], 1)

        stage2.close()
        stage_over()

        acur[0] = keep
        NR = 32
        tpool = [TT[:, :, :].rearrange("p a b -> p (a b)"), 0]

        def tt(*dims, r=128):
            n = int(np.prod(dims))
            v = tpool[0][0:r, tpool[1]:tpool[1] + n]
            tpool[1] += n
            assert tpool[1] <= 8 * SEQ, tpool[1]
            return v if len(dims) == 1 else v.rearrange("p (a b) -> p a b", a=dims[0])

        kring = [tt(4, 256) for _ in range(4)]
        vring = [tt(4, 256) for _ in range(4)]
        Ks = [big(NSEL, 64) for _ in range(2)]
        Vs = [big(NSEL, 64) for _ in range(2)]
        CK = [big(NR, 64) for _ in range(2)]
        CV = [big(NR, 64) for _ in range(2)]
        cursor[0] = 0
        WK = [tmp(NWIN, 64) for _ in range(2)]
        WV = [tmp(NWIN, 64) for _ in range(2)]
        MK = [tmp(2, 256) for _ in range(2)]
        MV = [tmp(2, 256) for _ in range(2)]
        qrow = [tmp(3, 256) for _ in range(2)]
        qTs = [tmp(4, r=64) for _ in range(2)]
        gs = [tmp(3, r=4) for _ in range(2)]
        prod = [tmp(2112) for _ in range(1)] * 2
        gtj = tmp(64, r=64)
        zAs = [tmp(4, NR) for _ in range(2)]
        labs, spS, Csuf, wA = (tmp(4, NR) for _ in range(4))
        aAs = [big(4, NR) for _ in range(2)]
        SCs = [tmp(4, 40) for _ in range(2)]
        pSCs = [big(4, 40) for _ in range(2)]
        ksums = [tmp(2, 64) for _ in range(2)]
        kmTs = tmp(2, 64, r=64)
        kcn, vcn, kcTs = (tmp(64, r=64) for _ in range(3))
        kq, kr = tmp(1, r=64), tmp(1, r=64)
        lcs, pcs = tmp(64, r=4), tmp(64, r=4)
        nml, lcl, rcl = tmp(1, r=4), tmp(1, r=4), tmp(1, r=4)
        srw, gtw = tmp(64, r=64), tmp(64, r=64)
        scol, rk1, rk2 = tmp(1, r=64), tmp(1, r=64), tmp(1, r=64)
        pcTs = tmp(4, r=64)
        mx12 = tmp(12)
        mcol = tmp(1, r=12)
        dg12 = tmp(12, r=12)
        lp12 = tmp(12)
        rl3s = [tmp(3, r=4) for _ in range(2)]
        gg3s = [tmp(3, r=4) for _ in range(2)]
        ocmps = [tmp(64, r=4) for _ in range(2)]
        om4 = tmp(256, r=4)
        orow = tmp(3, 64, r=4)
        KT = [VA[:, 2 * n:2 * n + 2, :].rearrange("p a b -> p (a b)") for n in range(4)]
        NKT = 5
        qpair = [tmp(2, 4) for _ in range(2)]
        samrows = prod[0][0:8, 0:1024]
        idxf = tmp(NB)
        idx_pt = small[:, cursor[0]:cursor[0] + NB].bitcast(I32)
        cursor[0] += NB
        idx_c = small[:, cursor[0]:cursor[0] + 9].bitcast(I32)
        cursor[0] += 9
        idx_all = small[:, cursor[0]:cursor[0] + 9 * NB].bitcast(I32)
        cursor[0] += 9 * NB
        slot_k, slot_v = ([small[:, cursor[0] + 9 * n:cursor[0] + 9 * n + 9].bitcast(I32) for n in m] for m in ((0, 1), (2, 3)))
        cursor[0] += 36
        assert cursor[0] <= SMALL

        names = ("pt_in", "idx_f", "idx_ready", "slot_ready", "zeroS", "kA_used", "vA_used", "z_all", "lS_ready",
                 "spS_ready", "suf_ready", "X_done", "w_ready", "aS_ready", "sum_ready", "km_doneS",
                 "km_readyS", "kcS_done", "kcS_sq", "kcS_ready", "kcT_done", "kcT_ready", "lcS_done", "lcS_ready", "pcS_exp",
                 "pcS_ready", "imp_done", "rank_ready", "exp_done", "mx_ready", "mxT_done", "mxc_ready", "mxb_done",
                 "scS_ready", "pS_ready", "lpS_ready", "lS_done", "AB_done", "gs_e", "orow_ready", "orow_out", "sel_scored",
                 "kt_tp", "kt_evac", "samT_in", "gather_go", "samT_done", "samT_ready", "pcT_ready", "chSA", "chSV")
        S3 = {n: sem(n) for n in names}
        ks_in = [sem(f"kring_in{n}") for n in range(4)]
        vs_in = [sem(f"vring_in{n}") for n in range(4)]
        kpages_in = [sem(f"kpages_in{n}") for n in range(2)]
        vpages_in = [sem(f"vpages_in{n}") for n in range(2)]
        row_in = [sem(f"row_in{n}") for n in range(2)]
        vrow_in = [sem(f"vrow_in{n}") for n in range(2)]
        PARTS = (0, 1, 2, 3, 4, 5, 6, 7, 8, 12, 13, 14, 15)
        NROW, NVROW = 9, 4

        sbk = I["cache_sb_k"][0].rearrange("n (s r) h d -> (n s) (r h d)", r=4)
        sbv = I["cache_sb_v"][0].rearrange("n (s r) h d -> (n s) (r h d)", r=4)
        small_caches = [I[n][0].rearrange("n (s r) d -> (n s) (r d)", r=NR)
                        for n in ("cache_nsa_sel_k", "cache_nsa_sel_v", "cache_nsa_cmp_k", "cache_nsa_cmp_v")]

        stageS = ExitStack()
        block = stageS.enter_context(nc.Block())

        @block.sync
        def _(sy):
            sy.dma_start(idx_c, RO_d).then_inc(S3["pt_in"], 16)
            for s in range(4):
                sy.dma_start(idx_pt[s:128:4, :], I["page_table"].rearrange("b j -> j b")).then_inc(S3["pt_in"], 16)

            row = lambda b, c, w: srow_d[bass.ds(b, 1), c:c + w]

            def score_rows(b, par):
                def load(dst, src):
                    sy.dma_start(dst, src).then_inc(row_in[par], 16)
                one = bass.ds(b, 1)
                load(qrow[par].rearrange("p a b -> p (a b)"), row(b, RQA, 768).broadcast_to([128, 768]))
                load(Ks[par][0:1, NR, :], row(b, RKS, 64))
                load(WK[par][0:1, 4, :], row(b, RKW, 64))
                load(WK[par][:, 0:4, :], I["cache_nsa_win_k"][0, one].rearrange("a (p r) d -> p (a r) d", r=4))
                load(MK[par][:, :, :], I["cache_mem_k"][0, one].rearrange("a (p r) h d -> p (a r) (h d)", r=2))
                load(qTs[par], srow_d[one, RQB:RQB + 256].rearrange("a (h d) -> d (a h)", d=64))
                for n in range(2):
                    load(qpair[par][64 * n:64 * n + 64, n, :], srow_d[one, RQB:RQB + 256].rearrange("a (h d) -> d (a h)", d=64))
                load(gs[par], srow_d[one, RG:RG + 12].rearrange("a (h g) -> h (a g)", g=3))

            def value_rows(b, par):
                def load(dst, src):
                    sy.dma_start(dst, src).then_inc(vrow_in[par], 16)
                one = bass.ds(b, 1)
                load(Vs[par][0:1, NR, :], row(b, RVS, 64))
                load(WV[par][0:1, 4, :], row(b, RVW, 64))
                load(WV[par][:, 0:4, :], I["cache_nsa_win_v"][0, one].rearrange("a (p r) d -> p (a r) d", r=4))
                load(MV[par][:, :, :], I["cache_mem_v"][0, one].rearrange("a (p r) h d -> p (a r) (h d)", r=2))

            def store(b):
                sy.wait_ge(S3["orow_ready"], b + 1)
                for n, c in ((0, 0), (1, 256), (2, 768)):
                    sy.dma_start(osam_d[bass.ds(b, 1), c:c + 256].rearrange("a (h d) -> h (a d)", d=64),
                                 orow[:, n, :]).then_inc(S3["orow_out"], 16)

            sy.wait_ge(S3["zeroS"], 1)
            for par in range(2):
                score_rows(par, par)
                value_rows(par, par)
            with sy.Fori(0, NB // 2 - 1) as pair:
                i = pair * 2
                for par in range(2):
                    sy.wait_ge(S3["gs_e"], i + (par + 1))
                    score_rows(i + par + 2, par)
                    store(i + par)
                    value_rows(i + par + 2, par)
            for b in range(NB - 2, NB):
                store(b)
            sy.wait_ge(S3["orow_out"], 16 * 3 * NB)
            for c in (0, 256, 768):
                sy.dma_start(samrows[:, c:c + 256], osam_d[:, c:c + 256]).then_inc(S3["samT_in"], 16)

        @block.gpsimd
        def _(pool):
            G = nc.gpsimd
            for par in range(2):
                for x in (Ks, Vs):
                    G.memset(x[par][:, NR, :], 0.0)
                G.memset(qpair[par], 0.0)
                for x in (WK, WV):
                    last = G.memset(x[par][:, 4, :], 0.0)
            last.then_inc(S3["zeroS"], 1)
            pool.wait_ge(S3["idx_ready"], 1)

            def wait(s, v):
                pool.wait_ge(s, v)
                pool.sem_inc(S3["gather_go"], 1)

            def gather(dst, src, slot, c, s):
                G.indirect_dma_start(dst, None, src, bass.IndirectOffsetOnAxis(ap=slot.bitcast(U32)[:, c:c + 1], axis=0)).then_inc(s, 16)

            def rows(slot, b, used, n):
                if used is not None:
                    wait(*used)
                G.tensor_copy(slot, idx_all[:, bass.ds(b * 9, 9)]).then_inc(S3["slot_ready"], 1)
                wait(S3["slot_ready"], n)

            def keys(b, par, cs, first=False):
                for c in cs:
                    if not first:
                        wait(S3["kA_used"], 8 * b + (c - 3))
                    gather(kring[c % 4].rearrange("p a b -> p (a b)"), sbk, slot_k[par], c, ks_in[c % 4])

            def values(b, par, cs, first=False):
                for c in cs:
                    if not first:
                        wait(S3["vA_used"], 8 * b + (c - 3))
                    gather(vring[c % 4].rearrange("p a b -> p (a b)"), sbv, slot_v[par], c, vs_in[c % 4])

            def key_pages(b, par):
                for n, x in ((0, Ks), (2, CK), (3, CV)):
                    gather(x[par][:, 0:NR, :].rearrange("p a b -> p (a b)"), small_caches[n], slot_k[par], 8, kpages_in[par])

            def step(b, par, kind):
                keyed, valued = kind < 7, kind > 0
                if keyed:
                    rows(slot_k[1 - par], b + 1, None if kind == 0 else (S3["kA_used"], 8 * b), 2 * b + (2 if kind == 0 else 1))
                    keys(b + 1, 1 - par, range(4))
                if valued:
                    v = b - 1
                    rows(slot_v[1 - par], v, None if kind < 3 and isinstance(b, int) and b < 3 else (S3["vA_used"], 8 * b - 16),
                         2 * b + 2 if keyed else 2 * b + (1 if kind == 7 else 0))
                    if kind == 1:
                        pass
                    elif not (isinstance(b, int) and b == 2):
                        wait(S3["orow_ready"], b - 2)
                    gather(Vs[1 - par][:, 0:NR, :].rearrange("p a b -> p (a b)"), small_caches[1], slot_v[1 - par], 8, vpages_in[1 - par])
                    values(v, 1 - par, range(4), first=(kind == 1))
                if keyed:
                    if kind:
                        wait(S3["gs_e"], b)
                    key_pages(b + 1, 1 - par)
                    keys(b + 1, 1 - par, range(4, 8))
                if valued:
                    values(v, 1 - par, range(4, 8))

            rows(slot_k[0], 0, None, 1)
            keys(0, 0, range(4), first=True)
            key_pages(0, 0)
            keys(0, 0, range(4, 8))
            for b in range(3):
                step(b, b % 2, b)
            with pool.Fori(0, NB // 2 - 2) as pair:
                for n in range(2):
                    step(pair * 2 + (3 + n), (3 + n) % 2, 2)
            step(NB - 1, 1, 7)
            step(NB, 0, 8)

        @block.vector
        def _(dve):
            V = nc.vector
            chain = Chain(dve, S3["chSV"])
            dve.wait_ge(S3["pt_in"], 80)
            chain(V.tensor_scalar(idxf, idx_pt, 32.0, None, ALU.mult))
            for b in range(NB):
                last = V.tensor_scalar(idx_all[:, 9 * b:9 * b + 8], idx_c[:, 0:8], idxf[:, b:b + 1], None, ALU.add)
            chain(last)
            chain(V.tensor_scalar(idxf, idx_pt, 4.0, None, ALU.mult))
            for b in range(NB):
                last = V.tensor_scalar(idx_all[:, 9 * b + 8:9 * b + 9], idx_c[:, 8:9], idxf[:, b:b + 1], None, ALU.add)
            last.then_inc(S3["idx_ready"], 1)

            def score(b, par, i, n):
                zA, SC, ksum = zAs[par], SCs[par], ksums[par]
                qA, qB, qM = (qrow[par][:, a, :] for a in range(3))
                if n == 0:
                    dve.wait_ge(row_in[par], i * (8 * NROW) + 16 * NROW)
                if n < 8:
                    c = n
                    pr = prod[0][:, (c % 2) * 1024:(c % 2) * 1024 + 1024]
                    if not (isinstance(b, int) and b == 0 and c < 2):
                        dve.wait_ge(S3["kA_used"], 8 * b + (c - 1))
                    dve.wait_ge(ks_in[c % 4], b * 32 + 16 * (c // 4 + 1))
                    chain(V.tensor_tensor(pr.rearrange("p (r x) -> p r x", r=4), kring[c % 4],
                                          qA[:, None, :].broadcast_to([128, 4, 256]), ALU.mult))
                    V.tensor_reduce(zA[:, :, 4 * c:4 * c + 4].rearrange("p h r -> p r h"),
                                    pr.rearrange("p (r h d) -> p r h d", r=4, h=4), AX.X, ALU.add).then_inc(S3["kA_used"], 1)
                elif n == 8:
                    dve.wait_ge(S3["kA_used"], 8 * b + 8)
                    V.tensor_scalar(zA, zA, 0.125, None, ALU.mult).then_inc(S3["z_all"], 1)
                elif n == 12:
                    pr = prod[0][:, 0:1280].rearrange("p (h r d) -> p h r d", h=4, r=NWIN)
                    for h in range(4):
                        last = V.tensor_tensor(pr[:, h], WK[par], qB[:, None, h * 64:h * 64 + 64].broadcast_to([128, NWIN, 64]), ALU.mult)
                    chain(last)
                    chain(V.tensor_reduce(SC[:, :, 33:38], pr, AX.X, ALU.add))
                elif n == 13:
                    pr = prod[0][:, 0:512]
                    chain(V.tensor_tensor(pr.rearrange("p (r x) -> p r x", r=2), MK[par], qM[:, None, :].broadcast_to([128, 2, 256]), ALU.mult))
                    chain(V.tensor_reduce(SC[:, :, 38:40].rearrange("p h r -> p r h"),
                                          pr.rearrange("p (r h d) -> p r h d", r=2, h=4), AX.X, ALU.add))
                elif n == 14:
                    dve.wait_ge(kpages_in[par], i * 24 + 48)
                    chain(V.tensor_reduce(ksum[:, 0, :], CK[par].rearrange("p r d -> p d r"), AX.X, ALU.add))
                else:
                    chain(V.tensor_tensor(SC[:, :, 33:38], SC[:, :, 33:38], bwin.rearrange("p r h -> p h r"), ALU.add))
                    dve.wait_ge(S3["sel_scored"], b + 1)
                    V.tensor_tensor(SC[:, :, 0:NSEL], bank(0)[:, 128:128 + 4 * NSEL].rearrange("p (r h) -> p h r", h=4),
                                    bsel.rearrange("p r h -> p h r"), ALU.add)
                    V.tensor_reduce(ksum[:, 1, :], CV[par].rearrange("p r d -> p d r"), AX.X, ALU.add).then_inc(S3["sum_ready"], 1)

            def outputs(b, par):
                gg3, rl3 = gg3s[par], rl3s[par]
                dve.wait_ge(S3["AB_done"], b + 1)
                if not (isinstance(b, int) and b == 0):
                    dve.wait_ge(S3["orow_out"], b * 48)
                chain(V.scalar_tensor_tensor(orow[:, 1, :], bank(5)[0:4, 0:64], gg3[:, 1:2], ocmps[par], ALU.mult, ALU.add))
                chain(V.scalar_tensor_tensor(orow[:, 1, :], bank(5)[0:4, 64:128], gg3[:, 2:3], orow[:, 1, :], ALU.mult, ALU.add))
                chain(V.scalar_tensor_tensor(om4, bank(4)[0:4, 256:512], rl3[:, 2:3], K("blk4", 4), ALU.mult, ALU.mult))
                chain(V.tensor_reduce(orow[:, 2, :], om4.rearrange("p (h d) -> p d h", h=4), AX.X, ALU.add))
                dve.wait_ge(S3["vA_used"], 8 * b + 8)
                chain(V.tensor_tensor(om4, bank(4)[0:4, 0:256], K("blk4", 4), ALU.mult))
                V.tensor_reduce(orow[:, 0, :], om4.rearrange("p (h d) -> p d h", h=4), AX.X, ALU.add).then_inc(S3["orow_ready"], 1)

            def seq(b, par, i, following=True):
                zA, SC, pSC, gg3, rl3 = zAs[par], SCs[par], pSCs[par], gg3s[par], rl3s[par]

                def nxt(n):
                    if following:
                        score(b + 1, 1 - par, i + 2 * par, n)

                nxt(0)
                dve.wait_ge(S3["lS_ready"], b + 1)
                chain(V.scalar_tensor_tensor(spS, zA, 0.0, labs, ALU.max, ALU.add))
                chain(V.tensor_tensor_scan(Csuf.rearrange("p a b -> p (a b)")[:, ::-1], K("restart")[:, ::-1],
                                           spS.rearrange("p a b -> p (a b)")[:, ::-1], 0.0, ALU.mult, ALU.add))
                V.tensor_tensor(wA, zA, Csuf, ALU.subtract).then_inc(S3["suf_ready"], 1)
                dve.wait_ge(S3["suf_ready"], b + 1)
                nxt(1)
                dve.wait_ge(S3["X_done"], b + 1)
                V.tensor_tensor(wA, wA, bank(2)[:, 260:264][:, :, None].broadcast_to([128, 4, NR]), ALU.subtract)\
                    .then_inc(S3["w_ready"], 1)
                dve.wait_ge(S3["km_doneS"], b + 1)
                for n in range(2):
                    last = V.tensor_scalar(kmTs[:, n, :], bank(0)[0:64, 64 * n:64 * n + 64], pe_mean[:, n:n + 1], None, ALU.add)
                last.then_inc(S3["km_readyS"], 1)
                nxt(2)
                dve.wait_ge(S3["kcS_sq"], b + 1)
                V.tensor_copy(vcn, bank(1)[0:64, 64:128])
                V.scalar_tensor_tensor(kcn, bank(1)[0:64, 0:64], kr, kn_cmp[0:64, :], ALU.mult, ALU.mult).then_inc(S3["kcS_ready"], 1)
                nxt(3)
                dve.wait_ge(S3["kcT_done"], b + 1)
                V.tensor_copy(kcTs, bank(1)[0:64, 128:192]).then_inc(S3["kcT_ready"], 1)
                nxt(4)
                dve.wait_ge(S3["lcS_done"], b + 1)
                chain(V.tensor_tensor(lcs, bank(1)[0:4, 256:320], bcmp[0:4, :], ALU.add))
                V.tensor_reduce(nml, lcs, AX.X, ALU.max, negate=True).then_inc(S3["lcS_ready"], 1)
                nxt(5)
                dve.wait_ge(S3["pcS_exp"], b + 1)
                chain(V.tensor_scalar(rcl, lcl, 1e-30, None, ALU.max))
                chain(V.reciprocal(rcl, rcl))
                V.tensor_scalar(pcs, pcs, rcl, None, ALU.mult).then_inc(S3["pcS_ready"], 1)
                nxt(6)
                dve.wait_ge(S3["imp_done"], b + 1)
                V.tensor_copy(pcTs, bank(2)[0:64, 64:68]).then_inc(S3["pcT_ready"], 1)
                chain(V.tensor_tensor(srw, bank(2)[0:64, 0:64], K("forced", 64), ALU.max))
                chain(V.tensor_tensor(gtw, srw, K("ident", 64)[:, 0:64], ALU.mult))
                chain(V.tensor_reduce(scol, gtw, AX.X, ALU.add))
                chain(V.tensor_scalar(gtw, srw, scol, None, ALU.is_gt))
                chain(V.tensor_reduce(rk1, gtw, AX.X, ALU.add))
                chain(V.scalar_tensor_tensor(gtw, srw, scol, K("jlti", 64), ALU.is_equal, ALU.mult))
                chain(V.tensor_reduce(rk2, gtw, AX.X, ALU.add))
                chain(V.tensor_tensor(rk1, rk1, rk2, ALU.add))
                chain(V.tensor_scalar(rk1, rk1, 14.5, None, ALU.is_lt))
                V.tensor_scalar(rk1, rk1, -1.0, 1e30, ALU.add, ALU.mult).then_inc(S3["rank_ready"], 1)
                nxt(7)
                dve.wait_ge(S3["exp_done"], b + 1)
                chain(V.tensor_scalar(SC[:, :, 0:32], SC[:, :, 0:32], bank(2)[:, 256:257], None, ALU.add))
                segs = ((0, 33), (33, 38), (38, 40))
                for n, (a, c) in enumerate(segs):
                    last = V.tensor_reduce(mx12[:, 4 * n:4 * n + 4], SC[:, :, a:c], AX.X, ALU.max)
                last.then_inc(S3["mx_ready"], 1)
                nxt(8)
                nxt(12)
                dve.wait_ge(S3["mxT_done"], b + 1)
                chain(V.tensor_reduce(mcol, bank(3)[0:12, 0:128], AX.X, ALU.max))
                V.tensor_scalar(dg12, K("ident", 12)[:, 0:12], mcol, None, ALU.mult).then_inc(S3["mxc_ready"], 1)
                nxt(13)
                dve.wait_ge(S3["mxb_done"], b + 1)
                for n, (a, c) in enumerate(segs):
                    last = V.tensor_tensor(SC[:, :, a:c], SC[:, :, a:c],
                                           bank(3)[:, 128 + 4 * n:132 + 4 * n][:, :, None].broadcast_to([128, 4, c - a]), ALU.subtract)
                last.then_inc(S3["scS_ready"], 1)
                nxt(14)
                dve.wait_ge(S3["pS_ready"], b + 1)
                for n, (a, c) in enumerate(segs):
                    last = V.tensor_reduce(lp12[:, 4 * n:4 * n + 4], pSC[:, :, a:c], AX.X, ALU.add)
                last.then_inc(S3["lpS_ready"], 1)
                dve.wait_ge(S3["gs_e"], b + 1)
                chain(V.tensor_scalar(gg3, gg3, 1.0, None, ALU.add))
                chain(V.reciprocal(gg3, gg3))
                dve.wait_ge(S3["lS_done"], b + 1)
                chain(V.reciprocal(rl3, bank(3)[0:4, 144:147]))
                chain(V.tensor_tensor(gg3[:, 1:3], gg3[:, 1:3], rl3[:, 0:2], ALU.mult))
                chain(V.tensor_scalar(ocmps[par], bank(7)[0:4, 0:64], gg3[:, 0:1], None, ALU.mult))
                nxt(15)
                if not (isinstance(b, int) and b == 0):
                    outputs(b - 1, 1 - par)

            for n in PARTS:
                score(0, 0, 0, n)
            for b in range(2):
                n0 = chain.n
                seq(b, b, 0)
            CHAIN_VS = chain.n - n0
            with dve.Fori(1, NB // 2 - 1) as pair:
                i = pair * 2
                chain.enter(i - 2, CHAIN_VS)
                for par in range(2):
                    seq(i + par, par, i)
            chain.leave(NB - 4, 2)
            seq(NB - 2, 0, NB - 2)
            seq(NB - 1, 1, NB - 2, following=False)
            outputs(NB - 1, 1)

        @block.scalar
        def _(act):
            A = nc.scalar.activation
            chain = Chain(act, S3["chSA"])
            nc.scalar.preload_act_table_set("natural_log_exp_and_others")

            def turned(b, g):
                act.wait_ge(S3["kt_tp"], b * NKT + (g + 1))
                src, dst = bank(6), KT[g % 4]
                if g == NKT - 1:
                    src, dst = src[0:64, 0:128], dst[0:64, 0:128]
                A(dst, src, ACT.Copy).then_inc(S3["kt_evac"], 1)

            def seq(b, par, i, following=True):
                zA, SC, gg3 = zAs[par], SCs[par], gg3s[par]
                act.wait_ge(S3["z_all"], b + 1)
                chain(A(labs, zA, ACT.Abs))
                chain(A(labs, labs, ACT.Exp, scale=-1.0))
                A(labs, labs, ACT.Ln, bias=one[:, :]).then_inc(S3["lS_ready"], 1)
                act.wait_ge(S3["w_ready"], b + 1)
                A(aAs[par], wA, ACT.Exp).then_inc(S3["aS_ready"], 1)
                act.wait_ge(S3["kcS_done"], b + 1)
                chain(A(gtj, bank(1)[0:64, 0:64], ACT.Square, accum_out=kq))
                chain(A(kr, kq, ACT.Ln, bias=eps[0:64, :], scale=1.0 / 64))
                A(kr, kr, ACT.Exp, scale=-0.5).then_inc(S3["kcS_sq"], 1)
                act.wait_ge(S3["lcS_ready"], b + 1)
                A(pcs, lcs, ACT.Exp, bias=nml, accum_out=lcl).then_inc(S3["pcS_exp"], 1)
                act.wait_ge(row_in[par], i * (8 * NROW) + 16 * NROW)
                A(gg3, gs[par], ACT.Exp, scale=-1.0).then_inc(S3["gs_e"], 1)
                if following:
                    for g in range(NKT - 1):
                        turned(b + 1, g)
                act.wait_ge(S3["scS_ready"], b + 1)
                A(pSCs[par], SC, ACT.Exp).then_inc(S3["pS_ready"], 1)
                if following:
                    turned(b + 1, NKT - 1)

            for g in range(NKT):
                turned(0, g)
            for b in range(2):
                n0 = chain.n
                seq(b, b, 0)
            CHAIN_AS = chain.n - n0
            with act.Fori(1, NB // 2 - 1) as pair:
                i = pair * 2
                chain.enter(i - 2, CHAIN_AS)
                for par in range(2):
                    seq(i + par, par, i)
            chain.leave(NB - 4, 2)
            seq(NB - 2, 0, NB - 2)
            seq(NB - 1, 1, NB - 2, following=False)
            act.wait_ge(S3["samT_done"], 1)
            samT = bank(7)[:, 0:64].rearrange("p (a b) -> p a b", b=8)
            A(OT[:, 0:4, SEQ:NCOL], samT[:, 0:4, :], ACT.Copy)
            A(OT[:, 6:8, SEQ:NCOL], samT[:, 6:8, :], ACT.Copy).then_inc(S3["samT_ready"], 1)

        @block.tensor
        def _(pe):
            MM, TR = nc.tensor.matmul, nc.tensor.transpose
            ident = K("ident")

            def wait(s, v):
                at = v if isinstance(v, int) else pe.snap(v)
                pe.wait_ge(S3["zeroS"], 1)
                pe.wait_ge(s, at)

            def values(b, par, i, n):
                pSC = pSCs[par]
                if n in (0, 1, 4, 7):
                    if n == 0:
                        if not (isinstance(b, int) and b == 0):
                            wait(S3["orow_ready"], b)
                        wait(S3["aS_ready"], b + 1)
                    for c in {0: (0, 1), 1: (2, 3), 4: (4, 5), 7: (6, 7)}[n]:
                        wait(vs_in[c % 4], b * 32 + 16 * (c // 4 + 1))
                        for r in range(4):
                            last = MM(bank(4)[0:4, 0:256], aAs[par][:, :, 4 * c + r], vring[c % 4][:, r, :],
                                      start=(c == 0 and r == 0), stop=(c == 7 and r == 3))
                        last.then_inc(S3["vA_used"], 1)
                elif n < 7:
                    if n == 2:
                        wait(vpages_in[par], i * 8 + 16)
                        wait(vrow_in[par], i * (8 * NVROW) + 16 * NVROW)
                    for r in {2: range(8), 3: range(8, 16), 5: range(16, 24), 6: range(24, NSEL)}[n]:
                        MM(bank(5)[0:4, 0:64], pSC[:, :, r], Vs[par][:, r, :], start=(r == 0), stop=(r == NSEL - 1))
                else:
                    for r in range(NWIN):
                        MM(bank(5)[0:4, 64:128], pSC[:, :, 33 + r], WV[par][:, r, :], start=(r == 0), stop=(r == NWIN - 1))
                    for r in range(2):
                        last = MM(bank(4)[0:4, 256:512], pSC[:, :, 38 + r], MV[par][:, r, :], start=(r == 0), stop=(r == 1))
                    last.then_inc(S3["AB_done"], 1)

            def turn(b, par, i, g):
                if g == 0:
                    wait(kpages_in[par], i * 24 + 48)
                    wait(row_in[par], i * (8 * NROW) + 16 * NROW)
                if not (isinstance(b, int) and b == 0 and g == 0):
                    wait(S3["kt_evac"], b * NKT + g)
                flat = Ks[par].rearrange("p a b -> p (a b)")
                if g < NKT - 1:
                    for n in range(4):
                        last = TR(bank(6)[:, n * 128:n * 128 + 128], flat[:, (4 * g + n) * 128:(4 * g + n) * 128 + 128], ident)
                else:
                    last = TR(bank(6)[0:64, 0:128], flat[:, 32 * 64:33 * 64], ident)
                last.then_inc(S3["kt_tp"], 1)

            def score(b, par, g):
                wait(S3["kt_evac"], b * NKT + (g + 1))
                if g < NKT - 1:
                    for n in range(4):
                        c = 128 + 8 * (4 * g + n)
                        MM(bank(0)[:, c:c + 8], KT[g % 4][:, n * 128:n * 128 + 128], qpair[par].rearrange("p a b -> p (a b)"),
                           start=True, stop=True)
                else:
                    MM(bank(0)[:, 256:260], KT[0][0:64, 0:128], qpair[par][0:64, 0, :], start=True, stop=True)\
                        .then_inc(S3["sel_scored"], 1)

            def seq(b, par, i, following=True):
                first = isinstance(b, int) and b == 0
                ipast = i if par else i - 2
                inext = i + 2 * par

                def fill(n):
                    if not first:
                        values(b - 1, 1 - par, ipast, n)
                    if following and n >= 5:
                        if n > 5:
                            score(b + 1, 1 - par, n - 6)
                        turn(b + 1, 1 - par, inext, n - 5)

                wait(row_in[par], i * (8 * NROW) + 16 * NROW)
                wait(S3["sum_ready"], b + 1)
                for n in range(2):
                    last = MM(bank(0)[0:64, 64 * n:64 * n + 64], ksums[par][:, n, :], K("pair"), start=True, stop=True)
                last.then_inc(S3["km_doneS"], 1)
                fill(0)
                wait(S3["suf_ready"], b + 1)
                MM(bank(2)[:, 260:264], K("strict"), Csuf[:, :, 0], start=True, stop=True).then_inc(S3["X_done"], 1)
                fill(1)
                wait(S3["km_readyS"], b + 1)
                for n in range(2):
                    last = MM(bank(1)[0:64, 64 * n:64 * n + 64], kmTs[:, n, :], phi_kv[:, n, :], start=True, stop=True)
                last.then_inc(S3["kcS_done"], 1)
                fill(2)
                wait(S3["kcS_ready"], b + 1)
                TR(bank(1)[0:64, 128:192], kcn, ident[0:64, 0:64]).then_inc(S3["kcT_done"], 1)
                fill(3)
                wait(S3["kcT_ready"], b + 1)
                MM(bank(1)[0:4, 256:320], qTs[par], kcTs, start=True, stop=True).then_inc(S3["lcS_done"], 1)
                fill(4)
                wait(S3["pcS_ready"], b + 1)
                MM(bank(2)[0:64, 0:64], K("ones", 4)[:, 0:64], pcs, start=True, stop=True)
                TR(bank(2)[0:64, 64:68], pcs, ident[0:4, 0:4]).then_inc(S3["imp_done"], 1)
                fill(5)
                wait(S3["pcT_ready"], b + 1)
                MM(bank(7)[0:4, 0:64], pcTs, vcn, start=True, stop=True)
                wait(S3["rank_ready"], b + 1)
                MM(bank(2)[:, 256:257], K("expand", 64), rk1, start=True, stop=True).then_inc(S3["exp_done"], 1)
                fill(6)
                wait(S3["mx_ready"], b + 1)
                TR(bank(3)[0:12, 0:128], mx12, ident).then_inc(S3["mxT_done"], 1)
                fill(7)
                wait(S3["mxc_ready"], b + 1)
                MM(bank(3)[:, 128:140], K("ones", 12), dg12, start=True, stop=True).then_inc(S3["mxb_done"], 1)
                fill(8)
                wait(S3["lpS_ready"], b + 1)
                for n in range(3):
                    last = MM(bank(3)[0:4, 144 + n:145 + n], lp12[:, 4 * n:4 * n + 4], K("ones")[:, 0:1], start=True, stop=True)
                last.then_inc(S3["lS_done"], 1)
                if following:
                    score(b + 1, 1 - par, NKT - 2)
                    turn(b + 1, 1 - par, inext, NKT - 1)
                    score(b + 1, 1 - par, NKT - 1)

            for g in range(NKT):
                turn(0, 0, 0, g)
                score(0, 0, g)
            for b in range(2):
                seq(b, b, 0)
            with pe.Fori(1, NB // 2 - 1) as pair:
                i = pair * 2
                for par in range(2):
                    seq(i + par, par, i)
            seq(NB - 2, 0, NB - 2)
            seq(NB - 1, 1, NB - 2, following=False)
            for n in range(9):
                values(NB - 1, 1, NB - 2, n)
            pe.wait_ge(S3["samT_in"], 48)
            for a in (0, 1, 2, 3, 6, 7):
                last = TR(bank(7)[:, 8 * a:8 * a + 8], samrows[:, a * 128:a * 128 + 128], ident[0:8, 0:8])
            last.then_inc(S3["samT_done"], 1)

        stageS.close()
        stage_over()

        first_stages.close()
        stage3 = ExitStack()

        def split_part(name, shape):
            return stage3.enter_context(nc.sbuf_tensor(name, shape, F32R))

        TC = NCOL // 3
        hTh, hTl = split_part("rows_high", [128, KD, NCOL]), split_part("rows_low", [128, KD, NCOL])
        whigh = [split_part(f"gate_high{n}", [128, KD, 128]) for n in range(2)]
        wlow = [split_part(f"gate_low{n}", [128, KD, 128]) for n in range(2)]
        wgate = [stage3.enter_context(nc.sbuf_tensor(f"gate{n}", [128, KD, 128], F32)) for n in range(2)]
        wout = TT[:, :, :]
        cursor[0] = 0
        mT = tmp(KD, NCOL)
        hT = mT
        wbr = [tmp(2, 128) for _ in range(2)]
        sgm = [tmp(TC) for _ in range(2)]
        mtmp = tmp(TC)
        hT_in, out_in = [sem(f"hT_in{c}") for c in range(3)], sem("w_out_in")
        gate_in = [sem(f"gate_in{n}") for n in range(2)]
        gu_done, sg_ready, mrg_done, mtmp_ready, xhigh_ready, xlow_ready, whigh_ready, wlow_ready = (sem(n) for n in (
            "gu_done", "sg_ready", "mrg_done", "mtmp_ready", "xhigh_ready", "xlow_ready", "whigh_ready", "wlow_ready"))
        f32 = lambda v: v.bitcast(F32)
        NG_U = 12
        br_d = I["w_branch"][0].rearrange("n (a p) d -> n p a d", p=128)

        block = stage3.enter_context(nc.Block())

        @block.sync
        def _(sy):
            def load(j, n):
                cols = bass.ds(j * 128 + (NP1 + n * D), 128)
                sy.dma_start(wgate[n % 2][:, :, :], W1_d[:, :, cols]).then_inc(gate_in[n % 2], 16)
                sy.dma_start(wbr[n % 2], br_d[n][:, :, bass.ds(j * 128, 128)]).then_inc(gate_in[n % 2], 16)

            load(0, 0)
            for c in range(3):
                cols = slice(c * TC, min(c * TC + TC, SEQ))
                sy.dma_start(hT[:, :, cols], hT_d[:, :, cols]).then_inc(hT_in[c], 16)
            load(0, 1)
            sy.dma_start(wout, I["w_out"][0].rearrange("(k p) n -> p k n", p=128)).then_inc(out_in, 16)
            with sy.Fori(0, KD - 1) as j:
                for n in range(4):
                    sy.wait_ge(gu_done, j * NG_U + 3 * (n + 1))
                    load(j + (n + 2) // 4, (n + 2) % 4)
            for n in range(2):
                sy.wait_ge(gu_done, (KD - 1) * NG_U + 3 * (n + 1))
                load(KD - 1, n + 2)

        @block.tensor
        def _(pe):
            MM = nc.tensor.matmul

            def channels(j, first=False):
                for n in range(4):
                    pe.wait_ge(wlow_ready, j * 4 + (n + 1))
                    H, L = whigh[n % 2], wlow[n % 2]
                    for c in range(3):
                        u = 3 * n + c
                        if first and n == 0:
                            pe.wait_ge(xlow_ready, c + 1)
                        if not (first and u < 4):
                            pe.wait_ge(mrg_done, j * NG_U + (u - 3))
                        cols = slice(c * TC, c * TC + TC)
                        G, U = bank(2 * (u % 4))[:, 0:TC], bank(2 * (u % 4) + 1)[:, 0:TC]
                        for k in range(KD):
                            MM(G, H[:, k, :], hTh[:, k, cols], start=(k == 0), stop=False)
                            MM(G, H[:, k, :], hTl[:, k, cols], start=False, stop=False)
                            MM(G, L[:, k, :], hTh[:, k, cols], start=False, stop=(k == KD - 1))
                        for a in range(2):
                            last = MM(U, wbr[n % 2][:, a, :], OT[:, 2 * n + a, cols], start=(a == 0), stop=(a == 1))
                        last.then_inc(gu_done, 1)

            channels(0, True)
            with pe.Fori(1, KD) as j:
                channels(j)

        @block.scalar
        def _(act):
            nc.scalar.preload_act_table(ACT.Sigmoid)

            def weights_high(j, n):
                act.wait_ge(gate_in[n % 2], j * 64 + 32 * (n // 2 + 1))
                nc.scalar.copy(whigh[n % 2][:, :, :], wgate[n % 2][:, :, :]).then_inc(whigh_ready, 1)

            def channels(j, first=False, last=False):
                for u in range(NG_U):
                    n, c = u // 3, u % 3
                    act.wait_ge(gu_done, j * NG_U + (u + 1))
                    if not (first and u < 2):
                        act.wait_ge(mrg_done, j * NG_U + (u - 1))
                    nc.scalar.activation(sgm[u % 2], bank(2 * (u % 4))[:, 0:TC], ACT.Sigmoid).then_inc(sg_ready, 1)
                    if c == 0 and not (last and n == 3):
                        weights_high(j + (n + 1) // 4, (n + 1) % 4)

            weights_high(0, 0)
            for c in range(3):
                act.wait_ge(hT_in[c], 16 if c < 2 else 17)
                cols = slice(c * TC, c * TC + TC)
                nc.scalar.copy(hTh[:, :, cols], hT[:, :, cols]).then_inc(xhigh_ready, 1)
            channels(0, True)
            with act.Fori(1, KD - 1) as j:
                channels(j)
            channels(KD - 1, last=True)

        @block.vector
        def _(dve):
            V = nc.vector
            V.tensor_copy(hT[:, :, SEQ:NCOL], hT_s[:, :, :]).then_inc(hT_in[2], 1)

            def weights_low(j, n):
                dve.wait_ge(whigh_ready, j * 4 + (n + 1))
                V.tensor_tensor(wlow[n % 2][:, :, :], wgate[n % 2][:, :, :], f32(whigh[n % 2][:, :, :]), ALU.subtract).then_inc(wlow_ready, 1)

            def channels(j, first=False, last=False):
                for u in range(NG_U):
                    n, c = u // 3, u % 3
                    U = bank(2 * (u % 4) + 1)[:, 0:TC]
                    dst = mT[:, bass.ds(j, 1), c * TC:c * TC + TC]
                    dve.wait_ge(sg_ready, j * NG_U + (u + 1))
                    if n == 0:
                        V.tensor_tensor(dst, sgm[u % 2][:, None, :], U[:, None, :], ALU.mult).then_inc(mrg_done, 1)
                    else:
                        dve.wait_ge(mrg_done, j * NG_U + u)
                        V.tensor_tensor(mtmp, sgm[u % 2], U, ALU.mult).then_inc(mtmp_ready, 1)
                        dve.wait_ge(mtmp_ready, j * 9 + (u - 2))
                        V.tensor_tensor(dst, dst, mtmp[:, None, :], ALU.add).then_inc(mrg_done, 1)
                    if c == 0 and not (last and n == 3):
                        weights_low(j + (n + 1) // 4, (n + 1) % 4)

            weights_low(0, 0)
            for c in range(3):
                cols = slice(c * TC, c * TC + TC)
                dve.wait_ge(xhigh_ready, c + 1)
                V.tensor_tensor(hTl[:, :, cols], hT[:, :, cols], f32(hTh[:, :, cols]), ALU.subtract).then_inc(xlow_ready, 1)
            dve.wait_ge(xlow_ready, 3)
            channels(0, True)
            with dve.Fori(1, KD - 1) as j:
                channels(j)
            channels(KD - 1, last=True)

        @block.gpsimd
        def _(pool):
            pool.wait_ge(out_in, 16)

        stage3.close()
        stage_over()

        arena = sb("arena_last", [128, KD * NP1])
        NTS = NT + 1
        x2 = arena[:, 0:NTS * D].rearrange("p (t n) -> p t n", t=NTS)
        a4 = NTS * D
        cw = arena[:, a4:a4 + 2 * NTS].rearrange("p (c t) -> p c t", c=2)
        a4 += 2 * NTS
        posI = arena[:, a4:a4 + 2 * NTS].bitcast(I32)
        a4 += 2 * NTS
        slotI = arena[:, a4:a4 + 2 * NSLOT].bitcast(I32).rearrange("p (s n) -> p s n", n=2)
        a4 += 2 * NSLOT
        assert a4 <= KD * NP1 - SMALL
        tT = OT
        cursor[0], room[0] = 0, arena[:, KD * NP1 - SMALL:KD * NP1]
        xr = [tmp(D) for _ in range(2)]
        xm = [tmp(D) for _ in range(2)]
        sqj = tmp(D)
        wr = tmp(KD, 20)
        rbias = tmp(20)
        lg = tmp(NTS, 20)
        q1, q2 = tmp(1), tmp(1)
        gmx, gsum = tmp(NTS), tmp(NTS)
        e4, oh, eq = tmp(NTS, 4), tmp(NTS, 4), tmp(NTS, 4)
        cov = tmp(NTS)
        t16 = tmp(NTS, 16)
        le, le2, ee, o1, o2 = (tmp(NTS, 4) for _ in range(5))
        m1, s1 = tmp(NTS), tmp(NTS)
        rt_cols = consts_at["row"][0] + 1 - consts_at["iota"][0]
        rtc = tmp(rt_cols)
        RC = lambda n: rtc[:, consts_at[n][0] - consts_at["iota"][0]:][:, 0:consts_at[n][1]]
        before = tmp(128)
        Mc = [tmp(NTS, NE) for _ in range(2)]
        Mb, pos, junk9 = tmp(NTS, NE), tmp(NTS, NE), tmp(NTS, NE)
        cumt = tmp(NTS + 1, NE)
        cnt9 = tmp(NE, NTS)
        nsl, csum, base = tmp(NE), tmp(NE), tmp(NE)
        le16 = tmp(NE, NE)
        posc = tmp(2 * NTS)
        nsl2, rr = tmp(2 * NTS), tmp(2 * NTS)
        reach = tmp(2 * NTS, NSLOT + 1)
        tokB = tmp(2 * NTS, NSLOT)
        ecmp = tmp(NSLOT, NE)
        eslot = tmp(NSLOT)
        rowA = TT[:, :, :].rearrange("p a b -> p (a b)")[:, 0:2 * NTS * 128].rearrange("p (n r) -> p n r", r=128)
        NM4 = ("A_ready", "A_done", "B_ready", "ids_done", "xr_in", "wr_in", "op_done", "x2_ready", "rs_ready", "xm_ready", "xm_tp", "tT_ready", "rt_done", "lg_ready",
               "ex_in", "ex_out", "ex2_in", "ex2_out", "ch4A", "ch4V")
        S4 = {n: sem(n) for n in NM4}
        xm_out = [sem(f"xm_out{n}") for n in range(2)]
        R_ = lambda t: 128 if t < NT else NB
        C_ = lambda t: slice(t * 128, t * 128 + R_(t))

        stage4 = ExitStack()
        block = stage4.enter_context(nc.Block())

        @block.sync
        def _(sy):
            sy.dma_start(wr[:, :, 0:4], I["w_grp"][0].rearrange("(p j) n -> p j n", j=KD)).then_inc(S4["wr_in"], 16)
            sy.dma_start(wr[:, :, 4:20], I["w_rt"][0].rearrange("(p j) n -> p j n", j=KD)).then_inc(S4["wr_in"], 16)
            sy.dma_start(rbias[:, 0:4], I["b_grp"][0:1].broadcast_to([128, 4])).then_inc(S4["wr_in"], 16)
            sy.dma_start(rbias[:, 4:20], I["b_rt"][0:1].broadcast_to([128, 16])).then_inc(S4["wr_in"], 16)
            sy.dma_start(rtc, C_d[:, consts_at["iota"][0]:consts_at["iota"][0] + rt_cols]).then_inc(S4["wr_in"], 16)
            c0 = consts_at["causal01"][0]
            sy.dma_start(before, C_d[:, c0:c0 + 128]).then_inc(S4["wr_in"], 16)

            def store(t):
                sy.wait_ge(S4["xm_ready"], t + 1)
                sy.dma_start(xm_d[t * 128:t * 128 + R_(t), :], xm[t % 2][0:R_(t), :]).then_inc(xm_out[t % 2], 16)

            for t in range(NTS):
                if t >= 1:
                    sy.wait_ge(S4["x2_ready"], t)
                src = x_p[t * 128:t * 128 + 128, :] if t < NT else x_s
                sy.dma_start(xr[t % 2][0:R_(t), :], src).then_inc(S4["xr_in"], 16)
                if t >= 1:
                    store(t - 1)
            store(NT)
            for n in range(2):
                sy.wait_ge(xm_out[n], 16 * ((NTS + 1 - n) // 2))

        @block.tensor
        def _(pe):
            MM, TR = nc.tensor.matmul, nc.tensor.transpose
            ident = K("ident")

            def project(t):
                R = R_(t)
                if t >= 2:
                    pe.wait_ge(S4["x2_ready"], t - 1)
                for half in range(2):
                    for k in range(KD):
                        last = MM(bank(2 * (t % 2) + half)[0:R, :], mT[:, k, C_(t)], wout[:, k, half * 512:half * 512 + 512],
                                  start=(k == 0), stop=(k == KD - 1))
                last.then_inc(S4["op_done"], 1)

            def route(t):
                R = R_(t)
                pe.wait_ge(S4["xm_ready"], t + 1)
                if t:
                    pe.wait_ge(S4["tT_ready"], t)
                for k in range(KD):
                    last = TR(bank(4, 2)[:, k * 128:k * 128 + R], xm[t % 2][0:R, k:D:KD], ident[0:R, 0:R])
                last.then_inc(S4["xm_tp"], 1)
                pe.wait_ge(S4["tT_ready"], t + 1)
                if t:
                    pe.wait_ge(S4["lg_ready"], t)
                for k in range(KD):
                    last = MM(bank(6)[0:R, 0:20], tT[:, k, C_(t)], wr[:, k, :], start=(k == 0), stop=(k == KD - 1))
                last.then_inc(S4["rt_done"], 1)

            project(0)
            pe.wait_ge(S4["wr_in"], 96)
            for t in range(NTS):
                if t + 1 < NTS:
                    project(t + 1)
                route(t)
            flat = Mb.rearrange("p t e -> p (t e)")
            pe.wait_ge(S4["A_ready"], 1)
            MM(bank(0)[:, 0:NTS * NE], before, flat, start=True, stop=True)
            MM(bank(1)[:, 0:NTS * NE], K("ones"), flat, start=True, stop=True).then_inc(S4["A_done"], 1)
            pe.wait_ge(S4["B_ready"], 1)
            for n in range(2 * NTS):
                last = MM(bank(2)[:, 0:NSLOT], rowA[:, n, :], tokB[:, n, :], start=(n == 0), stop=(n == 2 * NTS - 1))
            last.then_inc(S4["ids_done"], 1)

        @block.scalar
        def _(act):
            A = nc.scalar.activation
            chain = Chain(act, S4["ch4A"])
            nc.scalar.preload_act_table_set("natural_log_exp_and_others")
            for t in range(NTS):
                R = R_(t)
                act.wait_ge(S4["x2_ready"], t + 1)
                chain(A(sqj[0:R, :], x2[0:R, t, :], ACT.Square, accum_out=q1[0:R, :]))
                chain(A(q1[0:R, :], q1[0:R, :], ACT.Ln, bias=eps[0:R, :], scale=1.0 / D))
                if t:
                    act.wait_ge(S4["xm_ready"], t)
                A(q2[0:R, :], q1[0:R, :], ACT.Exp, scale=-0.5).then_inc(S4["rs_ready"], 1)
            act.wait_ge(S4["ex_in"], 1)
            A(e4, e4, ACT.Exp).then_inc(S4["ex_out"], 1)
            act.wait_ge(S4["ex2_in"], 1)
            A(ee, ee, ACT.Exp).then_inc(S4["ex2_out"], 1)

        @block.vector
        def _(dve):
            V = nc.vector
            chain = Chain(dve, S4["ch4V"])
            chain(V.memset(lg[:, NT, :], 0.0))
            dve.wait_ge(S4["wr_in"], 96)

            def residual(t):
                R = R_(t)
                dve.wait_ge(S4["xr_in"], 16 * (t + 1))
                dve.wait_ge(S4["op_done"], t + 1)
                V.tensor_tensor(x2[0:R, t, :], bank(2 * (t % 2), 2)[0:R, :], xr[t % 2][0:R, :], ALU.add)\
                    .then_inc(S4["x2_ready"], 1)

            residual(0)
            for t in range(NTS):
                R = R_(t)
                dve.wait_ge(S4["rs_ready"], t + 1)
                if t >= 2:
                    dve.wait_ge(S4["xm_tp"], t - 1)
                    dve.wait_ge(xm_out[t % 2], 16 * (t // 2))
                V.tensor_scalar(xm[t % 2][0:R, :], x2[0:R, t, :], q2[0:R, :], None, ALU.mult).then_inc(S4["xm_ready"], 1)
                if t + 1 < NTS:
                    residual(t + 1)
                dve.wait_ge(S4["xm_tp"], t + 1)
                V.tensor_tensor(tT[:, :, C_(t)], bank(4, 2).rearrange("p (j t) -> p j t", j=KD)[:, :, 0:R],
                                g_ffn[:, :, None].broadcast_to([128, KD, R]), ALU.mult).then_inc(S4["tT_ready"], 1)
                dve.wait_ge(S4["rt_done"], t + 1)
                V.tensor_tensor(lg[0:R, t, :], bank(6)[0:R, 0:20], rbias[0:R, :], ALU.add).then_inc(S4["lg_ready"], 1)
            dve.wait_ge(S4["lg_ready"], NTS)
            wide = lambda v: v[:, :, None].broadcast_to([128, NTS, 4])

            def first_max(x, mx, out):
                chain(V.tensor_tensor(eq, x, wide(mx), ALU.is_equal))
                V.tensor_copy(out[:, :, 0], eq[:, :, 0])
                chain(V.tensor_copy(cov, eq[:, :, 0]))
                for n in range(1, 4):
                    chain(V.scalar_tensor_tensor(out[:, :, n], cov, 0.5, eq[:, :, n], ALU.is_lt, ALU.mult))
                    if n < 3:
                        chain(V.tensor_tensor(cov, cov, eq[:, :, n], ALU.max))

            grp = lg[:, :, 0:4]
            chain(V.tensor_reduce(gmx, grp, AX.X, ALU.max))
            V.tensor_tensor(e4, grp, wide(gmx), ALU.subtract).then_inc(S4["ex_in"], 1)
            first_max(grp, gmx, oh)
            chain(V.tensor_tensor(t16.rearrange("p t (e g) -> p t e g", e=4), lg[:, :, 4:20].rearrange("p t (g e) -> p t e g", g=4),
                                  oh[:, :, None, :].broadcast_to([128, NTS, 4, 4]), ALU.mult))
            chain(V.tensor_reduce(le, t16.rearrange("p t (e g) -> p t e g", e=4), AX.X, ALU.add))
            chain(V.tensor_reduce(m1, le, AX.X, ALU.max))
            V.tensor_tensor(ee, le, wide(m1), ALU.subtract).then_inc(S4["ex2_in"], 1)
            first_max(le, m1, o1)
            chain(V.scalar_tensor_tensor(le2, o1, NEG, le, ALU.mult, ALU.add))
            chain(V.tensor_reduce(m1, le2, AX.X, ALU.max))
            first_max(le2, m1, o2)
            chain(V.tensor_tensor(oh, oh, wide(RC("valid")), ALU.mult))
            for n, o in enumerate((o1, o2)):
                V.tensor_tensor(Mc[n].rearrange("p t (g e) -> p t g e", g=4), oh[:, :, :, None].broadcast_to([128, NTS, 4, 4]),
                                o[:, :, None, :].broadcast_to([128, NTS, 4, 4]), ALU.mult).then_inc(S4["ch4V"], 1)
                chain.n += 1
            dve.wait_ge(S4["ch4V"], chain.n)
            V.tensor_tensor(Mb, Mc[0], Mc[1], ALU.add).then_inc(S4["A_ready"], 1)
            chain(V.memset(cumt[:, 0, :], 0.0))
            dve.wait_ge(S4["A_done"], 1)
            within, total = (bank(n)[:, 0:NTS * NE].rearrange("p (t e) -> p t e", e=NE) for n in range(2))
            for t in range(NTS):
                chain(V.tensor_tensor(cumt[:, t + 1, :], cumt[:, t, :], total[:, t, :], ALU.add))
            chain(V.tensor_tensor(cnt9, cumt[:, NTS, :, None].broadcast_to([128, NE, NTS]),
                                  RC("slot_lo")[:, None, 0:NTS].broadcast_to([128, NE, NTS]), ALU.is_gt))
            chain(V.tensor_reduce(nsl, cnt9, AX.X, ALU.add))
            chain(V.tensor_tensor(le16, RC("upto").rearrange("p (a b) -> p a b", a=NE),
                                  nsl[:, None, :].broadcast_to([128, NE, NE]), ALU.mult))
            chain(V.tensor_reduce(csum, le16, AX.X, ALU.add))
            chain(V.tensor_tensor(base, csum, nsl, ALU.subtract))
            chain(V.tensor_scalar(base, base, 128.0, None, ALU.mult))
            chain(V.tensor_tensor(pos, within, cumt[:, 0:NTS, :], ALU.add))
            chain(V.tensor_tensor(pos, pos, base[:, None, :].broadcast_to([128, NTS, NE]), ALU.add))
            for n in range(2):
                chain(V.tensor_tensor(junk9, Mc[n], pos, ALU.mult))
                chain(V.tensor_reduce(posc[:, n * NTS:n * NTS + NTS], junk9, AX.X, ALU.add))
            chain(V.tensor_tensor(reach, posc[:, :, None].broadcast_to([128, 2 * NTS, NSLOT + 1]),
                                  RC("slot_lo")[:, None, :].broadcast_to([128, 2 * NTS, NSLOT + 1]), ALU.is_ge))
            chain(V.tensor_reduce(nsl2, reach, AX.X, ALU.add))
            chain(V.scalar_tensor_tensor(rr, nsl2, -128.0, posc, ALU.mult, ALU.add))
            chain(V.tensor_tensor(rowA, RC("iota")[:, None, :].broadcast_to([128, 2 * NTS, 128]),
                                  rr[:, :, None].broadcast_to([128, 2 * NTS, 128]), ALU.is_equal))
            chain(V.tensor_tensor(tokB, reach[:, :, 0:NSLOT], reach[:, :, 1:NSLOT + 1], ALU.subtract))
            for n in range(2):
                half = tokB[:, n * NTS:n * NTS + NTS, :]
                last = V.tensor_tensor(half, half, RC("token")[:, :, None].broadcast_to([128, NTS, NSLOT]), ALU.mult)
                last.then_inc(S4["ch4V"], 1)
            chain.n += 2
            dve.wait_ge(S4["ch4V"], chain.n)
            V.tensor_copy(posI, posc).then_inc(S4["B_ready"], 1)
            chain(V.tensor_tensor(ecmp, csum[:, None, :].broadcast_to([128, NSLOT, NE]),
                                  RC("slot_id")[:, :, None].broadcast_to([128, NSLOT, NE]), ALU.is_le))
            chain(V.tensor_reduce(eslot, ecmp, AX.X, ALU.add))
            chain(V.tensor_scalar(eslot, eslot, NE - 1.0, 128.0, ALU.min, ALU.mult))
            V.tensor_scalar(slotI[:, :, 1], eslot, RC("row"), None, ALU.add)
            dve.wait_ge(S4["ex2_out"], 1)
            for n, o in enumerate((o1, o2)):
                chain(V.tensor_tensor(o, ee, o, ALU.mult))
                chain(V.tensor_reduce(cw[:, n, :], o, AX.X, ALU.add))
            chain(V.tensor_tensor(s1, cw[:, 0, :], cw[:, 1, :], ALU.add))
            dve.wait_ge(S4["ex_out"], 1)
            chain(V.tensor_reduce(gsum, e4, AX.X, ALU.add))
            chain(V.tensor_tensor(s1, s1, gsum, ALU.mult))
            chain(V.reciprocal(s1, s1))
            V.tensor_tensor(cw, cw, s1[:, None, :].broadcast_to([128, 2, NTS]), ALU.mult)
            dve.wait_ge(S4["ids_done"], 1)
            V.tensor_copy(slotI[:, :, 0], bank(2)[:, 0:NSLOT])

        stage4.close()
        stage_over()

        flatTT = TT[:, :, :].rearrange("p a b -> p (a b)")
        weg = [flatTT[:, n * 4096:n * 4096 + 2048].rearrange("p (k f) -> p k f", k=KD) for n in range(2)]
        weu = [flatTT[:, n * 4096 + 2048:n * 4096 + 4096].rearrange("p (k f) -> p k f", k=KD) for n in range(2)]
        flatOT = OT[:, :, :].rearrange("p a b -> p (a b)")
        rowsT = [flatOT[:, n * D:n * D + D].rearrange("p (k r) -> p k r", k=KD) for n in range(2)]
        cursor[0], room[0] = 0, small
        wed = [tmp(2, D) for _ in range(2)]
        rows_g = [tmp(D) for _ in range(2)]
        orows = [tmp(D) for _ in range(2)]
        sil5 = [tmp(DE) for _ in range(2)]
        hid = [tmp(DE) for _ in range(2)]
        hidT = [tmp(2, 128) for _ in range(2)]
        idx5 = [small[:, cursor[0] + 2 * n:cursor[0] + 2 * n + 2].bitcast(I32) for n in range(2)]
        cursor[0] += 4
        idx5z = tmp(1)
        NGB = 8
        back = [flatTT[:, n * D:n * D + D] for n in range(NGB)]
        NM5 = ("zero5", "idx_set", "go5", "x_tp5", "xT_ready5", "up_done", "silu_ready", "hid_ready", "h_tp", "hT_ready5",
               "dn_done", "o_ready5", "row_done", "y_out")
        S5 = {n: sem(n) for n in NM5}
        rows_in = [sem(f"rows_in{n}") for n in range(2)]
        gu_in = [sem(f"gu_in{n}") for n in range(2)]
        dn_in = [sem(f"dn_in{n}") for n in range(2)]
        o_out = [sem(f"o_out{n}") for n in range(2)]
        back_in = [sem(f"back_in{n}") for n in range(NGB)]
        NPAIR = NSLOT // 2
        assert NSLOT % 2 == 0

        stage5 = ExitStack()
        block = stage5.enter_context(nc.Block())

        @block.sync
        def _(sy):
            dst = slots_d.rearrange("(s p) d -> p s d", p=128)
            with sy.Fori(0, NPAIR) as i:
                for par in range(2):
                    sy.wait_ge(S5["o_ready5"], i * 2 + (par + 1))
                    sy.dma_start(dst[:, bass.ds(i * 2 + par, 1), :], orows[par][:, None, :]).then_inc(o_out[par], 16)
            for t in range(NTS):
                sy.wait_ge(S5["row_done"], 2 * (t + 1))
                dst = O[0][0, t * 128:t * 128 + 128, :] if t < NT else O[1][:, 0, :]
                sy.dma_start(dst, x2[0:R_(t), t, :]).then_inc(S5["y_out"], 16)
            sy.wait_ge(S5["y_out"], 16 * NTS)

        @block.gpsimd
        def _(pool):
            G = nc.gpsimd
            eg_d = I["w_eg"][0].rearrange("e (p j) f -> (e p) (j f)", j=KD)
            eu_d = I["w_eu"][0].rearrange("e (p j) f -> (e p) (j f)", j=KD)
            ed_d = I["w_ed"][0].rearrange("e (p a) d -> (e p) (a d)", a=2)

            def wait(s, v):
                pool.wait_ge(s, v)
                pool.sem_inc(S5["go5"], 1)

            def gather(dst, src, idx, s):
                G.indirect_dma_start(dst, None, src, bass.IndirectOffsetOnAxis(ap=idx.bitcast(U32), axis=0)).then_inc(s, 16)

            def slot(i, par, first=False):
                if not first:
                    wait(S5["up_done"], i * 2 + (par - 1))
                    wait(dn_in[par], i * 16)
                G.tensor_copy(idx5[par][:, None, :], slotI[:, bass.ds(i * 2 + par, 1), :]).then_inc(S5["idx_set"], 1)
                wait(S5["idx_set"], i * 2 + (par + 1))
                gather(rows_g[par], xm_d, idx5[par][:, 0:1], rows_in[par])
                gather(weg[par].rearrange("p k f -> p (k f)"), eg_d, idx5[par][:, 1:2], gu_in[par])
                gather(weu[par].rearrange("p k f -> p (k f)"), eu_d, idx5[par][:, 1:2], gu_in[par])
                if not first:
                    wait(S5["dn_done"], i * 2 + (par - 1))
                gather(wed[par].rearrange("p a d -> p (a d)"), ed_d, idx5[par][:, 1:2], dn_in[par])

            slot(0, 0, True)
            slot(0, 1, True)
            with pool.Fori(1, NPAIR) as i:
                for par in range(2):
                    slot(i, par)
            for par in range(2):
                pool.wait_ge(o_out[par], 16 * NPAIR)
            for t in range(NTS):
                for c in range(2):
                    n = 2 * t + c
                    if n >= NGB:
                        pool.wait_ge(S5["row_done"], n - NGB + 1)
                    R = R_(t)
                    gather(back[n % NGB][0:R, :], slots_d, posI[0:R, c * NTS + t:c * NTS + t + 1], back_in[n % NGB])

        @block.tensor
        def _(pe):
            MM, TR = nc.tensor.matmul, nc.tensor.transpose
            ident = K("ident")

            def wait(s, v):
                at = v if isinstance(v, int) else pe.snap(v)
                pe.wait_ge(S5["zero5"], 1)
                pe.wait_ge(s, at)

            def turn(s2, i, par):
                wait(rows_in[par], i * 16 + 16)
                if not (isinstance(s2, int) and s2 == 0):
                    wait(S5["xT_ready5"], s2)
                for k in range(KD):
                    last = TR(bank(2, 2)[:, k * 128:k * 128 + 128], rows_g[par][:, k:D:KD], ident)
                last.then_inc(S5["x_tp5"], 1)

            def up(s, i, par, first=False):
                wait(S5["xT_ready5"], s + 1)
                wait(gu_in[par], i * 32 + 32)
                if not first:
                    wait(S5["hid_ready"], s - 1)
                for n, w in enumerate((weg, weu)):
                    for k in range(KD):
                        last = MM(bank(par)[:, n * DE:n * DE + DE], rowsT[par][:, k, :], w[par][:, k, :],
                                  start=(k == 0), stop=(k == KD - 1))
                last.then_inc(S5["up_done"], 1)

            def hidden(s, par):
                wait(S5["hid_ready"], s + 1)
                for a in range(2):
                    last = TR(bank(4)[:, a * 128:a * 128 + 128], hid[par][:, a:DE:2], ident)
                last.then_inc(S5["h_tp"], 1)

            def down(s, i, par, first=False):
                wait(dn_in[par], i * 16 + 16)
                wait(S5["hT_ready5"], s + 1)
                if not first:
                    wait(S5["o_ready5"], s)
                for half in range(2):
                    for a in range(2):
                        last = MM(bank(6 + half), hidT[par][:, a, :], wed[par][:, a, half * 512:half * 512 + 512],
                                  start=(a == 0), stop=(a == 1))
                last.then_inc(S5["dn_done"], 1)

            pe.wait_ge(S5["zero5"], 1)
            turn(0, 0, 0)
            up(0, 0, 0, True)
            turn(1, 0, 1)
            up(1, 0, 1, True)
            hidden(0, 0)
            turn(2, 1, 0)
            down(0, 0, 0, True)

            def step(s, i, par, last=False):
                up(s, i, par)
                hidden(s - 1, 1 - par)
                if not last:
                    turn(s + 1, i + par, 1 - par)
                down(s - 1, i + (par - 1), 1 - par)

            with pe.Fori(1, NPAIR - 1) as i:
                for par in range(2):
                    step(i * 2 + par, i, par)
            step(NSLOT - 2, NPAIR - 1, 0)
            step(NSLOT - 1, NPAIR - 1, 1, True)
            hidden(NSLOT - 1, 1)
            down(NSLOT - 1, NPAIR - 1, 1)

        @block.scalar
        def _(act):
            nc.scalar.preload_act_table(ACT.Silu)

            def silu(s, par, first=False):
                act.wait_ge(S5["up_done"], s + 1)
                if not first:
                    act.wait_ge(S5["hid_ready"], s - 1)
                nc.scalar.activation(sil5[par], bank(par)[:, 0:DE], ACT.Silu).then_inc(S5["silu_ready"], 1)

            def finish(s, i, par, first=False):
                act.wait_ge(S5["h_tp"], s + 1)
                if not first:
                    act.wait_ge(S5["dn_done"], s - 1)
                nc.scalar.copy(hidT[par], bank(4)[:, 0:256].rearrange("p (a r) -> p a r", a=2)).then_inc(S5["hT_ready5"], 1)
                act.wait_ge(S5["dn_done"], s + 1)
                if not first:
                    act.wait_ge(o_out[par], i * 16)
                nc.scalar.copy(orows[par], bank(6, 2)).then_inc(S5["o_ready5"], 1)

            silu(0, 0, True)
            silu(1, 1, True)
            finish(0, 0, 0, True)
            silu(2, 0)
            finish(1, 0, 1, True)
            silu(3, 1)
            finish(2, 1, 0)
            with act.Fori(2, NPAIR) as i:
                for par in range(2):
                    silu(i * 2 + par, par)
                    finish(i * 2 + (par - 1), i + (par - 1), 1 - par)
            finish(NSLOT - 1, NPAIR - 1, 1)

        @block.vector
        def _(dve):
            V = nc.vector
            V.memset(idx5z, 0.0).then_inc(S5["zero5"], 1)

            def turned(s, par, first=False):
                dve.wait_ge(S5["x_tp5"], s + 1)
                if not first:
                    dve.wait_ge(S5["up_done"], s - 1)
                V.tensor_tensor(rowsT[par], bank(2, 2).rearrange("p (k r) -> p k r", k=KD),
                                g_ffn[:, :, None].broadcast_to([128, KD, 128]), ALU.mult).then_inc(S5["xT_ready5"], 1)

            def gate(s, par, first=False):
                dve.wait_ge(S5["silu_ready"], s + 1)
                if not first:
                    dve.wait_ge(S5["h_tp"], s - 1)
                V.tensor_tensor(hid[par], sil5[par], bank(par)[:, DE:2 * DE], ALU.mult).then_inc(S5["hid_ready"], 1)

            turned(0, 0, True)
            turned(1, 1, True)
            gate(0, 0, True)
            gate(1, 1, True)
            turned(2, 0)
            with dve.Fori(1, NPAIR - 1) as i:
                for par in range(2):
                    gate(i * 2 + par, par)
                    turned(i * 2 + (par + 1), 1 - par)
            gate(NSLOT - 2, 0)
            turned(NSLOT - 1, 1)
            gate(NSLOT - 1, 1)
            for t in range(NTS):
                R = R_(t)
                for c in range(2):
                    n = 2 * t + c
                    dve.wait_ge(back_in[n % NGB], 16 * (n // NGB + 1))
                    if c:
                        dve.wait_ge(S5["row_done"], n)
                    V.scalar_tensor_tensor(x2[0:R, t, :], back[n % NGB][0:R, :], cw[0:R, c, t:t + 1], x2[0:R, t, :],
                                           ALU.mult, ALU.add).then_inc(S5["row_done"], 1)

        stage5.close()


INPUTS = ['x_prompt', 'x_sample', 'mem_prompt', 'cache_sb_k', 'cache_sb_v', 'cache_nsa_cmp_k', 'cache_nsa_cmp_v',
          'cache_nsa_sel_k', 'cache_nsa_sel_v', 'cache_nsa_win_k', 'cache_nsa_win_v', 'state_gla', 'cache_mem_k',
          'cache_mem_v', 'page_table', 'norm_mix_g', 'norm_ffn_g', 'norm_mem_g', 'w_in', 'gla_gate_up', 'gla_gate_b',
          'gla_norm_g', 'nsa_pe_k', 'nsa_pe_v', 'nsa_phi_k', 'nsa_phi_v', 'nsa_qn_g', 'nsa_kn_g', 'mem_qn_g',
          'mem_kn_g', 'w_mem_kv', 'w_branch', 'w_out', 'rel_bias', 'w_grp', 'b_grp', 'w_rt', 'b_rt', 'w_eg', 'w_eu',
          'w_ed']
OUTPUTS = [(1, SEQ, D), (NB, 1, D), (1, 1, SEQ, 4, 64), (1, 1, SEQ, 4, 64), (1, 1, SEQ, 64), (1, 1, SEQ, 64),
           (1, 1, SEQ, 64), (1, 1, SEQ, 64), (1, 1, 512, 64), (1, 1, 512, 64), (1, 1, 4, 32, 64),
           (1, 1, MEM, 4, 64), (1, 1, MEM, 4, 64), (1, NB, 1, 4, 64), (1, NB, 1, 4, 64), (1, NB, 1, 64),
           (1, NB, 1, 64), (1, NB, 1, 64), (1, NB, 1, 64), (1, NB, 512, 64), (1, NB, 512, 64), (1, NB, 4, 32, 64)]


def kernel(**inputs):
    import concourse.bacc as bacc
    from concourse.bass_utils import run_bass_kernel_spmd

    nc = bacc.Bacc("TRN2", target_bir_lowering=False, num_devices=1)
    at, table = shape_constants()
    arrays = {n: np.ascontiguousarray(inputs[n]) for n in INPUTS}
    arrays.update(shape_table=table, distance_table=distance_onehots(), row_table=row_offsets())
    aps = {n: nc.dram_tensor("in_" + n, a.shape, mybir.dt.from_np(a.dtype), kind="ExternalInput").ap()
           for n, a in arrays.items()}
    outs = [nc.dram_tensor(f"out_{i}", s, F32, kind="ExternalOutput").ap() for i, s in enumerate(OUTPUTS)]
    build(nc, aps, outs, at, aps["shape_table"], aps["distance_table"], aps["row_table"], None)
    r = run_bass_kernel_spmd(nc, [{"in_" + n: a for n, a in arrays.items()}], core_ids=[0])
    return tuple(r.results[0][f"out_{i}"] for i in range(len(OUTPUTS)))
```
